# Optimizing a Trainium2 kernel written in Bass

```python
import jax, jax.numpy as jnp
from jax import lax
import numpy as np

D_MODEL = 1024
BATCH = 1
SEQ = 256
DEPTH = 2

D_MIX = D_MODEL
GROUP_W = D_MIX // 4
ROPE_THETA = 500000.0
NORM_EPS = 1e-6
Q_BLOCK = 128
NEG = -1e30
FORCE = 1e4
F32 = jnp.float32

MLA_HEADS = 4
MLA_NOPE = 64
MLA_ROPE = 32
MLA_V = GROUP_W // MLA_HEADS
MLA_Q_RANK = 192
MLA_KV_RANK = 128

NSA_HEADS = 4
NSA_HD = GROUP_W // NSA_HEADS
NSA_ROT = NSA_HD // 4
CMP_STRIDE = 16
CMP_LEN = 2 * CMP_STRIDE
SEL_LEN = 64
SEL_TOPN = 16
WINDOW = 512

LRU_W = GROUP_W
LRU_BLOCKS = 4
LRU_BW = LRU_W // LRU_BLOCKS
LRU_C = 8.0
CONV_W = 4

SSD_HEADS = 4
SSD_HD = GROUP_W // SSD_HEADS
SSD_GROUPS = 2
SSD_STATE = 128
SSD_CHUNK = 128
SSD_DI = SSD_HEADS * SSD_HD
SSD_XBC = SSD_DI + 2 * SSD_GROUPS * SSD_STATE

MLA_COLS = MLA_Q_RANK + MLA_KV_RANK + MLA_ROPE
NSA_COLS = NSA_HEADS * NSA_HD + 6 * NSA_HD + 3 * NSA_HEADS
LRU_COLS = 2 * LRU_W
SSD_COLS = SSD_DI + SSD_XBC + SSD_HEADS
IN_COLS = MLA_COLS + NSA_COLS + LRU_COLS + SSD_COLS

D_FF = 3584
N_EXPERTS = 8
TOP_K = 2
N_DENSE = (DEPTH + 1) // 2
N_MOE = DEPTH // 2

kernel_name = 'hybrid_mla_nsa_rglru_ssd_moe'

def rms_norm(x, g):
    xf = x.astype(F32)
    y = xf * lax.rsqrt(jnp.mean(xf * xf, axis=-1, keepdims=True) + NORM_EPS)
    return (y * g.astype(F32)).astype(x.dtype)

def rope_tables(positions, rot_dim):
    inv = ROPE_THETA ** (-jnp.arange(0, rot_dim, 2, dtype=F32) / rot_dim)
    ang = positions.astype(F32)[:, None] * inv[None, :]
    return jnp.cos(ang), jnp.sin(ang)

def apply_rope(x, cos, sin, rot_dim):
    half = rot_dim // 2
    xf = x.astype(F32)
    x1, x2, xp = xf[..., :half], xf[..., half:rot_dim], xf[..., rot_dim:]
    c, s = cos[None, :, None, :], sin[None, :, None, :]
    return jnp.concatenate([x1 * c - x2 * s, x2 * c + x1 * s, xp], axis=-1).astype(x.dtype)

def causal_dwconv(x, w, b):
    K, C = w.shape
    y = lax.conv_general_dilated(x, w[:, None, :].astype(x.dtype), window_strides=(1,),
                                 padding=[(K - 1, 0)], dimension_numbers=('NWC', 'WIO', 'NWC'),
                                 feature_group_count=C)
    return y + b.astype(x.dtype)

def swiglu(h, wg, wu, wd):
    return (jax.nn.silu(h @ wg) * (h @ wu)) @ wd

def causal_attention_blocks(q, k, v, scale):
    B, S, H, Dk = q.shape
    nb = S // Q_BLOCK
    qb = q.reshape(B, nb, Q_BLOCK, H, Dk).transpose(1, 0, 2, 3, 4)
    kf, vf = k.astype(F32), v.astype(F32)
    kpos = jnp.arange(S)

    def one(args):
        i, qi = args
        s = jnp.einsum('bqhd,bkhd->bhqk', qi.astype(F32), kf) * scale
        qpos = i * Q_BLOCK + jnp.arange(Q_BLOCK)
        s = jnp.where(kpos[None, :] <= qpos[:, None], s, NEG)
        p = jax.nn.softmax(s, axis=-1)
        return jnp.einsum('bhqk,bkhd->bqhd', p, vf)

    o = lax.map(one, (jnp.arange(nb), qb))
    return o.transpose(1, 0, 2, 3, 4).reshape(B, S, H, v.shape[-1])

def mla_mixer(u, cos, sin, q_norm, w_uq, kv_norm, w_ukv):
    B, S, _ = u.shape
    c_q = u[..., :MLA_Q_RANK]
    c_kv = u[..., MLA_Q_RANK:MLA_Q_RANK + MLA_KV_RANK]
    k_pe = u[..., MLA_Q_RANK + MLA_KV_RANK:][:, :, None, :]
    q = (rms_norm(c_q, q_norm) @ w_uq).reshape(B, S, MLA_HEADS, MLA_NOPE + MLA_ROPE)
    kv = (rms_norm(c_kv, kv_norm) @ w_ukv).reshape(B, S, MLA_HEADS, MLA_NOPE + MLA_V)
    q = jnp.concatenate([q[..., :MLA_NOPE], apply_rope(q[..., MLA_NOPE:], cos, sin, MLA_ROPE)], axis=-1)
    k_pe = jnp.broadcast_to(apply_rope(k_pe, cos, sin, MLA_ROPE), (B, S, MLA_HEADS, MLA_ROPE))
    k = jnp.concatenate([kv[..., :MLA_NOPE], k_pe.astype(kv.dtype)], axis=-1)
    v = kv[..., MLA_NOPE:]
    o = causal_attention_blocks(q, k, v, (MLA_NOPE + MLA_ROPE) ** -0.5)
    return o.reshape(B, S, MLA_HEADS * MLA_V)

def nsa_mixer(u, cos, sin, cmp_pe, w_cmp):
    B, S, _ = u.shape
    H, d = NSA_HEADS, NSA_HD
    q = apply_rope(u[..., :H * d].reshape(B, S, H, d), cos, sin, NSA_ROT)
    kvs = u[..., H * d:H * d + 6 * d].reshape(B, S, 6, d)
    gates = jax.nn.sigmoid(u[..., H * d + 6 * d:].astype(F32)).reshape(B, S, H, 3)
    keys = apply_rope(kvs[:, :, 0::2], cos, sin, NSA_ROT)
    vals = kvs[:, :, 1::2]
    scale = d ** -0.5

    nc = S // CMP_STRIDE - 1

    def compress(t, pe, w):
        ch = t.reshape(B, S // CMP_STRIDE, CMP_STRIDE, d)
        blk = jnp.concatenate([ch[:, :-1], ch[:, 1:]], axis=2)
        return ((blk + pe).reshape(B, nc, CMP_LEN * d) @ w).astype(F32)

    kc = compress(keys[:, :, 0], cmp_pe[0], w_cmp[0])
    vc = compress(vals[:, :, 0], cmp_pe[1], w_cmp[1])
    cmp_start = jnp.arange(nc) * CMP_STRIDE
    cmp_last = cmp_start + CMP_LEN - 1

    n_sel = S // SEL_LEN
    n_top = min(SEL_TOPN, n_sel)
    ks_blk = keys[:, :, 1].astype(F32).reshape(B, n_sel, SEL_LEN, d)
    vs_blk = vals[:, :, 1].astype(F32).reshape(B, n_sel, SEL_LEN, d)
    sel_start = jnp.arange(n_sel) * SEL_LEN
    overlap = ((cmp_start[:, None] <= sel_start[None, :] + SEL_LEN - 1)
               & (cmp_last[:, None] >= sel_start[None, :])).astype(F32)

    kw_pad = jnp.pad(keys[:, :, 2].astype(F32), ((0, 0), (WINDOW, 0), (0, 0)))
    vw_pad = jnp.pad(vals[:, :, 2].astype(F32), ((0, 0), (WINDOW, 0), (0, 0)))

    nb = S // Q_BLOCK
    qb = q.reshape(B, nb, Q_BLOCK, H, d).transpose(1, 0, 2, 3, 4)
    gb = gates.reshape(B, nb, Q_BLOCK, H, 3).transpose(1, 0, 2, 3, 4)
    jj = jnp.arange(n_sel)
    woff = jnp.arange(WINDOW + Q_BLOCK)

    def one(args):
        i, qi, gi = args
        qf = qi.astype(F32)
        qpos = i * Q_BLOCK + jnp.arange(Q_BLOCK)
        m_c = cmp_last[None, :] <= qpos[:, None]
        s_c = jnp.einsum('bqhd,bnd->bhqn', qf, kc) * scale
        p_c = jax.nn.softmax(jnp.where(m_c, s_c, NEG), axis=-1) * m_c
        o_c = jnp.einsum('bhqn,bnd->bqhd', p_c, vc)
        imp = jnp.einsum('bhqn,nj->bqj', p_c, overlap)
        cur = qpos // SEL_LEN
        forced = (jj[None, :] == 0) | (jj[None, :] == cur[:, None]) | (jj[None, :] == cur[:, None] - 1)
        imp = jnp.where(jj[None, :] <= cur[:, None], imp + FORCE * forced, NEG)
        top_v, idx = lax.top_k(imp, n_top)
        ok = top_v > 0.5 * NEG
        ksg = jax.vmap(lambda kb, ix: kb[ix])(ks_blk, idx)
        vsg = jax.vmap(lambda vb, ix: vb[ix])(vs_blk, idx)
        tok = idx[..., None] * SEL_LEN + jnp.arange(SEL_LEN)
        m_s = (tok <= qpos[None, :, None, None]) & ok[..., None]
        s_s = jnp.einsum('bqhd,bqnkd->bhqnk', qf, ksg) * scale
        s_s = jnp.where(m_s[:, None], s_s, NEG)
        p_s = jax.nn.softmax(s_s.reshape(B, H, Q_BLOCK, -1), axis=-1).reshape(s_s.shape)
        o_s = jnp.einsum('bhqnk,bqnkd->bqhd', p_s, vsg)
        kwi = lax.dynamic_slice_in_dim(kw_pad, i * Q_BLOCK, WINDOW + Q_BLOCK, axis=1)
        vwi = lax.dynamic_slice_in_dim(vw_pad, i * Q_BLOCK, WINDOW + Q_BLOCK, axis=1)
        kpos = i * Q_BLOCK - WINDOW + woff
        m_w = ((kpos[None, :] <= qpos[:, None]) & (kpos[None, :] > qpos[:, None] - WINDOW)
               & (kpos[None, :] >= 0))
        s_w = jnp.einsum('bqhd,bkd->bhqk', qf, kwi) * scale
        p_w = jax.nn.softmax(jnp.where(m_w, s_w, NEG), axis=-1)
        o_w = jnp.einsum('bhqk,bkd->bqhd', p_w, vwi)
        return gi[..., 0:1] * o_c + gi[..., 1:2] * o_s + gi[..., 2:3] * o_w

    o = lax.map(one, (jnp.arange(nb), qb, gb))
    return o.transpose(1, 0, 2, 3, 4).reshape(B, S, H * d)

def rglru_mixer(u, conv_w, conv_b, w_gate, b_gate, lam):
    B, S, _ = u.shape
    xb = causal_dwconv(u[..., :LRU_W], conv_w, conv_b).astype(F32)
    gbr = u[..., LRU_W:].astype(F32)
    xblk = xb.reshape(B, S, LRU_BLOCKS, LRU_BW)
    g = jnp.einsum('bsnc,gncd->gbsnd', xblk, w_gate.astype(F32)).reshape(2, B, S, LRU_W)
    g = g + b_gate.astype(F32)[:, None, None, :]
    r, i_g = jax.nn.sigmoid(g[0]), jax.nn.sigmoid(g[1])
    log_a = -LRU_C * r * jax.nn.softplus(-lam.astype(F32))
    a = jnp.exp(log_a)
    b = jnp.sqrt(jnp.maximum(-jnp.expm1(2.0 * log_a), 0.0)) * (i_g * xb)

    def comb(e1, e2):
        a1, b1 = e1
        a2, b2 = e2
        return a1 * a2, a2 * b1 + b2

    _, h = lax.associative_scan(comb, (a, b), axis=1)
    return h * jax.nn.gelu(gbr)

def segsum(x):
    T = x.shape[-1]
    xx = jnp.broadcast_to(x[..., None], x.shape + (T,))
    xx = jnp.where(jnp.tril(jnp.ones((T, T), bool), -1), xx, 0.0)
    cs = jnp.cumsum(xx, axis=-2)
    return jnp.where(jnp.tril(jnp.ones((T, T), bool), 0), cs, -jnp.inf)

def ssd_chunked(xdt, dA, Bm, Cm):
    B, S, H, P = xdt.shape
    N = Bm.shape[-1]
    L = SSD_CHUNK
    c = S // L
    x = xdt.reshape(B, c, L, H, P)
    Bc = Bm.reshape(B, c, L, H, N)
    Cc = Cm.reshape(B, c, L, H, N)
    a = dA.reshape(B, c, L, H).transpose(0, 3, 1, 2)
    a_cs = jnp.cumsum(a, axis=-1)
    Lm = jnp.exp(segsum(a))
    scores = jnp.einsum('bclhn,bcshn->bhcls', Cc, Bc) * Lm
    y_diag = jnp.einsum('bhcls,bcshp->bclhp', scores, x)
    decay_states = jnp.exp(a_cs[..., -1:] - a_cs)
    states = jnp.einsum('bclhn,bhcl,bclhp->bchpn', Bc, decay_states, x)
    states = jnp.concatenate([jnp.zeros_like(states[:, :1]), states], axis=1)
    decay_chunk = jnp.exp(segsum(jnp.pad(a_cs[..., -1], ((0, 0), (0, 0), (1, 0)))))
    states = jnp.einsum('bhzc,bchpn->bzhpn', decay_chunk, states)[:, :-1]
    y_off = jnp.einsum('bclhn,bchpn,bhcl->bclhp', Cc, states, jnp.exp(a_cs))
    return (y_diag + y_off).reshape(B, S, H, P)

def ssd_mixer(u, conv_w, conv_b, dt_bias, a_log, d_skip, norm_g):
    B, S, _ = u.shape
    z = u[..., :SSD_DI].astype(F32)
    xbc = jax.nn.silu(causal_dwconv(u[..., SSD_DI:SSD_DI + SSD_XBC], conv_w, conv_b).astype(F32))
    dt = u[..., SSD_DI + SSD_XBC:].astype(F32)
    gn = SSD_GROUPS * SSD_STATE
    xs = xbc[..., :SSD_DI].reshape(B, S, SSD_HEADS, SSD_HD)
    rep = SSD_HEADS // SSD_GROUPS
    Bm = jnp.repeat(xbc[..., SSD_DI:SSD_DI + gn].reshape(B, S, SSD_GROUPS, SSD_STATE), rep, axis=2)
    Cm = jnp.repeat(xbc[..., SSD_DI + gn:].reshape(B, S, SSD_GROUPS, SSD_STATE), rep, axis=2)
    dt = jax.nn.softplus(dt + dt_bias.astype(F32))
    A = -jnp.exp(a_log.astype(F32))
    y = ssd_chunked(xs * dt[..., None], dt * A, Bm, Cm)
    y = y + xs * d_skip.astype(F32)[:, None]
    y = y.reshape(B, S, SSD_DI) * jax.nn.silu(z)
    return rms_norm(y, norm_g)

def moe_ffn(h, router, w_gate, w_up, w_down):
    B, S, D = h.shape
    t = h.reshape(B * S, D)
    logits = (t @ router).astype(F32)
    top_v, idx = lax.top_k(logits, TOP_K)
    wts = jax.nn.softmax(top_v, axis=-1)
    gate = jnp.sum(jax.nn.one_hot(idx, N_EXPERTS, dtype=F32) * wts[..., None], axis=1)
    out = jnp.zeros((B * S, D), F32)
    for e in range(N_EXPERTS):
        out = out + gate[:, e:e + 1] * swiglu(t, w_gate[e], w_up[e], w_down[e]).astype(F32)
    return out.reshape(B, S, D)

def setup_inputs(seed: int = 0) -> dict:
    key = jax.random.key(seed)
    ks = iter(jax.random.split(key, 40))
    nrm = lambda shape, scale: jax.random.normal(next(ks), shape, F32) * scale
    gain = lambda shape: 1.0 + 0.02 * jax.random.normal(next(ks), shape, F32)
    L = DEPTH
    u_a = jax.random.uniform(next(ks), (L, LRU_W), F32, 0.9, 0.999)
    s_a = u_a ** (1.0 / LRU_C)
    dt0 = jnp.exp(jax.random.uniform(next(ks), (L, SSD_HEADS), F32, np.log(1e-3), np.log(1e-1)))
    return {
        'x': jax.random.normal(next(ks), (BATCH, SEQ, D_MODEL), F32),
        'positions': jnp.arange(SEQ, dtype=jnp.int32),
        'norm_mix': gain((L, D_MODEL)),
        'w_in': nrm((L, D_MODEL, IN_COLS), D_MODEL ** -0.5),
        'mla_q_norm': gain((L, MLA_Q_RANK)),
        'mla_w_uq': nrm((L, MLA_Q_RANK, MLA_HEADS * (MLA_NOPE + MLA_ROPE)), MLA_Q_RANK ** -0.5),
        'mla_kv_norm': gain((L, MLA_KV_RANK)),
        'mla_w_ukv': nrm((L, MLA_KV_RANK, MLA_HEADS * (MLA_NOPE + MLA_V)), MLA_KV_RANK ** -0.5),
        'nsa_cmp_pe': nrm((L, 2, CMP_LEN, NSA_HD), 0.02),
        'nsa_w_cmp': nrm((L, 2, CMP_LEN * NSA_HD, NSA_HD), (CMP_LEN * NSA_HD) ** -0.5),
        'lru_conv_w': nrm((L, CONV_W, LRU_W), CONV_W ** -0.5),
        'lru_conv_b': nrm((L, LRU_W), 0.01),
        'lru_w_gate': nrm((L, 2, LRU_BLOCKS, LRU_BW, LRU_BW), LRU_BW ** -0.5),
        'lru_b_gate': nrm((L, 2, LRU_W), 0.01),
        'lru_lambda': jnp.log(s_a / (1.0 - s_a)),
        'ssd_conv_w': nrm((L, CONV_W, SSD_XBC), CONV_W ** -0.5),
        'ssd_conv_b': nrm((L, SSD_XBC), 0.01),
        'ssd_dt_bias': dt0 + jnp.log(-jnp.expm1(-dt0)),
        'ssd_a_log': jnp.log(jax.random.uniform(next(ks), (L, SSD_HEADS), F32, 1.0, 16.0)),
        'ssd_d': gain((L, SSD_HEADS)),
        'group_norm': gain((L, 4, GROUP_W)),
        'w_out': nrm((L, D_MIX, D_MODEL), D_MIX ** -0.5),
        'norm_ffn': gain((L, D_MODEL)),
        'ffn_w_gate': nrm((N_DENSE, D_MODEL, D_FF), D_MODEL ** -0.5),
        'ffn_w_up': nrm((N_DENSE, D_MODEL, D_FF), D_MODEL ** -0.5),
        'ffn_w_down': nrm((N_DENSE, D_FF, D_MODEL), D_FF ** -0.5),
        'moe_router': nrm((N_MOE, D_MODEL, N_EXPERTS), D_MODEL ** -0.5),
        'moe_w_gate': nrm((N_MOE, N_EXPERTS, D_MODEL, D_FF), D_MODEL ** -0.5),
        'moe_w_up': nrm((N_MOE, N_EXPERTS, D_MODEL, D_FF), D_MODEL ** -0.5),
        'moe_w_down': nrm((N_MOE, N_EXPERTS, D_FF, D_MODEL), D_FF ** -0.5),
        'norm_final': gain((D_MODEL,)),
    }

def reference(x, positions, norm_mix, w_in, mla_q_norm, mla_w_uq, mla_kv_norm, mla_w_ukv,
              nsa_cmp_pe, nsa_w_cmp, lru_conv_w, lru_conv_b, lru_w_gate, lru_b_gate, lru_lambda,
              ssd_conv_w, ssd_conv_b, ssd_dt_bias, ssd_a_log, ssd_d, group_norm, w_out, norm_ffn,
              ffn_w_gate, ffn_w_up, ffn_w_down, moe_router, moe_w_gate, moe_w_up, moe_w_down,
              norm_final):
    cos_m, sin_m = rope_tables(positions, MLA_ROPE)
    cos_n, sin_n = rope_tables(positions, NSA_ROT)
    o1 = MLA_COLS
    o2 = o1 + NSA_COLS
    o3 = o2 + LRU_COLS
    h_res = x
    for l in range(DEPTH):
        h = rms_norm(h_res, norm_mix[l])
        u = h @ w_in[l]
        y_a = mla_mixer(u[..., :o1], cos_m, sin_m, mla_q_norm[l], mla_w_uq[l], mla_kv_norm[l], mla_w_ukv[l])
        y_b = nsa_mixer(u[..., o1:o2], cos_n, sin_n, nsa_cmp_pe[l], nsa_w_cmp[l])
        y_c = rglru_mixer(u[..., o2:o3], lru_conv_w[l], lru_conv_b[l], lru_w_gate[l], lru_b_gate[l], lru_lambda[l])
        y_d = ssd_mixer(u[..., o3:], ssd_conv_w[l], ssd_conv_b[l], ssd_dt_bias[l], ssd_a_log[l], ssd_d[l],
                        group_norm[l, 3])
        g = group_norm[l]
        y = jnp.concatenate([rms_norm(y_a, g[0]), rms_norm(y_b, g[1]), rms_norm(y_c, g[2]), y_d], axis=-1)
        h_res = h_res + y @ w_out[l]
        h = rms_norm(h_res, norm_ffn[l])
        if l % 2 == 0:
            f = swiglu(h, ffn_w_gate[l // 2], ffn_w_up[l // 2], ffn_w_down[l // 2])
        else:
            f = moe_ffn(h, moe_router[l // 2], moe_w_gate[l // 2], moe_w_up[l // 2], moe_w_down[l // 2])
        h_res = h_res + f
    return rms_norm(h_res, norm_final).astype(x.dtype)


_drawn_inputs = setup_inputs


def setup_inputs(seed=0):
    import zlib

    import numpy as np

    out = dict(_drawn_inputs(seed))
    spreads = {}
    factors = {'mla_q_norm': 3.422,
     'lru_b_gate': 8.0,
     'ssd_conv_b': 4.398,
     'ssd_d': 3.514,
     'norm_final': 2.942}
    for name, (base, spread) in spreads.items():
        noise = np.random.default_rng([zlib.crc32(name.encode()), seed]).standard_normal(out[name].shape)
        drawn = base * np.exp(spread * noise) if base else spread * noise
        out[name] = __import__('jax').numpy.asarray(drawn.astype(out[name].dtype))
    for name, factor in factors.items():
        out[name] = (out[name] * factor).astype(out[name].dtype)
    return out
```

```python
from contextlib import ExitStack

import numpy as np

import concourse.bass as bass
from concourse import mybir

F32 = mybir.dt.float32
I32 = mybir.dt.int32
U32 = mybir.dt.uint32
ALU = mybir.AluOpType
ACT = mybir.ActivationFunctionType
AX = mybir.AxisListType

P = 128
ROPE_THETA = 500000.0
EPS = 1e-6
NEG = -1e30
MLA_H, NOPE, ROPE, QR, KVR = 4, 64, 32, 192, 128
QK = NOPE + ROPE
HD, NROT, NH = 64, 16, 4
CSTRIDE, CLEN = 16, 32
SSD_H, SSD_G = 4, 2
GW = 256
RING = 7
SLOT = 2048
FC = 512


def trunk(nc, x, positions, norm_mix, w_in, mla_q_norm, mla_w_uq, mla_kv_norm, mla_w_ukv, nsa_cmp_pe,
          nsa_w_cmp, lru_conv_w, lru_conv_b, lru_w_gate, lru_b_gate, lru_lambda, ssd_conv_w, ssd_conv_b,
          ssd_dt_bias, ssd_a_log, ssd_d, group_norm, w_out, norm_ffn, ffn_w_gate, ffn_w_up, ffn_w_down,
          moe_router, moe_w_gate, moe_w_up, moe_w_down, norm_final, out):
    D = x.shape[2]
    S = x.shape[1]
    L = norm_mix.shape[0]
    TB = S // P
    KT = D // P
    FF = ffn_w_gate.shape[2]
    NCH = FF // FC
    FT = FC // P
    NE = moe_w_gate.shape[1]
    NC = S // CSTRIDE - 1
    O_NSA = QR + KVR + ROPE
    O_LRU = O_NSA + NH * HD + 6 * HD + 3 * NH
    O_SSD = O_LRU + 2 * GW
    O_XBC = O_SSD + GW
    O_DT = O_XBC + 3 * GW
    IN = O_DT + SSD_H
    assert L == 2 and TB == 2 and KT == 8 and FF % FC == 0 and w_in.shape[2] == IN
    assert S // 64 <= 16 and S <= 512
    UA = 512
    UB = O_LRU - UA
    UT = O_LRU + SSD_H
    MIX_SLOTS, FFN_SLOTS = 14, 6 * NCH
    assert MIX_SLOTS % RING == 0 and FFN_SLOTS % RING == 0
    BASE_MIX = [0, MIX_SLOTS + FFN_SLOTS]
    BASE_FFN = [MIX_SLOTS, 2 * MIX_SLOTS + FFN_SLOTS]
    JOBS = NE + 3
    JT = JOBS + 1

    ctx = ExitStack()
    with ctx:
        def sb(name, shape, dt=F32):
            return ctx.enter_context(nc.sbuf_tensor(name, shape, dt))

        def sem(name):
            return ctx.enter_context(nc.semaphore(name))

        ring = sb("ring", [P, RING, SLOT])
        ident = sb("ident", [P, P])
        upper = sb("upper", [P, P])
        strict = sb("strict", [P, P])
        ones = sb("ones", [P, P])
        cbias = sb("cbias", [P, 2 * P])
        cmask = sb("cmask", [P, TB, NC])
        cmbias = sb("cmbias", [P, TB, NC])
        iota = sb("iota", [P, P])
        minus_half = sb("minus_half", [P, 4])
        prow = sb("prow", [P, L, P])
        par = sb("par", [P, L, P])
        w_uq = sb("w_uq", [96, 2, 384])
        w_ukv = sb("w_ukv", [P, 512])
        w_cmp = sb("w_cmp", [P, CLEN, HD])
        pe_row = sb("pe_row", [CLEN, L, P])
        pe_t = sb("pe_t", [P, L, CLEN])
        lru_w = sb("lru_w", [P, L, 2, 2, P])
        ssd_par = sb("ssd_par", [P, L, 3, SSD_H])
        neg_a = sb("neg_a", [P, L, SSD_H])
        lru_c = sb("lru_c", [P, L, 4])
        lru_t = sb("lru_t", [P, L, 6, 2])
        half_b = sb("half_b", [P, L, 4])
        router = sb("router", [P, KT, NE])
        gfin = sb("gfin", [P, D])
        pos_i = sb("pos_i", [P, TB], I32)
        pos_f = sb("pos_f", [P, TB])
        inv = sb("inv", [P, 16])
        ang = sb("ang", [P, TB, 16])
        rk = sb("rk", [P, 2, TB, 16])
        rr = sb("rr", [P, 2, TB, 16])
        trig = sb("trig", [P, 2, TB, 16])
        xres = sb("xres", [P, TB, D])
        hn = sb("hn", [P, TB, D])
        hT = sb("hT", [P, KT, S])
        stat = sb("stat", [P, 44])
        rstd = sb("rstd", [P, 44])
        closed = sb("closed", [P, 1])
        hT_flag = sb("hT_flag", [P, 1])
        WORK = 24832
        work = sb("work", [P, WORK])
        used = [0]

        def take(*shape):
            n = int(np.prod(shape))
            at = used[0]
            used[0] += n
            assert used[0] <= WORK, used
            v = work[:, at:at + n]
            if len(shape) > 1:
                names = " ".join("abcd"[:len(shape)])
                v = v.rearrange(f"p ({names}) -> p {names}", **dict(zip("bcd", shape[1:])))
            return v

        lraw = take(4, 3 + S)
        xraw = take(6, 3 + S)
        ffn_scratch = used[0]
        utok = take(TB, UT)
        yT = take(KT, S)
        junk = take(2, 256)
        qk_scratch = used[0]
        cqn = take(TB, QR)
        ckvn = take(TB, KVR)
        cqT = take(2, S)
        ckvT = take(S)
        qtok = take(TB, MLA_H, QK)
        kcat = take(TB, MLA_H, QK)
        vtok = take(TB, MLA_H, HD)
        qT = take(MLA_H, S)
        kT = take(MLA_H, S)
        rt = take(4, TB * 4 * 16)
        nqT = take(NH, S)
        kvcT = take(S)
        ksT = take(S)
        kwT = take(S)
        qk_end = used[0]
        cin = take(CLEN, NC)
        kcT = take(NC)
        vc = take(HD)
        gates = take(TB, 3 * NH)
        yn = work[:, used[0]:used[0] + 3 * TB * GW].rearrange("p (i t c) -> p i t c", i=3, t=TB)
        prob = take(2, 4, S)
        probT = take(2, 8 * P)
        rmax = take(8, 4)
        rsum = take(8, 4)
        coef = take(8, 4)
        oa = take(TB, GW)
        ob = take(TB, GW)
        ot = take(GW)
        xb = take(2, S)
        xbc = take(6, S)
        zs = take(TB, GW)
        dts = take(6, TB, SSD_H)
        used[0] = qk_scratch
        lth = take(4, S)
        la = take(2, S)
        lt1 = take(2, S)
        lt2 = take(2, S)
        ld = take(2, S)
        lb = take(2, S)
        lgate = take(2, S)
        lrstd = take(S)
        xtok = take(TB, GW)
        xdt = take(TB, GW)
        nacs = take(TB, SSD_H)
        dec0 = take(SSD_H, S)
        dec1 = take(SSD_H, P)
        yd = take(TB, GW)
        assert used[0] <= qk_end
        used[0] = ffn_scratch
        xT = take(KT, P)
        sgate = take(2, FC)
        hid = take(2, FC)
        hidT = take(2, FT * P)
        ysb = take(D)
        pick = take(TB, P)
        pickw = take(TB, P)
        pickT = take(TB, P)
        logit = take(TB, NE)
        top = take(TB, 8)
        topf = take(TB, 8)
        topw = take(4, TB)
        hot = take(2, TB, NE)
        sel = take(TB, NE)
        gatew = take(TB, NE)
        rank1 = take(TB, NE)
        rank = take(TB, JT)
        jgate = take(TB, JT)
        cnt = take(NE)
        ovf = take(NE)
        ovpos = take(NE)
        in_job = take(NE)
        prod8 = take(TB, NE)
        steer_f = take(4)
        topi = sb("topi", [P, TB, 8], U32)
        steer = sb("steer", [1, 4], I32)

        banks = [ctx.enter_context(nc.psum_tensor(f"bank{i}", [P, 512], F32)) for i in range(8)]

        slot_full = [sem(f"slot_full{i}") for i in range(RING)]
        x_in, prow_in, mixw_in, misc_in = sem("x_in"), sem("prow_in"), sem("mixw_in"), sem("misc_in")
        consts_ready = sem("consts_ready")
        pool_chain, dve_chain, act_chain = sem("pool_chain"), sem("dve_chain"), sem("act_chain")
        for_dve, dve_took = sem("for_dve"), sem("dve_took")
        for_act, act_took = sem("for_act"), sem("act_took")
        lam_args, lam_logs, half_b_ready = sem("lam_args"), sem("lam_logs"), sem("half_b_ready")
        rope_args, trig_ready = sem("rope_args"), sem("trig_ready")
        ms_ready, rstd_ready = sem("ms_ready"), sem("rstd_ready")
        hn_ready, hT_ready, res_ready = sem("hn_ready"), sem("hT_ready"), sem("res_ready")
        cn_ready, cT_ready = sem("cn_ready"), sem("cT_ready")
        qk_roped, nsa_roped, cin_ready, gate_th = sem("qk_roped"), sem("nsa_roped"), sem("cin_ready"), sem("gate_th")
        cmp_ready, rmax_ready, exp_ready, masked = sem("cmp_ready"), sem("rmax_ready"), sem("exp_ready"), sem("masked")
        o_ready, yn_ready, yT_ready = sem("o_ready"), sem("yn_ready"), sem("yT_ready")
        lru_conv, ssd_conv = sem("lru_conv"), sem("ssd_conv")
        lru_vec, lru_act, ssd_vec, ssd_act = sem("lru_vec"), sem("lru_act"), sem("ssd_vec"), sem("ssd_act")
        dec_ready = sem("dec_ready")
        gate_done, up_done, silu_done, hid_ready = sem("gate_done"), sem("up_done"), sem("silu_done"), sem("hid_ready")
        hidT_done, hidT_ready, down_done = sem("hidT_done"), sem("hidT_ready"), sem("down_done")
        route_logits, route_diff, route_exp = sem("route_logits"), sem("route_diff"), sem("route_exp")
        sel_ready, ranks_done, steer_ready = sem("sel_ready"), sem("ranks_done"), sem("steer_ready")
        pick_ready, pickT_done, pickT_ready = sem("pick_ready"), sem("pickT_done"), sem("pickT_ready")
        xg_done, xT_ready = sem("xg_done"), sem("xT_ready")
        y_act, y_dve, comb_done, comb_took = sem("y_act"), sem("y_dve"), sem("comb_done"), sem("comb_took")
        job_closed = sem("job_closed")
        out_ready, out_stored = sem("out_ready"), sem("out_stored")

        PR, n = {}, 0
        for name, rows in (("mix", 8), ("ffn", 8), ("grp", 8), ("lcw", 8), ("lcb", 2), ("lbg", 4), ("lam", 2),
                           ("scw", 24), ("scb", 6), ("kvn", 1), ("qn", 2)):
            PR[name] = n
            n += rows
        assert n <= P
        N_PROW = 13 * L
        N_MISC = 1 + 3 * L + 8 * L + 2

        def pcol(l, name, i=0, rows=P):
            return par[0:rows, l, PR[name] + i:PR[name] + i + 1]

        def slot(p):
            return ring[:, p % RING, :]

        def slot_k(p):
            return slot(p).rearrange("p (k n) -> p k n", k=4)

        def slot_r(p):
            return slot(p).rearrange("p (k n) -> p k n", k=2)

        AJ = [(br, tb) for br in ("mla", "cmp", "sel", "win") for tb in range(TB)]
        KV0 = O_NSA + NH * HD
        FFN_ORDER = []
        for c in range(NCH + 1):
            if c < NCH:
                FFN_ORDER += [("gate", c), ("up", c)]
            if c >= 1:
                FFN_ORDER += [("down", c - 1)]
        AT = {key: 2 * i for i, key in enumerate(FFN_ORDER)}
        assert 2 * len(FFN_ORDER) == FFN_SLOTS
        DENSE = NCH * TB
        freed = {}
        mark = {}

        block = ctx.enter_context(nc.Block())

        @block.tensor
        def _(pe):
            gave = [0, 0]

            def bank(who):
                k = gave[who]
                gave[who] += 1
                if k >= 4:
                    pe.wait_ge((dve_took, act_took)[who], k - 3)
                return banks[4 * who + k % 4]

            def give(mm, who):
                mm.then_inc((for_dve, for_act)[who], 1)

            seen = [0] * RING

            def full(p, dmas=1):
                seen[p % RING] += 16 * dmas
                pe.wait_ge(slot_full[p % RING], seen[p % RING])

            def turn_normed():
                for g in range(4):
                    b = bank(0)
                    for k in range(2):
                        for tb in range(TB):
                            mm = pe.transpose(b[:, (2 * k + tb) * P:(2 * k + tb + 1) * P],
                                              hn[:, tb, (2 * g + k) * P:(2 * g + k + 1) * P], ident[:, :])
                    give(mm, 0)

            pe.wait_ge(consts_ready, 1)
            pe.wait_ge(prow_in, 16 * N_PROW)
            b = bank(0)
            for l in range(L):
                pe.transpose(b[:, l * P:(l + 1) * P], prow[:, l, :], ident[:, :])
            for l in range(L):
                mm = pe.transpose(b[:, 2 * P + l * CLEN:2 * P + (l + 1) * CLEN], pe_row[:, l, :],
                                  ident[0:CLEN, 0:CLEN])
            give(mm, 0)

            for l in range(L):
                pe.wait_ge(hn_ready, 2 * l + 1)
                turn_normed()
                pe.wait_ge(hT_ready, 2 * l + 1)
                p = BASE_MIX[l]

                for unit, n in ((0, UA), (1, UB + SSD_H)):
                    for h in range(2):
                        full(p + h, 1 + unit)
                    for tb in range(TB):
                        b = bank(1)
                        for k in range(KT):
                            mm = pe.matmul(b[:, 0:n], hT[:, k, tb * P:(tb + 1) * P],
                                           slot_k(p + k // 4)[:, k % 4, 0:n], start=(k == 0), stop=(k == KT - 1))
                        give(mm, 1)
                    for h in range(2):
                        freed[p + h] = (for_act, gave[1])
                    p += 2
                mark["u", l] = gave[1]
                for unit in range(3):
                    for h in range(2):
                        full(p + h, 2 if unit == 2 else 1)
                    for half in range(2):
                        b = bank(0)
                        for i in range(2):
                            if unit == 2 and half == 1:
                                for k in range(KT):
                                    mm = pe.matmul(b[:, i * GW:(i + 1) * GW], hT[:, k, i * P:(i + 1) * P],
                                                   slot_k(p + k // 4)[:, k % 4, GW:2 * GW], start=(k == 0),
                                                   stop=(k == KT - 1))
                            else:
                                c0 = (2 * half + i) * P
                                for k in range(KT):
                                    mm = pe.matmul(b[:, i * S:(i + 1) * S], slot_k(p + k // 4)[:, k % 4, c0:c0 + P],
                                                   hT[:, k, :], start=(k == 0), stop=(k == KT - 1))
                        give(mm, 0)
                    for h in range(2):
                        freed[p + h] = (for_dve, gave[0])
                    p += 2

                pe.wait_ge(cn_ready, l + 1)
                b = bank(0)
                for i in range(2):
                    for tb in range(TB):
                        mm = pe.transpose(b[0:96, (2 * i + tb) * P:(2 * i + tb + 1) * P],
                                          cqn[:, tb, i * 96:(i + 1) * 96], ident[:, :])
                give(mm, 0)
                b = bank(0)
                for tb in range(TB):
                    mm = pe.transpose(b[:, tb * P:(tb + 1) * P], ckvn[:, tb, :], ident[:, :])
                give(mm, 0)
                pe.wait_ge(cT_ready, l + 1)
                pe.wait_ge(mixw_in, 64 * (l + 1))
                for tb in range(TB):
                    b = bank(1)
                    for i in range(2):
                        mm = pe.matmul(b[:, 0:384], cqT[0:96, i, tb * P:(tb + 1) * P], w_uq[:, i, :],
                                       start=(i == 0), stop=(i == 1))
                    give(mm, 1)
                    b = bank(1)
                    give(pe.matmul(b[:, :], ckvT[:, tb * P:(tb + 1) * P], w_ukv[:, :], start=True, stop=True), 1)
                mark["qkv", l] = gave[1]

                pe.wait_ge(nsa_roped, l + 1)
                for hp in range(2):
                    b = bank(1)
                    for i in range(2):
                        c0 = O_NSA + (2 * hp + i) * HD
                        for tb in range(TB):
                            mm = pe.transpose(b[0:HD, (2 * i + tb) * P:(2 * i + tb + 1) * P],
                                              utok[:, tb, c0:c0 + HD], ident[:, :])
                    give(mm, 1)
                b = bank(1)
                for tb in range(TB):
                    pe.transpose(b[:, tb * P:(tb + 1) * P], utok[:, tb, KV0:KV0 + 2 * HD], ident[:, :])
                for tb in range(TB):
                    mm = pe.transpose(b[0:HD, S + tb * P:S + (tb + 1) * P],
                                      utok[:, tb, KV0 + 2 * HD:KV0 + 3 * HD], ident[:, :])
                give(mm, 1)
                b = bank(1)
                for tb in range(TB):
                    mm = pe.transpose(b[0:HD, tb * P:(tb + 1) * P],
                                      utok[:, tb, KV0 + 4 * HD:KV0 + 5 * HD], ident[:, :])
                give(mm, 1)
                mark["nsa", l] = gave[1]
                pe.wait_ge(qk_roped, l + 1)
                for src in (qtok, kcat):
                    for hp in range(2):
                        b = bank(1)
                        for i in range(2):
                            for tb in range(TB):
                                mm = pe.transpose(b[0:QK, (2 * i + tb) * P:(2 * i + tb + 1) * P],
                                                  src[:, tb, 2 * hp + i, :], ident[:, :])
                        give(mm, 1)
                pe.wait_ge(cin_ready, l + 1)
                b = bank(0)
                for j in range(CLEN):
                    pe.matmul(b[0:HD, 0:NC], w_cmp[0:HD, j, :], cin[0:HD, j, :], start=(j == 0),
                              stop=(j == CLEN - 1))
                for j in range(CLEN):
                    mm = pe.matmul(b[0:NC, 64:64 + HD], cin[HD:P, j, :], w_cmp[HD:P, j, :], start=(j == 0),
                                   stop=(j == CLEN - 1))
                give(mm, 0)
                mark["cmp", l] = gave[0]
                pe.wait_ge(act_took, gave[1])

                def scores(n):
                    br, tb = AJ[n]
                    t0, t1 = tb * P, (tb + 1) * P
                    nk = NC if br == "cmp" else t1
                    if br == "cmp":
                        pe.wait_ge(cmp_ready, l + 1)
                    per = 4 if br == "cmp" else 512 // nk
                    for g in range(4 // per):
                        b = bank(0)
                        for i in range(per):
                            h = g * per + i
                            q, k = {"mla": (qT[0:QK, h, t0:t1], kT[0:QK, h, 0:nk]),
                                    "cmp": (nqT[0:HD, h, t0:t1], kcT[0:HD, :]),
                                    "sel": (nqT[0:HD, h, t0:t1], ksT[0:HD, 0:nk]),
                                    "win": (nqT[0:HD, h, t0:t1], kwT[0:HD, 0:nk])}[br]
                            mm = pe.matmul(b[:, i * nk:(i + 1) * nk], q, k, start=True, stop=True)
                        give(mm, 0)

                def turn_probs(n):
                    br, tb = AJ[n]
                    pe.wait_ge(exp_ready, 8 * l + n + 1)
                    nb = 1 if br == "cmp" else tb + 1
                    if br == "cmp":
                        pe.wait_ge(masked, 2 * l + tb + 1)
                    rows = NC if br == "cmp" else P
                    for g in range(nb):
                        b = bank(1)
                        for i in range(4):
                            h, kb = divmod(4 * g + i, nb)
                            mm = pe.transpose(b[0:rows, i * P:(i + 1) * P],
                                              prob[:, n % 2, h, kb * P:kb * P + rows], ident[:, :])
                        give(mm, 1)
                    mark["probT", l, n] = gave[1]

                def products(n):
                    br, tb = AJ[n]
                    pe.wait_ge(act_took, mark["probT", l, n])
                    b = bank(0)
                    nb = 1 if br == "cmp" else tb + 1
                    for h in range(4):
                        for kb in range(nb):
                            i = h * nb + kb
                            rows = NC if br == "cmp" else P
                            v = {"mla": vtok[:, kb, h, :], "cmp": vc[0:NC, :],
                                 "sel": utok[:, kb, KV0 + 3 * HD:KV0 + 4 * HD],
                                 "win": utok[:, kb, KV0 + 5 * HD:KV0 + 6 * HD]}[br]
                            mm = pe.matmul(b[:, h * HD:(h + 1) * HD], probT[0:rows, n % 2, i * P:(i + 1) * P], v,
                                           start=(kb == 0), stop=(kb == nb - 1))
                    give(mm, 0)
                    mark["pv", l, n] = gave[0]

                for n in range(len(AJ) + 2):
                    if n < len(AJ):
                        scores(n)
                    if n >= 2:
                        products(n - 2)
                    if 1 <= n <= len(AJ):
                        turn_probs(n - 1)

                pe.wait_ge(lru_conv, l + 1)
                pe.wait_ge(misc_in, 16 * N_MISC)
                for g in range(2):
                    b = bank(1)
                    for i in range(2):
                        mm = pe.matmul(b[:, i * S:(i + 1) * S], lru_w[:, l, g, i, :], xb[:, i, :], start=True,
                                       stop=True)
                    give(mm, 1)
                mark["lgate", l] = gave[1]

                pe.wait_ge(ssd_act, 3 * l + 2)
                b = bank(0)
                for tb in range(TB):
                    for i in range(2):
                        mm = pe.transpose(b[:, tb * GW + i * P:tb * GW + (i + 1) * P],
                                          xbc[:, i, tb * P:(tb + 1) * P], ident[:, :])
                give(mm, 0)
                pe.wait_ge(ssd_vec, 4 * l + 2)
                b = bank(0)
                pe.matmul(b[:, 0:SSD_H], upper[:, :], dts[:, 5, 0, :], start=True, stop=True)
                pe.matmul(b[:, SSD_H:2 * SSD_H], ones[:, :], dts[:, 5, 0, :], start=True, stop=False)
                give(pe.matmul(b[:, SSD_H:2 * SSD_H], upper[:, :], dts[:, 5, 1, :], start=False, stop=True), 0)
                for hp in range(2):
                    b = bank(0)
                    for i in range(2):
                        h = 2 * hp + i
                        da = [dts[:, 5, tb, h:h + 1].broadcast_to([P, P]) for tb in range(TB)]
                        pe.matmul(b[:, i * S:i * S + P], da[0], upper[:, :], start=True, stop=True)
                        pe.matmul(b[:, i * S + P:(i + 1) * S], da[0], ones[:, :], start=True, stop=False)
                        mm = pe.matmul(b[:, i * S + P:(i + 1) * S], da[1], upper[:, :], start=False, stop=True)
                    give(mm, 0)
                for sb_ in range(TB):
                    b = bank(0)
                    n = S - sb_ * P
                    for g in range(SSD_G):
                        mm = pe.matmul(b[:, g * n:(g + 1) * n], xbc[:, 2 + g, sb_ * P:(sb_ + 1) * P],
                                       xbc[:, 4 + g, sb_ * P:S], start=True, stop=True)
                    give(mm, 0)
                pe.wait_ge(lru_act, 5 * l + 4)
                b = bank(0)
                for i in range(2):
                    mm = pe.matmul(b[:, 0:S], ones[:, :], lt1[:, i, :], start=(i == 0), stop=(i == 1))
                give(mm, 0)
                pe.wait_ge(dec_ready, l + 1)
                for tb in range(TB):
                    b = bank(0)
                    for h in range(SSD_H):
                        o = b[:, h * HD:(h + 1) * HD]
                        mm = pe.matmul(o, dec0[:, h, tb * P:(tb + 1) * P], xdt[:, 0, h * HD:(h + 1) * HD],
                                       start=True, stop=(tb == 0))
                        if tb == 1:
                            mm = pe.matmul(o, dec1[:, h, :], xdt[:, 1, h * HD:(h + 1) * HD], start=False, stop=True)
                    give(mm, 0)
                for i in range(3):
                    pe.wait_ge(yn_ready, 2 * l + (2 if i == 2 else 1))
                    b = bank(0)
                    for j in range(2):
                        for tb in range(TB):
                            mm = pe.transpose(b[:, (2 * j + tb) * P:(2 * j + tb + 1) * P],
                                              yn[:, i, tb, j * P:(j + 1) * P], ident[:, :])
                    give(mm, 0)

                pe.wait_ge(yT_ready, l + 1)
                for q in range(4):
                    full(p + q)
                for tb in range(TB):
                    for half in range(2):
                        b = bank(0)
                        for k in range(KT):
                            mm = pe.matmul(b[:, :], yT[:, k, tb * P:(tb + 1) * P],
                                           slot_r(p + k // 2)[:, k % 2, half * 512:(half + 1) * 512],
                                           start=(k == 0), stop=(k == KT - 1))
                        give(mm, 0)
                for q in range(4):
                    freed[p + q] = (for_dve, gave[0])

                pe.wait_ge(hn_ready, 2 * l + 2)
                turn_normed()
                pe.wait_ge(hT_ready, 2 * l + 2)
                pe.wait_ge(act_took, gave[1])
                pe.wait_ge(dve_took, gave[0])

                if l == 0:
                    base = BASE_FFN[0]

                    def down(s):
                        c, tb = divmod(s, TB)
                        q = base + AT["down", c]
                        if tb == 0:
                            full(q)
                            full(q + 1)
                        pe.wait_ge(hidT_ready, s + 1)
                        for half in range(2):
                            for f in range(FT):
                                mm = pe.matmul(banks[4 + 2 * tb + half][:, :],
                                               hidT[:, s % 2, f * P:(f + 1) * P],
                                               slot_r(q + f // 2)[:, f % 2, half * 512:(half + 1) * 512],
                                               start=(c == 0 and f == 0), stop=(c == NCH - 1 and f == FT - 1))
                        mm.then_inc(down_done, 1)

                    def turn_hid(s):
                        pe.wait_ge(hid_ready, s + 1)
                        for f in range(FT):
                            mm = pe.transpose(banks[2 + s % 2][:, f * P:(f + 1) * P],
                                              hid[:, s % 2, f * P:(f + 1) * P], ident[:, :])
                        mm.then_inc(hidT_done, 1)

                    for s in range(DENSE):
                        c, tb = divmod(s, TB)
                        for i, (w, done, left) in enumerate((("gate", gate_done, silu_done),
                                                             ("up", up_done, hidT_ready))):
                            q = base + AT[w, c]
                            if tb == 0:
                                full(q)
                                full(q + 1)
                            if s >= 2:
                                pe.wait_ge(left, s - 1)
                            for k in range(KT):
                                mm = pe.matmul(banks[2 * i + s % 2][:, :], hT[:, k, tb * P:(tb + 1) * P],
                                               slot_k(q + k // 4)[:, k % 4, :], start=(k == 0), stop=(k == KT - 1))
                            mm.then_inc(done, 1)
                        if s >= 2:
                            down(s - 2)
                        if s >= 1:
                            turn_hid(s - 1)
                    down(DENSE - 2)
                    turn_hid(DENSE - 1)
                    down(DENSE - 1)
                    pe.wait_ge(res_ready, 2)

            pe.wait_ge(misc_in, 16 * N_MISC)
            for tb in range(TB):
                for k in range(KT):
                    mm = pe.matmul(banks[0][:, tb * NE:(tb + 1) * NE], hT[:, k, tb * P:(tb + 1) * P],
                                   router[:, k, :], start=(k == 0), stop=(k == KT - 1))
            mm.then_inc(route_logits, 1)
            pe.wait_ge(sel_ready, 1)
            pe.matmul(banks[1][:, 0:NE], strict[:, :], sel[:, 0, :], start=True, stop=True)
            pe.matmul(banks[1][:, NE:2 * NE], ones[:, :], sel[:, 0, :], start=True, stop=False)
            pe.matmul(banks[1][:, NE:2 * NE], strict[:, :], sel[:, 1, :], start=False, stop=True)
            pe.matmul(banks[1][:, 2 * NE:3 * NE], ones[:, :], sel[:, 0, :], start=True, stop=False)
            pe.matmul(banks[1][:, 2 * NE:3 * NE], ones[:, :], sel[:, 1, :], start=False, stop=True)\
                .then_inc(ranks_done, 1)

            def gather(jobs_before):
                pe.wait_ge(pick_ready, jobs_before + 1)
                for d in range(KT):
                    for tb in range(TB):
                        mm = pe.matmul(banks[6 + d // 4][:, (d % 4) * P:(d % 4 + 1) * P],
                                       hn[:, tb, d * P:(d + 1) * P], pick[:, tb, :], start=(tb == 0),
                                       stop=(tb == TB - 1))
                mm.then_inc(xg_done, 1)

            gather(0)
            base = BASE_FFN[1]
            seen0 = list(seen)

            def job(j, s0):
                landed = [0] * RING

                def full_in_job(q):
                    i = (base + q) % RING
                    landed[i] += 16
                    pe.wait_ge(slot_full[i], j * (16 * FFN_SLOTS // RING) + (seen0[i] + landed[i]))

                def down(c):
                    q = AT["down", c]
                    full_in_job(q)
                    full_in_job(q + 1)
                    pe.wait_ge(hidT_ready, s0 + (c + 1))
                    for half in range(2):
                        for f in range(FT):
                            mm = pe.matmul(banks[4 + half][:, :], hidT[:, c % 2, f * P:(f + 1) * P],
                                           slot_r(base + q + f // 2)[:, f % 2, half * 512:(half + 1) * 512],
                                           start=(c == 0 and f == 0), stop=(c == NCH - 1 and f == FT - 1))
                    mm.then_inc(down_done, 1)

                def turn_hid(c):
                    pe.wait_ge(hid_ready, s0 + (c + 1))
                    for f in range(FT):
                        mm = pe.transpose(banks[2 + c % 2][:, f * P:(f + 1) * P],
                                          hid[:, c % 2, f * P:(f + 1) * P], ident[:, :])
                    mm.then_inc(hidT_done, 1)

                pe.wait_ge(xT_ready, j + 1)
                for c in range(NCH):
                    for i, (w, done, left) in enumerate((("gate", gate_done, silu_done),
                                                         ("up", up_done, hidT_ready))):
                        q = AT[w, c]
                        full_in_job(q)
                        full_in_job(q + 1)
                        pe.wait_ge(left, s0 + max(c - 1, 0))
                        for k in range(KT):
                            mm = pe.matmul(banks[2 * i + c % 2][:, :], xT[:, k, :],
                                           slot_k(base + q + k // 4)[:, k % 4, :], start=(k == 0),
                                           stop=(k == KT - 1))
                        mm.then_inc(done, 1)
                    if c == 2:
                        pe.wait_ge(comb_took, 2 * j + 2)
                    if c >= 2:
                        down(c - 2)
                    if c == 2:
                        pe.wait_ge(pick_ready, j + 1)
                        for tb in range(TB):
                            mm = pe.transpose(banks[6][:, tb * P:(tb + 1) * P], pickw[:, tb, :], ident[:, :])
                        mm.then_inc(pickT_done, 1)
                    if c >= 1:
                        turn_hid(c - 1)
                down(NCH - 2)
                turn_hid(NCH - 1)
                down(NCH - 1)
                pe.wait_ge(pickT_ready, j + 1)
                gather(j + 1)
                pe.wait_ge(y_act, j + 1)
                pe.wait_ge(y_dve, j + 1)
                for tb in range(TB):
                    if tb == 1:
                        pe.wait_ge(xT_ready, j + 2)
                    for half in range(2):
                        mm = pe.matmul(banks[4 + 2 * tb + half][:, :], pickT[:, tb, :],
                                       ysb[:, half * 512:(half + 1) * 512], start=True, stop=True)
                    mm.then_inc(comb_done, 1)

            with pe.Fori(0, NE) as e:
                job(e, e * NCH + DENSE)
            pe.wait_ge(steer_ready, 1)
            novf_r = pe.value_load(steer[0:1, 3:4], min_val=0, max_val=3)
            with pe.Fori(0, 3) as o:
                with pe.If(novf_r > o):
                    job(o + NE, o * NCH + (DENSE + NE * NCH))

        @block.sync
        def _(sp):
            def mixer_loads(l):
                p = BASE_MIX[l]
                for segs in ([(0, 0, UA)], [(0, UA, UB), (UB, O_DT, SSD_H)], [(0, O_LRU, 512)],
                             [(0, O_XBC, 512)], [(0, O_XBC + 512, 256), (256, O_SSD, GW)]):
                    for half in range(2):
                        rows = w_in[l, half * 512:(half + 1) * 512, :].rearrange("(k p) n -> p k n", p=P)
                        wait_free(p)
                        for at, src, n in segs:
                            sp.dma_start(slot_k(p)[:, :, at:at + n], rows[:, :, src:src + n])\
                                .then_inc(slot_full[p % RING], 16)
                        p += 1
                for q in range(4):
                    wait_free(p)
                    sp.dma_start(slot_r(p), w_out[l, q * 256:(q + 1) * 256, :].rearrange("(k p) n -> p k n", p=P))\
                        .then_inc(slot_full[p % RING], 16)
                    p += 1

            def wait_free(p):
                q = p - RING
                if q < 0:
                    return
                if q in freed:
                    sp.wait_ge(*freed[q])
                else:
                    w, c = FFN_ORDER[(q - BASE_FFN[0]) // 2]
                    sp.wait_ge({"gate": gate_done, "up": up_done, "down": down_done}[w], TB * (c + 1))

            def ffn_load(wg, wu, wd, at, p):
                (w, c), h = FFN_ORDER[at // 2], at % 2
                if w == "down":
                    r0 = c * FC + h * 256
                    dst, src = slot_r(p), wd[r0:r0 + 256, :]
                else:
                    dst = slot_k(p)
                    src = (wg if w == "gate" else wu)[h * 512:(h + 1) * 512, c * FC:(c + 1) * FC]
                sp.dma_start(dst, src.rearrange("(k p) n -> p k n", p=P)).then_inc(slot_full[p % RING], 16)

            def expert_loads(e, j, lo, hi, looked_up=False):
                waited = None
                for at in range(lo, hi):
                    w, c = FFN_ORDER[((at - RING) % FFN_SLOTS) // 2]
                    before = DENSE + c + 1 - (NCH if at < RING else 0)
                    if waited != (w, before):
                        waited = (w, before)
                        sp.wait_ge({"gate": gate_done, "up": up_done, "down": down_done}[w], j * NCH + before)
                        if looked_up:
                            sp.wait_ge(steer_ready, 1)
                    ffn_load(moe_w_gate[0, e], moe_w_up[0, e], moe_w_down[0, e], at, BASE_FFN[1] + at)

            mixer_loads(0)
            for at in range(FFN_SLOTS):
                wait_free(BASE_FFN[0] + at)
                ffn_load(ffn_w_gate[0], ffn_w_up[0], ffn_w_down[0], at, BASE_FFN[0] + at)
            mixer_loads(1)
            for at in range(RING):
                wait_free(BASE_FFN[1] + at)
                ffn_load(moe_w_gate[0, 0], moe_w_up[0, 0], moe_w_down[0, 0], at, BASE_FFN[1] + at)
            with sp.Fori(0, NE - 1) as e:
                expert_loads(e, e, RING, FFN_SLOTS)
                expert_loads(e + 1, e + 1, 0, RING)
            expert_loads(NE - 1, NE - 1, RING, FFN_SLOTS)
            sp.wait_ge(steer_ready, 1)
            novf_r = sp.value_load(steer[0:1, 3:4], min_val=0, max_val=3)
            with sp.Fori(0, 3) as o:
                with sp.If(novf_r > o):
                    ex = sp.value_load(steer[0:1, bass.ds(o, 1)], min_val=0, max_val=NE - 1)
                    expert_loads(ex, o + NE, 0, FFN_SLOTS, looked_up=True)
            for tb in range(TB):
                sp.wait_ge(out_ready, tb + 1)
                sp.dma_start(out[0, tb * P:(tb + 1) * P, :], hn[:, tb, :]).then_inc(out_stored, 16)
            sp.wait_ge(out_stored, 16 * TB)

        @block.gpsimd
        def _(pool):
            chain = [0]

            def link(ins):
                chain[0] += 1
                ins.then_inc(pool_chain, 1)
                pool.wait_ge(pool_chain, chain[0])

            for tb in range(TB):
                pool.dma_start(xres[:, tb, :], x[0, tb * P:(tb + 1) * P, :]).then_inc(x_in, 16)
            link(pool.memset(prow[:, :, :], 0.0))
            link(pool.memset(lru_w[:, :, :, :, :], 0.0))
            for l in range(L):
                def row(name, src, cols=P):
                    r0 = PR[name]
                    pool.dma_start(prow[r0:r0 + src.shape[0], l, 0:cols], src).then_inc(prow_in, 16)
                row("mix", norm_mix[l].rearrange("(a b) -> a b", b=P))
                row("ffn", norm_ffn[l].rearrange("(a b) -> a b", b=P))
                row("grp", group_norm[l].rearrange("g (a b) -> (g a) b", b=P))
                row("lcw", lru_conv_w[l].rearrange("g (a b) -> (g a) b", b=P))
                row("lcb", lru_conv_b[l].rearrange("(a b) -> a b", b=P))
                row("lbg", lru_b_gate[l].rearrange("g (a b) -> (g a) b", b=P))
                row("lam", lru_lambda[l].rearrange("(a b) -> a b", b=P))
                row("scw", ssd_conv_w[l].rearrange("g (a b) -> (g a) b", b=P))
                row("scb", ssd_conv_b[l].rearrange("(a b) -> a b", b=P))
                row("kvn", mla_kv_norm[l].rearrange("(a b) -> a b", b=P))
                row("qn", mla_q_norm[l].rearrange("(a b) -> a b", b=96), 96)
                for i in range(2):
                    pool.dma_start(pe_row[:, l, i * HD:(i + 1) * HD], nsa_cmp_pe[l, i]).then_inc(prow_in, 16)

            def mixer_weights(l):
                pool.dma_start(w_uq[:, :, :], mla_w_uq[l].rearrange("(i p) n -> p i n", p=96)).then_inc(mixw_in, 16)
                pool.dma_start(w_ukv[:, :], mla_w_ukv[l]).then_inc(mixw_in, 16)
                for i in range(2):
                    pool.dma_start(w_cmp[i * HD:(i + 1) * HD, :, :],
                                   nsa_w_cmp[l, i].rearrange("(j d) e -> d j e", d=HD)).then_inc(mixw_in, 16)

            pool.dma_start(pos_i[:, :], positions.rearrange("(t p) -> p t", p=P),
                           allow_slow_non_contiguous=True).then_inc(misc_in, 16)
            for l in range(L):
                for i, src in enumerate((ssd_dt_bias, ssd_a_log, ssd_d)):
                    pool.dma_start(ssd_par[:, l, i, :], src[l, :].partition_broadcast(P)).then_inc(misc_in, 16)
                for g in range(2):
                    for b in range(4):
                        o = (b % 2) * 64
                        pool.dma_start(lru_w[o:o + 64, l, g, b // 2, o:o + 64], lru_w_gate[l, g, b])\
                            .then_inc(misc_in, 16)
            pool.dma_start(router[:, :, :], moe_router[0].rearrange("(k p) e -> p k e", p=P)).then_inc(misc_in, 16)
            pool.dma_start(gfin[:, :], norm_final[:].partition_broadcast(P)).then_inc(misc_in, 16)
            mixer_weights(0)

            link(pool.memset(ones[:, :], 1.0))
            link(pool.memset(ident[:, :], 0.0))
            link(pool.memset(cbias[:, :], 0.0))
            link(pool.memset(cmask[:, :, :], 1.0))
            link(pool.memset(cmbias[:, :, :], 0.0))
            link(pool.memset(minus_half[:, :], -0.5))
            link(pool.memset(lraw[:, 0:2, 0:3], 0.0))
            link(pool.memset(xraw[:, :, 0:3], 0.0))
            inv_freq = np.float32(ROPE_THETA) ** (-np.arange(0, ROPE, 2, dtype=np.float32) / np.float32(ROPE))
            for i in range(16):
                link(pool.memset(inv[:, i:i + 1], float(inv_freq[i])))
            link(pool.affine_select(out=ident[:, :], in_=ident[:, :], compare_op=ALU.not_equal, fill=1.0, base=0,
                                    pattern=[[-1, P]], channel_multiplier=1))
            link(pool.affine_select(out=upper[:, :], in_=ones[:, :], compare_op=ALU.is_ge, fill=0.0, base=0,
                                    pattern=[[1, P]], channel_multiplier=-1))
            link(pool.affine_select(out=strict[:, :], in_=ones[:, :], compare_op=ALU.is_ge, fill=0.0, base=-1,
                                    pattern=[[1, P]], channel_multiplier=-1))
            link(pool.affine_select(out=cbias[:, P:2 * P], in_=cbias[:, P:2 * P], compare_op=ALU.is_ge, fill=NEG,
                                    base=0, pattern=[[-1, P]], channel_multiplier=1))
            for tb in range(TB):
                for m, fill in ((cmask, 0.0), (cmbias, NEG)):
                    link(pool.affine_select(out=m[:, tb, :], in_=m[:, tb, :], compare_op=ALU.is_ge, fill=fill,
                                            base=tb * P - (CLEN - 1), pattern=[[-CSTRIDE, NC]],
                                            channel_multiplier=1))
            pool.iota(iota[:, :], pattern=[[1, P]], base=0, channel_multiplier=0,
                      allow_small_or_imprecise_dtypes=True).then_inc(consts_ready, 1)
            pool.wait_ge(consts_ready, 1)

            sets = [0, 0]

            def roots(n):
                c0 = 4 * sets[0]
                sets[0] += 1
                sets[1] += n
                pool.wait_ge(ms_ready, sets[1])
                link(pool.tensor_scalar(stat[:, c0:c0 + n], stat[:, c0:c0 + n], EPS, None, ALU.add))
                pool.tensor_tensor(rstd[:, c0:c0 + n], stat[:, c0:c0 + n], minus_half[:, 0:n], ALU.pow)\
                    .then_inc(rstd_ready, 1)

            for l in range(L):
                roots(2)
                roots(4)
                if l == 0:
                    pool.wait_ge(for_dve, mark["cmp", 0])
                    mixer_weights(1)
                roots(4)
                roots(2)
                roots(2)
            roots(2)

        @block.scalar
        def _(act):
            chain = [0]
            took = [0]

            def link(ins):
                chain[0] += 1
                ins.then_inc(act_chain, 1)
                act.wait_ge(act_chain, chain[0])

            def filled():
                b = banks[4 + took[0] % 4]
                took[0] += 1
                act.wait_ge(for_act, took[0])
                return b

            squares = [0]

            def mean_square(dst_set, i, src, n, to):
                if squares[0]:
                    act.wait_ge(ms_ready, squares[0])
                squares[0] += 1
                act.activation(to, src, ACT.Square, scale=float(n) ** -0.5,
                               accum_out=stat[:, 4 * dst_set + i:4 * dst_set + i + 1]).then_inc(ms_ready, 1)

            act.wait_ge(x_in, 16 * TB)
            act.wait_ge(rope_args, 1)
            act.activation(trig[:, :, :, :], rr[:, :, :, :], ACT.Sin).then_inc(trig_ready, 1)
            act.wait_ge(misc_in, 16 * N_MISC)
            act.activation(neg_a[:, :, :], ssd_par[:, :, 1, :], ACT.Exp).then_inc(lam_logs, 1)
            act.wait_ge(lam_args, 1)
            act.activation(lru_t[:, :, 1, :], lru_t[:, :, 0, :], ACT.Exp).then_inc(lam_logs, 1)
            act.wait_ge(lam_logs, 2)
            act.activation(lru_t[:, :, 3, :], lru_t[:, :, 1, :], ACT.Ln, bias=1.0).then_inc(lam_logs, 1)

            for l in range(L):
                if l > 0:
                    act.wait_ge(res_ready, 2 * l)
                for tb in range(TB):
                    mean_square(5 * l, tb, xres[:, tb, :], D, hn[:, tb, :])
                for unit, n in ((0, UA), (1, UB + SSD_H)):
                    for tb in range(TB):
                        b = filled()
                        act.activation(utok[:, tb, unit * UA:unit * UA + n], b[:, 0:n], ACT.Copy)\
                            .then_inc(act_took, 1)
                act.wait_ge(act_took, took[0])
                for tb in range(TB):
                    mean_square(5 * l + 1, tb, utok[:, tb, 0:QR], QR, junk[:, 0, 0:QR])
                    mean_square(5 * l + 1, 2 + tb, utok[:, tb, QR:QR + KVR], KVR, junk[:, 1, 0:KVR])
                act.activation(gates[:, :, :], utok[:, :, O_LRU - 3 * NH:O_LRU], ACT.Tanh, scale=0.5)\
                    .then_inc(gate_th, 1)
                act.wait_ge(ssd_vec, 4 * l + 1)
                link(act.activation(dts[:, 2, :, :], dts[:, 1, :, :], ACT.Exp, scale=-1.0))
                act.activation(dts[:, 3, :, :], dts[:, 2, :, :], ACT.Ln, bias=1.0).then_inc(ssd_act, 1)
                for tb in range(TB):
                    b = filled()
                    act.activation(qtok[:, tb, :, :], b[:, 0:MLA_H * QK].rearrange("p (h d) -> p h d", h=MLA_H),
                                   ACT.Copy).then_inc(act_took, 1)
                    v = filled()[:, :].rearrange("p (h d) -> p h d", h=MLA_H)
                    act.activation(kcat[:, tb, :, 0:NOPE], v[:, :, 0:NOPE], ACT.Copy)
                    act.activation(vtok[:, tb, :, :], v[:, :, NOPE:], ACT.Copy).then_inc(act_took, 1)
                for hp in range(2):
                    b = filled()
                    act.activation(nqT[0:HD, 2 * hp:2 * hp + 2, :],
                                   b[0:HD, :].rearrange("p (h t) -> p h t", h=2), ACT.Copy).then_inc(act_took, 1)
                b = filled()
                act.activation(kvcT[:, :], b[:, 0:S], ACT.Copy)
                act.activation(ksT[0:HD, :], b[0:HD, S:2 * S], ACT.Copy).then_inc(act_took, 1)
                b = filled()
                act.activation(kwT[0:HD, :], b[0:HD, 0:S], ACT.Copy).then_inc(act_took, 1)
                for dst in (qT, kT):
                    for hp in range(2):
                        b = filled()
                        act.activation(dst[0:QK, 2 * hp:2 * hp + 2, :],
                                       b[0:QK, :].rearrange("p (h t) -> p h t", h=2), ACT.Copy)\
                            .then_inc(act_took, 1)

                def exps(n):
                    br, tb = AJ[n]
                    nk = NC if br == "cmp" else (tb + 1) * P
                    act.wait_ge(rmax_ready, 8 * l + n + 1)
                    for h in range(4):
                        e = act.activation(prob[:, n % 2, h, 0:nk], prob[:, n % 2, h, 0:nk], ACT.Exp,
                                           bias=rmax[:, n, h:h + 1], accum_out=rsum[:, n, h:h + 1])
                    e.then_inc(exp_ready, 1)

                def turned_probs(n):
                    br, tb = AJ[n]
                    if n >= 2:
                        act.wait_ge(for_dve, mark["pv", l, n - 2])
                    rows = NC if br == "cmp" else P
                    for i in range(1 if br == "cmp" else tb + 1):
                        b = filled()
                        act.activation(probT[0:rows, n % 2, i * 512:(i + 1) * 512], b[0:rows, :], ACT.Copy)\
                            .then_inc(act_took, 1)

                for n in range(len(AJ) + 1):
                    if n < len(AJ):
                        exps(n)
                    if n >= 1:
                        turned_probs(n - 1)

                act.wait_ge(o_ready, l + 1)
                for i, o in enumerate((oa, ob)):
                    for tb in range(TB):
                        mean_square(5 * l + 2, 2 * i + tb, o[:, tb, :], GW, junk[:, 0, :])

                act.wait_ge(half_b_ready, 1)
                for g in range(2):
                    b = filled()
                    for i in range(2):
                        e = act.activation(lth[:, 2 * g + i, :], b[:, i * S:(i + 1) * S], ACT.Tanh, scale=0.5,
                                           bias=half_b[:, l, 2 * g + i:2 * g + i + 1])
                    e.then_inc(act_took, 1)
                act.wait_ge(lru_vec, 5 * l + 1)
                act.activation(lt1[:, :, :], la[:, :, :], ACT.Tanh)
                act.activation(lt2[:, :, :], la[:, :, :], ACT.Tanh, scale=0.5).then_inc(lru_act, 1)
                act.wait_ge(lru_vec, 5 * l + 2)
                act.activation(lgate[:, :, :], lgate[:, :, :], ACT.Tanh, scale=float(np.sqrt(2 / np.pi)))\
                    .then_inc(lru_act, 1)
                act.wait_ge(ssd_conv, l + 1)
                act.activation(xbc[:, :, :], xbc[:, :, :], ACT.Silu)
                act.activation(zs[:, :, :], zs[:, :, :], ACT.Silu).then_inc(ssd_act, 1)
                act.wait_ge(lru_vec, 5 * l + 3)
                act.activation(lb[:, :, :], lb[:, :, :], ACT.Sqrt).then_inc(lru_act, 1)
                act.wait_ge(lru_vec, 5 * l + 4)
                act.activation(lt1[:, :, :], xb[:, :, :], ACT.Square, scale=GW ** -0.5).then_inc(lru_act, 1)
                act.wait_ge(ssd_vec, 4 * l + 3)
                act.activation(dec0[:, :, :], dec0[:, :, :], ACT.Exp)
                act.activation(dec1[:, :, :], dec1[:, :, :], ACT.Exp).then_inc(ssd_act, 1)
                act.wait_ge(lru_vec, 5 * l + 5)
                act.activation(lrstd[:, :], lrstd[:, :], ACT.Sqrt).then_inc(lru_act, 1)
                act.wait_ge(ssd_vec, 4 * l + 4)
                for tb in range(TB):
                    mean_square(5 * l + 3, tb, yd[:, tb, :], GW, junk[:, 1, :])

                act.wait_ge(res_ready, 2 * l + 1)
                for tb in range(TB):
                    mean_square(5 * l + 4, tb, xres[:, tb, :], D, hn[:, tb, :])
                if l == 0:
                    for s in range(DENSE + 1):
                        if s < DENSE:
                            act.wait_ge(gate_done, s + 1)
                            if s >= 2:
                                act.wait_ge(hid_ready, s - 1)
                            act.activation(sgate[:, s % 2, :], banks[s % 2][:, :], ACT.Silu)\
                                .then_inc(silu_done, 1)
                        if s >= 1:
                            act.wait_ge(hidT_done, s)
                            if s >= 3:
                                act.wait_ge(down_done, s - 2)
                            act.activation(hidT[:, (s - 1) % 2, :], banks[2 + (s - 1) % 2][:, :], ACT.Copy)\
                                .then_inc(hidT_ready, 1)

            act.wait_ge(route_diff, 1)
            act.activation(topw[:, 1, :], topw[:, 0, :], ACT.Exp).then_inc(route_exp, 1)

            def job(s0):
                for c in range(NCH + 1):
                    if c < NCH:
                        act.wait_ge(gate_done, s0 + (c + 1))
                        act.wait_ge(hid_ready, s0 + (c - 1))
                        act.activation(sgate[:, c % 2, :], banks[c % 2][:, :], ACT.Silu).then_inc(silu_done, 1)
                    if c >= 1:
                        act.wait_ge(hidT_done, s0 + c)
                        act.wait_ge(down_done, s0 + (c - 2))
                        act.activation(hidT[:, (c - 1) % 2, :], banks[2 + (c - 1) % 2][:, :], ACT.Copy)\
                            .then_inc(hidT_ready, 1)
                act.wait_ge(down_done, s0 + NCH)
                act.activation(ysb[:, 0:512], banks[4][:, :], ACT.Copy).then_inc(y_act, 1)

            with act.Fori(0, NE) as e:
                job(e * NCH + DENSE)
            act.wait_ge(steer_ready, 1)
            novf_r = act.value_load(steer[0:1, 3:4], min_val=0, max_val=3)
            with act.Fori(0, 3) as o:
                with act.If(novf_r > o):
                    job(o * NCH + (DENSE + NE * NCH))

        @block.vector
        def _(dve):
            chain = [0]
            took = [0]

            def link(ins):
                chain[0] += 1
                ins.then_inc(dve_chain, 1)
                dve.wait_ge(dve_chain, chain[0])

            counts = {}

            def signal(ins, name, s):
                counts[name] = counts.get(name, 0) + 1
                ins.then_inc(s, 1)
                dve.wait_ge(s, counts[name])

            def filled():
                b = banks[took[0] % 4]
                took[0] += 1
                dve.wait_ge(for_dve, took[0])
                return b

            def take_bank(ins):
                ins.then_inc(dve_took, 1)
                dve.wait_ge(dve_took, took[0])

            dve.wait_ge(consts_ready, 1)
            dve.wait_ge(misc_in, 16 * N_MISC)
            link(dve.tensor_copy(pos_f[:, :], pos_i[:, :]))
            for tb in range(TB):
                link(dve.tensor_scalar(ang[:, tb, :], inv[:, :], pos_f[:, tb:tb + 1], None, ALU.mult))
            TURN = 2 * np.pi
            MAGIC = 1.5 * 2.0 ** 23
            PARTS = [6.28125, 1.93500518798828125e-3]
            PARTS.append(TURN - sum(PARTS))
            for i in range(2):
                link(dve.tensor_scalar(rk[:, i, :, :], ang[:, :, :], 1 / TURN, 0.25 * i, ALU.mult, ALU.add))
                link(dve.tensor_scalar(rk[:, i, :, :], rk[:, i, :, :], MAGIC, None, ALU.add))
                link(dve.tensor_scalar(rk[:, i, :, :], rk[:, i, :, :], -MAGIC, None, ALU.add))
                src = ang
                for part in PARTS:
                    s_ = src[:, :, :] if src is ang else rr[:, i, :, :]
                    link(dve.scalar_tensor_tensor(out=rr[:, i, :, :], in0=rk[:, i, :, :], scalar=-part, in1=s_,
                                                  op0=ALU.mult, op1=ALU.add))
                    src = rr
            link(dve.tensor_scalar(rr[:, 1, :, :], rr[:, 1, :, :], np.pi / 2, None, ALU.add))
            signal(dve.tensor_scalar(rr[:, :, :, :], rr[:, :, :, :], -3.1415925, 3.1415925, ALU.max, ALU.min),
                   "rope", rope_args)

            b = filled()
            link(dve.tensor_copy(par[:, :, :], b[:, 0:2 * P].rearrange("p (l c) -> p l c", l=L)))
            take_bank(dve.tensor_copy(pe_t[:, :, :], b[:, 2 * P:2 * P + L * CLEN].rearrange("p (l c) -> p l c", l=L)))
            lam = par[:, :, PR["lam"]:PR["lam"] + 2]
            link(dve.tensor_scalar(lru_t[:, :, 5, :], lam, -1.0, None, ALU.mult))
            signal(dve.tensor_tensor(lru_t[:, :, 0, :], lru_t[:, :, 5, :], lam, ALU.min), "lam", lam_args)
            signal(dve.tensor_scalar(half_b[:, :, :], par[:, :, PR["lbg"]:PR["lbg"] + 4], 0.5, None, ALU.mult),
                   "half_b", half_b_ready)
            dve.wait_ge(lam_logs, 3)
            e_, w_, lg, d_, t_ = (lru_t[:, :, i, :] for i in (1, 2, 3, 4, 5))
            link(dve.tensor_scalar(w_, e_, 1.0, None, ALU.add))
            link(dve.tensor_scalar(w_, w_, -1.0, None, ALU.add))
            link(dve.tensor_scalar(d_, w_, 1e-30, None, ALU.max))
            link(dve.reciprocal(d_, d_))
            link(dve.tensor_tensor(lg, lg, e_, ALU.mult))
            link(dve.tensor_tensor(lg, lg, d_, ALU.mult))
            link(dve.scalar_tensor_tensor(out=w_, in0=w_, scalar=0.0, in1=e_, op0=ALU.is_equal, op1=ALU.mult))
            link(dve.tensor_tensor(lg, lg, w_, ALU.add))
            link(dve.scalar_tensor_tensor(out=lg, in0=t_, scalar=0.0, in1=lg, op0=ALU.max, op1=ALU.add))
            link(dve.tensor_scalar(lru_c[:, :, 0:2], lg, -4.0, None, ALU.mult))
            dve.wait_ge(trig_ready, 1)
            dve.wait_ge(x_in, 16 * TB)

            def normed(l2, turn_set):
                dve.wait_ge(rstd_ready, turn_set + 1)
                for tb in range(TB):
                    ins = dve.tensor_scalar(hn[:, tb, :], xres[:, tb, :],
                                            rstd[:, 4 * turn_set + tb:4 * turn_set + tb + 1], None, ALU.mult)
                    if tb == TB - 1:
                        signal(ins, "hn", hn_ready)
                l, which = divmod(l2, 2)
                c0 = PR["ffn" if which else "mix"]
                for g in range(4):
                    b = filled()
                    gain = par[:, l, c0 + 2 * g:c0 + 2 * g + 2].unsqueeze(2).broadcast_to([P, 2, S])
                    take_bank(dve.tensor_tensor(hT[:, 2 * g:2 * g + 2, :], b[:, :].rearrange("p (k t) -> p k t", k=2),
                                                gain, ALU.mult))
                signal(dve.tensor_copy(hT_flag[:, 0:1], ones[:, 0:1]), "hT", hT_ready)

            def rope(v, cos, sin, shape):
                n = int(np.prod(shape[1:]))
                names = " ".join("abc"[:len(shape) - 1])
                r = [rt[:, i, 0:n].rearrange(f"p ({names}) -> p {names}", **dict(zip("bc", shape[2:])))
                     if len(shape) > 2 else rt[:, i, 0:n] for i in range(4)]
                for i, (a, t) in enumerate(((v[0], cos), (v[1], sin), (v[1], cos), (v[0], sin))):
                    link(dve.tensor_tensor(r[i], a, t, ALU.mult))
                link(dve.tensor_tensor(v[0], r[0], r[1], ALU.subtract))
                return dve.tensor_tensor(v[1], r[2], r[3], ALU.add)

            for l in range(L):
                normed(2 * l, 5 * l)

                dve.wait_ge(act_took, mark["u", l])
                bias = ssd_par[:, l, 0:1, :].broadcast_to([P, TB, SSD_H])
                link(dve.tensor_tensor(dts[:, 0, :, :], utok[:, :, O_LRU:O_LRU + SSD_H], bias, ALU.add))
                link(dve.tensor_scalar(dts[:, 1, :, :], dts[:, 0, :, :], -1.0, None, ALU.mult))
                signal(dve.tensor_tensor(dts[:, 1, :, :], dts[:, 1, :, :], dts[:, 0, :, :], ALU.max),
                       "ssd_vec", ssd_vec)
                dve.wait_ge(rstd_ready, 5 * l + 2)
                r0 = 4 * (5 * l + 1)
                for tb in range(TB):
                    link(dve.tensor_scalar(cqn[:, tb, :], utok[:, tb, 0:QR], rstd[:, r0 + tb:r0 + tb + 1], None,
                                           ALU.mult))
                    ins = dve.tensor_scalar(ckvn[:, tb, :], utok[:, tb, QR:QR + KVR],
                                            rstd[:, r0 + 2 + tb:r0 + 3 + tb], None, ALU.mult)
                    if tb == 0:
                        link(ins)
                    else:
                        signal(ins, "cn", cn_ready)
                cosn, sinn = trig[:, 1, :, 0:16:2], trig[:, 0, :, 0:16:2]
                for c0, n, step in ((O_NSA, NH, HD), (KV0, 3, 2 * HD)):
                    v = utok[:, :, c0:c0 + n * step].rearrange("p t (h d) -> p t h d", h=n)
                    sh = [P, TB, n, NROT // 2]
                    ins = rope((v[:, :, :, 0:8], v[:, :, :, 8:16]), cosn.unsqueeze(2).broadcast_to(sh),
                               sinn.unsqueeze(2).broadcast_to(sh), sh)
                    if c0 == O_NSA:
                        link(ins)
                    else:
                        signal(ins, "nsa_roped", nsa_roped)
                v = utok[:, :, QR + KVR:QR + KVR + ROPE]
                link(rope((v[:, :, 0:16], v[:, :, 16:32]), trig[:, 1, :, :], trig[:, 0, :, :], [P, TB, 16]))

                for i in range(2):
                    b = filled()
                    take_bank(dve.tensor_copy(lraw[:, 2 * i:2 * i + 2, 3:3 + S],
                                              b[:, :].rearrange("p (k t) -> p k t", k=2)))
                for i in range(3):
                    b = filled()
                    take_bank(dve.tensor_copy(xraw[:, 2 * i:2 * i + 2, 3:3 + S],
                                              b[:, :].rearrange("p (k t) -> p k t", k=2)))
                b = filled()
                take_bank(dve.tensor_copy(zs[:, :, :], b[:, :].rearrange("p (k t) -> p k t", k=2)))

                b = filled()
                gain = par[0:96, l, PR["qn"]:PR["qn"] + 2].unsqueeze(2).broadcast_to([96, 2, S])
                take_bank(dve.tensor_tensor(cqT[0:96, :, :], b[0:96, :].rearrange("p (k t) -> p k t", k=2), gain,
                                            ALU.mult))
                b = filled()
                take_bank(dve.tensor_scalar(ckvT[:, :], b[:, 0:S], pcol(l, "kvn"), None, ALU.mult))
                signal(dve.tensor_copy(hT_flag[:, 0:1], ones[:, 0:1]), "cT", cT_ready)

                def conv(dst, raw, w, bias_, n):
                    for i in range(n):
                        link(dve.tensor_scalar(dst[:, i, :], raw[:, i, 0:S], pcol(l, w, i), pcol(l, bias_, i),
                                               ALU.mult, ALU.add))
                        for t in range(1, 4):
                            ins = dve.scalar_tensor_tensor(out=dst[:, i, :], in0=raw[:, i, t:t + S],
                                                           scalar=pcol(l, w, n * t + i), in1=dst[:, i, :],
                                                           op0=ALU.mult, op1=ALU.add)
                            if not (t == 3 and i == n - 1):
                                link(ins)
                    return ins

                signal(conv(xb, lraw, "lcw", "lcb", 2), "lru_conv", lru_conv)

                dve.wait_ge(act_took, mark["qkv", l])
                sh = [P, TB, MLA_H, ROPE // 2]
                v = qtok[:, :, :, NOPE:QK]
                link(rope((v[:, :, :, 0:16], v[:, :, :, 16:32]), trig[:, 1, :, :].unsqueeze(2).broadcast_to(sh),
                          trig[:, 0, :, :].unsqueeze(2).broadcast_to(sh), sh))
                kpe = utok[:, :, QR + KVR:QR + KVR + ROPE].unsqueeze(2).broadcast_to([P, TB, MLA_H, ROPE])
                signal(dve.tensor_copy(kcat[:, :, :, NOPE:QK], kpe), "qk_roped", qk_roped)

                dve.wait_ge(act_took, mark["nsa", l])
                for i in range(2):
                    src = kvcT[:, 16 * i:16 * i + 16 * NC].rearrange("p (n j) -> p j n", j=16)
                    pos = pe_t[:, l, 16 * i:16 * i + 16].unsqueeze(2).broadcast_to([P, 16, NC])
                    ins = dve.tensor_tensor(cin[:, 16 * i:16 * i + 16, :], src, pos, ALU.add)
                    if i == 0:
                        link(ins)
                    else:
                        signal(ins, "cin", cin_ready)
                signal(conv(xbc, xraw, "scw", "scb", 6), "ssd_conv", ssd_conv)
                b = filled()
                link(dve.tensor_copy(kcT[0:HD, :], b[0:HD, 0:NC]))
                take_bank(dve.tensor_copy(vc[0:NC, :], b[0:NC, 64:64 + HD]))
                signal(dve.tensor_copy(hT_flag[:, 0:1], ones[:, 0:1]), "cmp", cmp_ready)
                dve.wait_ge(gate_th, l + 1)
                link(dve.tensor_scalar(gates[:, :, :], gates[:, :, :], 0.5, 0.5, ALU.mult, ALU.add))

                def score_rows(n):
                    br, tb = AJ[n]
                    nk = NC if br == "cmp" else (tb + 1) * P
                    if n >= 2:
                        dve.wait_ge(act_took, mark["probT", l, n - 2])
                    per = 4 if br == "cmp" else 512 // nk
                    scale = float(QK if br == "mla" else HD) ** -0.5
                    m = cmbias[:, tb, :] if br == "cmp" else cbias[:, P - tb * P:2 * P]
                    for g in range(4 // per):
                        b = filled()
                        take_bank(dve.scalar_tensor_tensor(
                            out=prob[:, n % 2, g * per:(g + 1) * per, 0:nk],
                            in0=b[:, 0:per * nk].rearrange("p (h k) -> p h k", h=per), scalar=scale,
                            in1=m.unsqueeze(1).broadcast_to([P, per, nk]), op0=ALU.mult, op1=ALU.add))
                    link(dve.tensor_reduce(rmax[:, n, :], prob[:, n % 2, :, 0:nk], AX.X, ALU.max))
                    signal(dve.tensor_scalar(rmax[:, n, :], rmax[:, n, :], -1.0, None, ALU.mult),
                           "rmax", rmax_ready)

                def mask_cmp(n):
                    tb = AJ[n][1]
                    dve.wait_ge(exp_ready, 8 * l + n + 1)
                    signal(dve.tensor_tensor(prob[:, n % 2, :, 0:NC], prob[:, n % 2, :, 0:NC],
                                             cmask[:, tb:tb + 1, :].broadcast_to([P, 4, NC]), ALU.mult),
                           "masked", masked)

                def outputs(n):
                    br, tb = AJ[n]
                    dve.wait_ge(exp_ready, 8 * l + n + 1)
                    link(dve.reciprocal(coef[:, n, :], rsum[:, n, :]))
                    if br != "mla":
                        i = ("cmp", "sel", "win").index(br)
                        link(dve.tensor_tensor(coef[:, n, :], coef[:, n, :],
                                               gates[:, tb, i:i + 3 * NH - 2:3], ALU.mult))
                    b = filled()
                    c = coef[:, n, :].unsqueeze(2).broadcast_to([P, 4, HD])
                    dst = {"mla": oa[:, tb, :], "cmp": ob[:, tb, :]}.get(br, ot[:, :])
                    take_bank(dve.tensor_tensor(dst.rearrange("p (h d) -> p h d", h=4),
                                                b[:, 0:GW].rearrange("p (h d) -> p h d", h=4), c, ALU.mult))
                    if br in ("sel", "win"):
                        ins = dve.tensor_tensor(ob[:, tb, :], ob[:, tb, :], ot[:, :], ALU.add)
                        if n == len(AJ) - 1:
                            signal(ins, "o", o_ready)
                        else:
                            link(ins)

                for n in range(len(AJ) + 2):
                    if n < len(AJ):
                        score_rows(n)
                    if 1 <= n <= len(AJ) and AJ[n - 1][0] == "cmp":
                        mask_cmp(n - 1)
                    if n >= 2:
                        outputs(n - 2)

                dve.wait_ge(ssd_act, 3 * l + 1)
                link(dve.scalar_tensor_tensor(out=dts[:, 4, :, :], in0=dts[:, 0, :, :], scalar=0.0,
                                              in1=dts[:, 3, :, :], op0=ALU.max, op1=ALU.add))
                signal(dve.scalar_tensor_tensor(out=dts[:, 5, :, :], in0=dts[:, 4, :, :], scalar=-1.0,
                                                in1=neg_a[:, l:l + 1, :].broadcast_to([P, TB, SSD_H]),
                                                op0=ALU.mult, op1=ALU.mult), "ssd_vec", ssd_vec)
                dve.wait_ge(act_took, mark["lgate", l])
                for i in range(2):
                    ins = dve.tensor_scalar(la[:, i, :], lth[:, i, :], 1.0, lru_c[:, l, i:i + 1], ALU.add, ALU.mult)
                    if i == 0:
                        link(ins)
                    else:
                        signal(ins, "lru_vec", lru_vec)
                g = lraw[:, 2:4, 3:3 + S]
                link(dve.tensor_tensor(lgate[:, :, :], g, g, ALU.mult))
                link(dve.tensor_scalar(lgate[:, :, :], lgate[:, :, :], 0.044715, 1.0, ALU.mult, ALU.add))
                signal(dve.tensor_tensor(lgate[:, :, :], lgate[:, :, :], g, ALU.mult), "lru_vec", lru_vec)
                dve.wait_ge(lru_act, 5 * l + 1)
                link(dve.tensor_scalar(ld[:, :, :], lt1[:, :, :], -1.0, 1.0, ALU.mult, ALU.add))
                link(dve.reciprocal(ld[:, :, :], ld[:, :, :]))
                link(dve.scalar_tensor_tensor(out=lb[:, :, :], in0=lt1[:, :, :], scalar=-2.0, in1=ld[:, :, :],
                                              op0=ALU.mult, op1=ALU.mult))
                signal(dve.tensor_scalar(lb[:, :, :], lb[:, :, :], 0.0, None, ALU.max), "lru_vec", lru_vec)
                link(dve.tensor_scalar(ld[:, :, :], lt2[:, :, :], -1.0, 1.0, ALU.mult, ALU.add))
                link(dve.reciprocal(ld[:, :, :], ld[:, :, :]))
                link(dve.scalar_tensor_tensor(out=lt2[:, :, :], in0=lt2[:, :, :], scalar=1.0, in1=ld[:, :, :],
                                              op0=ALU.add, op1=ALU.mult))
                link(dve.scalar_tensor_tensor(out=lt1[:, :, :], in0=lth[:, 2:4, :], scalar=1.0, in1=xb[:, :, :],
                                              op0=ALU.add, op1=ALU.mult))
                dve.wait_ge(lru_act, 5 * l + 2)
                link(dve.scalar_tensor_tensor(out=lgate[:, :, :], in0=lgate[:, :, :], scalar=1.0, in1=g,
                                              op0=ALU.add, op1=ALU.mult))
                dve.wait_ge(rstd_ready, 5 * l + 3)
                r0 = 4 * (5 * l + 2)
                for i, o in enumerate((oa, ob)):
                    for tb in range(TB):
                        ins = dve.tensor_scalar(yn[:, i, tb, :], o[:, tb, :],
                                                rstd[:, r0 + 2 * i + tb:r0 + 2 * i + tb + 1], None, ALU.mult)
                        if (i, tb) == (1, TB - 1):
                            signal(ins, "yn", yn_ready)
                        else:
                            link(ins)
                dve.wait_ge(lru_act, 5 * l + 3)
                link(dve.scalar_tensor_tensor(out=lb[:, :, :], in0=lb[:, :, :], scalar=0.5, in1=lt1[:, :, :],
                                              op0=ALU.mult, op1=ALU.mult))
                for i in range(2):
                    link(dve.tensor_tensor_scan(la[:, i, :], lt2[:, i, :], lb[:, i, :], 0.0, ALU.mult, ALU.add))
                signal(dve.scalar_tensor_tensor(out=xb[:, :, :], in0=lgate[:, :, :], scalar=0.5, in1=la[:, :, :],
                                                op0=ALU.mult, op1=ALU.mult), "lru_vec", lru_vec)

                b = filled()
                take_bank(dve.tensor_copy(xtok[:, :, :], b[:, :].rearrange("p (t c) -> p t c", t=TB)))
                for tb in range(TB):
                    link(dve.tensor_tensor(xdt[:, tb, :].rearrange("p (h d) -> p h d", h=SSD_H),
                                           xtok[:, tb, :].rearrange("p (h d) -> p h d", h=SSD_H),
                                           dts[:, 4, tb, :].unsqueeze(2).broadcast_to([P, SSD_H, HD]), ALU.mult))
                b = filled()
                take_bank(dve.tensor_scalar(nacs[:, :, :], b[:, 0:TB * SSD_H].rearrange("p (t h) -> p t h", t=TB),
                                            -1.0, None, ALU.mult))
                for hp in range(2):
                    b = filled()
                    for i in range(2):
                        h = 2 * hp + i
                        link(dve.tensor_scalar(dec0[:, h, :], b[:, i * S:(i + 1) * S], nacs[:, 0, h:h + 1], 0.0,
                                               ALU.add, ALU.min))
                        ins = dve.tensor_scalar(dec1[:, h, :], b[:, i * S + P:(i + 1) * S], nacs[:, 1, h:h + 1],
                                                0.0, ALU.add, ALU.min)
                        if i == 0:
                            link(ins)
                    take_bank(ins)
                signal(dve.tensor_copy(hT_flag[:, 0:1], ones[:, 0:1]), "ssd_vec", ssd_vec)
                dve.wait_ge(ssd_act, 3 * l + 3)
                tri = upper[:, :].unsqueeze(1).broadcast_to([P, SSD_H, P])
                link(dve.tensor_tensor(dec0[:, :, 0:P], dec0[:, :, 0:P], tri, ALU.mult))
                link(dve.tensor_tensor(dec1[:, :, :], dec1[:, :, :], tri, ALU.mult))
                for d, n in ((dec0, S), (dec1, P)):
                    b = filled()
                    for g_ in range(SSD_G):
                        v = d[:, 2 * g_:2 * g_ + 2, :]
                        sc = b[:, g_ * n:(g_ + 1) * n].unsqueeze(1).broadcast_to([P, 2, n])
                        ins = dve.tensor_tensor(v, v, sc, ALU.mult)
                        if g_ == 0:
                            link(ins)
                    take_bank(ins)
                signal(dve.tensor_copy(hT_flag[:, 0:1], ones[:, 0:1]), "dec", dec_ready)
                b = filled()
                take_bank(dve.tensor_scalar(lrstd[:, :], b[:, 0:S], EPS, None, ALU.add))
                signal(dve.tensor_copy(hT_flag[:, 0:1], ones[:, 0:1]), "lru_vec", lru_vec)
                for tb in range(TB):
                    link(dve.tensor_tensor(yd[:, tb, :].rearrange("p (h d) -> p h d", h=SSD_H),
                                           xtok[:, tb, :].rearrange("p (h d) -> p h d", h=SSD_H),
                                           ssd_par[:, l, 2, :].unsqueeze(2).broadcast_to([P, SSD_H, HD]), ALU.mult))
                for tb in range(TB):
                    b = filled()
                    take_bank(dve.tensor_tensor(yd[:, tb, :], yd[:, tb, :], b[:, 0:GW], ALU.add))
                signal(dve.tensor_tensor(yd[:, :, :], yd[:, :, :], zs[:, :, :], ALU.mult), "ssd_vec", ssd_vec)
                dve.wait_ge(lru_act, 5 * l + 5)
                link(dve.reciprocal(lrstd[:, :], lrstd[:, :]))
                for i in range(2):
                    link(dve.scalar_tensor_tensor(out=yT[:, 4 + i, :], in0=xb[:, i, :], scalar=pcol(l, "grp", 4 + i),
                                                  in1=lrstd[:, :], op0=ALU.mult, op1=ALU.mult))
                dve.wait_ge(rstd_ready, 5 * l + 4)
                r0 = 4 * (5 * l + 3)
                for tb in range(TB):
                    ins = dve.tensor_scalar(yn[:, 2, tb, :], yd[:, tb, :], rstd[:, r0 + tb:r0 + tb + 1], None,
                                            ALU.mult)
                    if tb == 0:
                        link(ins)
                    else:
                        signal(ins, "yn", yn_ready)
                for grp in (0, 1, 3):
                    b = filled()
                    gain = par[:, l, PR["grp"] + 2 * grp:PR["grp"] + 2 * grp + 2].unsqueeze(2)\
                        .broadcast_to([P, 2, S])
                    take_bank(dve.tensor_tensor(yT[:, 2 * grp:2 * grp + 2, :],
                                                b[:, :].rearrange("p (k t) -> p k t", k=2), gain, ALU.mult))
                signal(dve.tensor_copy(hT_flag[:, 0:1], ones[:, 0:1]), "yT", yT_ready)
                for tb in range(TB):
                    for half in range(2):
                        b = filled()
                        r = xres[:, tb, half * 512:(half + 1) * 512]
                        take_bank(dve.tensor_tensor(r, r, b[:, :], ALU.add))
                signal(dve.tensor_copy(hT_flag[:, 0:1], ones[:, 0:1]), "res", res_ready)
                normed(2 * l + 1, 5 * l + 4)

                if l == 0:
                    for s in range(DENSE):
                        dve.wait_ge(up_done, s + 1)
                        dve.wait_ge(silu_done, s + 1)
                        if s >= 2:
                            dve.wait_ge(hidT_done, s - 1)
                        dve.tensor_tensor(hid[:, s % 2, :], sgate[:, s % 2, :], banks[2 + s % 2][:, :], ALU.mult)\
                            .then_inc(hid_ready, 1)
                    for tb in range(TB):
                        dve.wait_ge(down_done, DENSE - 1 + tb)
                        for half in range(2):
                            r = xres[:, tb, half * 512:(half + 1) * 512]
                            ins = dve.tensor_tensor(r, r, banks[4 + 2 * tb + half][:, :], ALU.add)
                            if (tb, half) == (1, 1):
                                signal(ins, "res", res_ready)
                            else:
                                link(ins)

            dve.wait_ge(route_logits, 1)
            link(dve.tensor_copy(logit[:, :, :], banks[0][:, 0:TB * NE].rearrange("p (t e) -> p t e", t=TB)))
            for tb in range(TB):
                link(dve.max(out=top[:, tb, :], in_=logit[:, tb, :]))
                link(dve.max_index(out=topi[:, tb, :], in_max=top[:, tb, :], in_values=logit[:, tb, :]))
            link(dve.tensor_copy(topf[:, :, :], topi[:, :, :]))
            signal(dve.tensor_tensor(topw[:, 0, :], top[:, :, 1], top[:, :, 0], ALU.subtract), "diff", route_diff)
            for i in range(2):
                for tb in range(TB):
                    link(dve.tensor_scalar(hot[:, i, tb, :], iota[:, 0:NE], topf[:, tb, i:i + 1], None,
                                           ALU.is_equal))
            signal(dve.tensor_tensor(sel[:, :, :], hot[:, 0, :, :], hot[:, 1, :, :], ALU.add), "sel", sel_ready)
            dve.wait_ge(route_exp, 1)
            link(dve.tensor_scalar(topw[:, 2, :], topw[:, 1, :], 1.0, None, ALU.add))
            link(dve.reciprocal(topw[:, 2, :], topw[:, 2, :]))
            link(dve.tensor_tensor(topw[:, 3, :], topw[:, 1, :], topw[:, 2, :], ALU.mult))
            for tb in range(TB):
                link(dve.tensor_scalar(gatew[:, tb, :], hot[:, 0, tb, :], topw[:, 2, tb:tb + 1], None, ALU.mult))
                link(dve.scalar_tensor_tensor(out=gatew[:, tb, :], in0=hot[:, 1, tb, :],
                                              scalar=topw[:, 3, tb:tb + 1], in1=gatew[:, tb, :], op0=ALU.mult,
                                              op1=ALU.add))
            dve.wait_ge(ranks_done, 1)
            link(dve.scalar_tensor_tensor(out=rank1[:, :, :],
                                          in0=banks[1][:, 0:TB * NE].rearrange("p (t e) -> p t e", t=TB), scalar=1.0,
                                          in1=sel[:, :, :], op0=ALU.add, op1=ALU.mult))
            link(dve.memset(rank[:, :, NE:JT], -1.0))
            link(dve.memset(jgate[:, :, NE:JT], 0.0))
            link(dve.tensor_scalar(rank[:, :, 0:NE], rank1[:, :, :], -1.0, None, ALU.add))
            link(dve.tensor_copy(jgate[:, :, 0:NE], gatew[:, :, :]))
            link(dve.tensor_scalar(ovf[:, :], banks[1][:, 2 * NE:3 * NE], float(P), None, ALU.is_gt))
            link(dve.tensor_tensor_scan(ovpos[:, :], ones[:, 0:NE], ovf[:, :], 0.0, ALU.mult, ALU.add))
            for o in range(3):
                link(dve.scalar_tensor_tensor(out=in_job[:, :], in0=ovpos[:, :], scalar=float(o + 1), in1=ovf[:, :],
                                              op0=ALU.is_equal, op1=ALU.mult))
                pickj = in_job[:, :].unsqueeze(1).broadcast_to([P, TB, NE])
                for src, dst in ((rank1, rank), (gatew, jgate)):
                    link(dve.tensor_tensor(prod8[:, :, :], src[:, :, :], pickj, ALU.mult))
                    link(dve.tensor_reduce(dst[:, :, NE + o:NE + o + 1], prod8[:, :, :], AX.X, ALU.add))
                link(dve.tensor_scalar(rank[:, :, NE + o:NE + o + 1], rank[:, :, NE + o:NE + o + 1], -1.0 - P, None,
                                       ALU.add))
                link(dve.tensor_tensor(prod8[:, 0, :], in_job[:, :], iota[:, 0:NE], ALU.mult))
                link(dve.tensor_reduce(steer_f[:, o:o + 1], prod8[:, 0, :], AX.X, ALU.add))
            link(dve.tensor_reduce(steer_f[:, 3:4], ovf[:, :], AX.X, ALU.add))
            signal(dve.tensor_copy(steer[0:1, :], steer_f[0:1, :]), "steer", steer_ready)

            def picks(j):
                for tb in range(TB):
                    dve.tensor_scalar(pick[:, tb, :], iota[:, :], rank[:, tb, bass.ds(j, 1)], None, ALU.is_equal)
                    ins = dve.tensor_scalar(pickw[:, tb, :], iota[:, :], rank[:, tb, bass.ds(j, 1)],
                                            jgate[:, tb, bass.ds(j, 1)], ALU.is_equal, ALU.mult)
                ins.then_inc(pick_ready, 1)

            def gathered(jobs_before):
                dve.wait_ge(xg_done, jobs_before + 1)
                for i in range(2):
                    gain = par[:, 1, PR["ffn"] + 4 * i:PR["ffn"] + 4 * i + 4].unsqueeze(2).broadcast_to([P, 4, P])
                    ins = dve.tensor_tensor(xT[:, 4 * i:4 * i + 4, :],
                                            banks[6 + i][:, :].rearrange("p (d t) -> p d t", d=4), gain, ALU.mult)
                ins.then_inc(xT_ready, 1)

            picks(0)
            gathered(0)
            dve.tensor_copy(hT_flag[:, 0:1], ones[:, 0:1]).then_inc(comb_took, 2)
            dve.memset(closed[:, :], 0.0).then_inc(job_closed, 1)

            def job(j, s0):
                for c in range(NCH):
                    dve.wait_ge(up_done, s0 + (c + 1))
                    dve.wait_ge(silu_done, s0 + (c + 1))
                    dve.wait_ge(hidT_done, s0 + (c - 1))
                    dve.tensor_tensor(hid[:, c % 2, :], sgate[:, c % 2, :], banks[2 + c % 2][:, :], ALU.mult)\
                        .then_inc(hid_ready, 1)
                    if c == 2:
                        dve.wait_ge(pickT_done, j + 1)
                        dve.tensor_copy(pickT[:, :, :], banks[6][:, 0:TB * P].rearrange("p (t s) -> p t s", t=TB))\
                            .then_inc(pickT_ready, 1)
                    if c == 4:
                        picks(j + 1)
                dve.wait_ge(down_done, s0 + NCH)
                dve.tensor_copy(ysb[:, 512:D], banks[5][:, :]).then_inc(y_dve, 1)
                gathered(j + 1)
                for tb in range(TB):
                    dve.wait_ge(comb_done, 2 * j + (tb + 1))
                    for half in range(2):
                        r = xres[:, tb, half * 512:(half + 1) * 512]
                        ins = dve.tensor_tensor(r, r, banks[4 + 2 * tb + half][:, :], ALU.add)
                    ins.then_inc(comb_took, 1)
                dve.wait_ge(comb_took, 2 * j + 4)
                dve.wait_ge(job_closed, j + 1)
                dve.memset(closed[:, :], 0.0).then_inc(job_closed, 1)

            with dve.Fori(0, NE) as e:
                job(e, e * NCH + DENSE)
            novf_r = dve.value_load(steer[0:1, 3:4], min_val=0, max_val=3)
            with dve.Fori(0, 3) as o:
                with dve.If(novf_r > o):
                    job(o + NE, o * NCH + (DENSE + NE * NCH))

            dve.wait_ge(comb_took, 2 * NE + 2)
            for tb in range(TB):
                dve.tensor_tensor_reduce(hn[:, tb, :], xres[:, tb, :], xres[:, tb, :], 1.0 / D, 0.0, ALU.mult,
                                         ALU.add, stat[:, 40 + tb:41 + tb]).then_inc(ms_ready, 1)
            dve.wait_ge(rstd_ready, 5 * L + 1)
            for tb in range(TB):
                dve.scalar_tensor_tensor(out=hn[:, tb, :], in0=xres[:, tb, :], scalar=rstd[:, 40 + tb:41 + tb],
                                         in1=gfin[:, :], op0=ALU.mult, op1=ALU.mult).then_inc(out_ready, 1)


_INS = ['x', 'positions', 'norm_mix', 'w_in', 'mla_q_norm', 'mla_w_uq', 'mla_kv_norm', 'mla_w_ukv', 'nsa_cmp_pe',
        'nsa_w_cmp', 'lru_conv_w', 'lru_conv_b', 'lru_w_gate', 'lru_b_gate', 'lru_lambda', 'ssd_conv_w',
        'ssd_conv_b', 'ssd_dt_bias', 'ssd_a_log', 'ssd_d', 'group_norm', 'w_out', 'norm_ffn', 'ffn_w_gate',
        'ffn_w_up', 'ffn_w_down', 'moe_router', 'moe_w_gate', 'moe_w_up', 'moe_w_down', 'norm_final']


def kernel(**inputs):
    import concourse.bacc as bacc
    from concourse.bass_utils import run_bass_kernel_spmd

    nc = bacc.Bacc("TRN2", target_bir_lowering=False, num_devices=1)
    arrays, args = {}, []
    for name in _INS:
        a = np.ascontiguousarray(inputs[name])
        arrays[f"in_{name}_dram"] = a
        args.append(nc.dram_tensor(f"in_{name}_dram", a.shape, mybir.dt.from_np(a.dtype), kind="ExternalInput").ap())
    out = nc.dram_tensor("out_dram", inputs["x"].shape, F32, kind="ExternalOutput").ap()
    trunk(nc, *args, out)
    r = run_bass_kernel_spmd(nc, [arrays], core_ids=[0])
    return r.results[0]["out_dram"]
```

```python
from contextlib import ExitStack

import numpy as np

import concourse.bass as bass
from concourse import mybir

F32 = mybir.dt.float32
F32R = mybir.dt.float32r
I32 = mybir.dt.int32
U32 = mybir.dt.uint32
ALU = mybir.AluOpType
ACT = mybir.ActivationFunctionType
AX = mybir.AxisListType

P = 128
ROPE_THETA = 500000.0
EPS = 1e-6
NEG = -1e30
MLA_H, NOPE, ROPE, QR, KVR = 4, 64, 32, 192, 128
QK = NOPE + ROPE
HD, NROT, NH = 64, 16, 4
CSTRIDE, CLEN = 16, 32
SSD_H, SSD_G = 4, 2
GW = 256
RING = 7
SLOT = 2048
FC = 512
SPLIT = 3


def trunk(nc, x, positions, norm_mix, w_in, mla_q_norm, mla_w_uq, mla_kv_norm, mla_w_ukv, nsa_cmp_pe,
          nsa_w_cmp, lru_conv_w, lru_conv_b, lru_w_gate, lru_b_gate, lru_lambda, ssd_conv_w, ssd_conv_b,
          ssd_dt_bias, ssd_a_log, ssd_d, group_norm, w_out, norm_ffn, ffn_w_gate, ffn_w_up, ffn_w_down,
          moe_router, moe_w_gate, moe_w_up, moe_w_down, norm_final, out):
    D = x.shape[2]
    S = x.shape[1]
    L = norm_mix.shape[0]
    TB = S // P
    KT = D // P
    FF = ffn_w_gate.shape[2]
    NCH = FF // FC
    FT = FC // P
    NE = moe_w_gate.shape[1]
    NC = S // CSTRIDE - 1
    O_NSA = QR + KVR + ROPE
    O_LRU = O_NSA + NH * HD + 6 * HD + 3 * NH
    O_SSD = O_LRU + 2 * GW
    O_XBC = O_SSD + GW
    O_DT = O_XBC + 3 * GW
    IN = O_DT + SSD_H
    assert L == 2 and TB == 2 and KT == 8 and FF % FC == 0 and w_in.shape[2] == IN
    assert S // 64 <= 16 and S <= 512
    UA = 512
    UB = O_LRU - UA
    UT = O_LRU + SSD_H
    MIX_SLOTS, FFN_SLOTS = 14, 6 * NCH
    assert MIX_SLOTS % RING == 0 and FFN_SLOTS % RING == 0
    BASE_MIX = [0, MIX_SLOTS + FFN_SLOTS]
    BASE_FFN = [MIX_SLOTS, 2 * MIX_SLOTS + FFN_SLOTS]
    JOBS = NE + 3
    JT = JOBS + 1

    ctx = ExitStack()
    with ctx:
        def sb(name, shape, dt=F32):
            return ctx.enter_context(nc.sbuf_tensor(name, shape, dt))

        def sem(name):
            return ctx.enter_context(nc.semaphore(name))

        ring = sb("ring", [P, RING, SLOT])
        ident = sb("ident", [P, P])
        upper = sb("upper", [P, P])
        strict = sb("strict", [P, P])
        ones = sb("ones", [P, P])
        cbias = sb("cbias", [P, 2 * P])
        cmask = sb("cmask", [P, TB, NC])
        cmbias = sb("cmbias", [P, TB, NC])
        iota = sb("iota", [P, P])
        minus_half = sb("minus_half", [P, 4])
        prow = sb("prow", [P, L, P])
        par = sb("par", [P, L, P])
        w_uq = sb("w_uq", [96, 2, 384])
        w_ukv = sb("w_ukv", [P, 512])
        w_cmp = sb("w_cmp", [P, CLEN, HD])
        pe_row = sb("pe_row", [CLEN, L, P])
        pe_t = sb("pe_t", [P, L, CLEN])
        lru_w = sb("lru_w", [P, L, 2, 2, P])
        ssd_par = sb("ssd_par", [P, L, 3, SSD_H])
        neg_a = sb("neg_a", [P, L, SSD_H])
        lru_c = sb("lru_c", [P, L, 4])
        lru_t = sb("lru_t", [P, L, 6, 2])
        half_b = sb("half_b", [P, L, 4])
        router = sb("router", [P, KT, NE])
        gfin = sb("gfin", [P, D])
        pos_i = sb("pos_i", [P, TB], I32)
        pos_f = sb("pos_f", [P, TB])
        inv = sb("inv", [P, 16])
        ang = sb("ang", [P, TB, 16])
        rk = sb("rk", [P, 2, TB, 16])
        rr = sb("rr", [P, 2, TB, 16])
        trig = sb("trig", [P, 2, TB, 16])
        xres = sb("xres", [P, TB, D])
        hn = sb("hn", [P, TB, D])
        hT = sb("hT", [P, KT, S])
        stat = sb("stat", [P, 44])
        rstd = sb("rstd", [P, 44])
        closed = sb("closed", [P, 1])
        hT_flag = sb("hT_flag", [P, 1])
        WORK = 24832
        work_at = -(-nc.sbuf_base // 32) * 32
        work = sb("work", [P, WORK])
        used = [0]

        def take(*shape):
            n = int(np.prod(shape))
            at = used[0]
            used[0] += n
            assert used[0] <= WORK, used
            v = work[:, at:at + n]
            if len(shape) > 1:
                names = " ".join("abcd"[:len(shape)])
                v = v.rearrange(f"p ({names}) -> p {names}", **dict(zip("bcd", shape[1:])))
            return v

        lraw = take(4, 3 + S)
        xraw = take(6, 3 + S)
        ffn_scratch = used[0]
        utok = take(TB, UT)
        yT = take(KT, S)
        junk = take(2, 256)
        qk_scratch = used[0]
        cqn = take(TB, QR)
        ckvn = take(TB, KVR)
        cqT = take(2, S)
        ckvT = take(S)
        qtok = take(TB, MLA_H, QK)
        kcat = take(TB, MLA_H, QK)
        rt = take(4, TB * 4 * 16)
        qk_end = used[0]
        vtok = take(TB, MLA_H, HD)
        qT = take(MLA_H, S)
        kT = take(MLA_H, S)
        nqT = take(NH, S)
        kvcT = take(S)
        ksT = take(S)
        kwT = take(S)
        cin = take(CLEN, NC)
        kcT = take(NC)
        vc = take(HD)
        gates = take(TB, 3 * NH)
        yn = work[:, used[0]:used[0] + 3 * TB * GW].rearrange("p (i t c) -> p i t c", i=3, t=TB)
        prob = take(2, 4, S)
        probT = take(2, 8 * P)
        rmax = take(8, 4)
        rsum = take(8, 4)
        coef = take(8, 4)
        oa = take(TB, GW)
        ob = take(TB, GW)
        ot = take(GW)
        xb = take(2, S)
        xbc = take(6, S)
        zs = take(TB, GW)
        dts = take(6, TB, SSD_H)
        lth = hn[:, 0, :].rearrange("p (i t) -> p i t", i=4)
        lt1, lt2 = (hn[:, 1, i * 2 * S:(i + 1) * 2 * S].rearrange("p (i t) -> p i t", i=2) for i in range(2))
        la, ld, lb, lgate = (hT[:, 2 * i:2 * i + 2, :] for i in range(4))
        used[0] = qk_scratch
        lrstd = take(S)
        xtok = take(TB, GW)
        xdt = take(TB, GW)
        nacs = take(TB, SSD_H)
        dec0 = take(SSD_H, S)
        dec1 = take(SSD_H, P)
        yd = take(TB, GW)
        assert used[0] <= qk_end
        used[0] = ffn_scratch
        sgate = take(2, FC)
        hid = take(2, FC)

        def parts(name, *shape):
            used[0] += -used[0] % 8
            t = nc.alloc_sbuf_tensor_at(name, [P] + list(shape), F32R, offset=work_at + 4 * used[0])
            used[0] += int(np.prod(shape))
            assert used[0] <= WORK, used
            return t

        w_hi = parts("w_hi", SPLIT, SLOT)
        w_lo = parts("w_lo", SPLIT, SLOT)
        hidT_hi = parts("hidT_hi", 2, FT * P)
        hidT_lo = parts("hidT_lo", 2, FT * P)
        in_scratch = used[0]
        hT_hi = parts("hT_hi", KT, S)
        hT_lo = parts("hT_lo", KT, S)
        dense_end = used[0]
        used[0] = in_scratch
        xT_hi = parts("xT_hi", KT, P)
        xT_lo = parts("xT_lo", KT, P)
        xg = take(KT, P)
        ysb = take(D)
        used[0] = max(used[0], dense_end)
        pick = take(TB, P)
        pickw = take(TB, P)
        pickT = take(TB, P)
        logit = take(TB, NE)
        top = take(TB, 8)
        topf = take(TB, 8)
        topw = take(4, TB)
        hot = take(2, TB, NE)
        sel = take(TB, NE)
        gatew = take(TB, NE)
        rank1 = take(TB, NE)
        rank = take(TB, JT)
        jgate = take(TB, JT)
        cnt = take(NE)
        ovf = take(NE)
        ovpos = take(NE)
        in_job = take(NE)
        prod8 = take(TB, NE)
        steer_f = take(4)
        topi = sb("topi", [P, TB, 8], U32)
        steer = sb("steer", [1, 4], I32)

        banks = [ctx.enter_context(nc.psum_tensor(f"bank{i}", [P, 512], F32)) for i in range(8)]

        slot_full = [sem(f"slot_full{i}") for i in range(RING)]
        x_in, prow_in, mixw_in, misc_in = sem("x_in"), sem("prow_in"), sem("mixw_in"), sem("misc_in")
        pos_in, prow_zero, lru_w_zero = sem("pos_in"), sem("prow_zero"), sem("lru_w_zero")
        consts_ready = sem("consts_ready")
        pool_chain, dve_chain, act_chain = sem("pool_chain"), sem("dve_chain"), sem("act_chain")
        for_dve, dve_took = sem("for_dve"), sem("dve_took")
        for_act, act_took = sem("for_act"), sem("act_took")
        lam_args, lam_logs, half_b_ready = sem("lam_args"), sem("lam_logs"), sem("half_b_ready")
        rope_args, trig_ready = sem("rope_args"), sem("trig_ready")
        ms_ready, rstd_ready = sem("ms_ready"), sem("rstd_ready")
        hn_ready, hT_ready, res_ready = sem("hn_ready"), sem("hT_ready"), sem("res_ready")
        cn_ready, cT_ready = sem("cn_ready"), sem("cT_ready")
        qk_roped, nsa_roped, cin_ready, gate_th = sem("qk_roped"), sem("nsa_roped"), sem("cin_ready"), sem("gate_th")
        cmp_ready, rmax_ready, exp_ready, masked = sem("cmp_ready"), sem("rmax_ready"), sem("exp_ready"), sem("masked")
        o_ready, yn_ready, yT_ready = sem("o_ready"), sem("yn_ready"), sem("yT_ready")
        lru_conv, ssd_conv = sem("lru_conv"), sem("ssd_conv")
        lru_vec, lru_act, ssd_vec, ssd_act = sem("lru_vec"), sem("lru_act"), sem("ssd_vec"), sem("ssd_act")
        dec_ready = sem("dec_ready")
        hi_ready, lo_ready, units_used = sem("hi_ready"), sem("lo_ready"), sem("units_used")
        hT_hi_ready, hT_lo_ready = sem("hT_hi_ready"), sem("hT_lo_ready")
        silu_done, hid_ready, hidT_done = sem("silu_done"), sem("hid_ready"), sem("hidT_done")
        hidT_hi_ready, hidT_lo_ready = sem("hidT_hi_ready"), sem("hidT_lo_ready")
        route_logits, route_diff, route_exp = sem("route_logits"), sem("route_diff"), sem("route_exp")
        sel_ready, ranks_done, steer_ready = sem("sel_ready"), sem("ranks_done"), sem("steer_ready")
        pick_ready, pickT_done, pickT_ready = sem("pick_ready"), sem("pickT_done"), sem("pickT_ready")
        xg_done, xg_ready = sem("xg_done"), sem("xg_ready")
        xT_hi_ready, xT_lo_ready = sem("xT_hi_ready"), sem("xT_lo_ready")
        zero_sums, y_ready = sem("zero_sums"), sem("y_ready")
        comb_done, comb_took = sem("comb_done"), sem("comb_took")
        out_ready, out_stored = sem("out_ready"), sem("out_stored")

        PR, n = {}, 0
        for name, rows in (("mix", 8), ("ffn", 8), ("grp", 8), ("lcw", 8), ("lcb", 2), ("lbg", 4), ("lam", 2),
                           ("scw", 24), ("scb", 6), ("kvn", 1), ("qn", 2)):
            PR[name] = n
            n += rows
        assert n <= P
        N_PROW = 12
        N_MISC = 3 + 2 + 2

        def pcol(l, name, i=0, rows=P):
            return par[0:rows, l, PR[name] + i:PR[name] + i + 1]

        def slot(p):
            return ring[:, p % RING, :]

        def slot_k(p):
            return slot(p).rearrange("p (k n) -> p k n", k=4)

        def slot_r(p):
            return slot(p).rearrange("p (k n) -> p k n", k=2)

        AJ = [(br, tb) for br in ("mla", "cmp", "sel", "win") for tb in range(TB)]
        KV0 = O_NSA + NH * HD
        FFN_ORDER = []
        for c in range(NCH + 1):
            if c < NCH:
                FFN_ORDER += [("gate", c), ("up", c)]
            if c >= 1:
                FFN_ORDER += [("down", c - 1)]
        AT = {key: 2 * i for i, key in enumerate(FFN_ORDER)}
        assert 2 * len(FFN_ORDER) == FFN_SLOTS
        DENSE = NCH * TB
        assert FFN_SLOTS % SPLIT == 0
        def at_gate(c, h):
            return AT["gate", c] + h

        def at_up(c, h):
            return AT["up", c] + h

        def at_down(c, h):
            return AT["down", c] + h

        fills = []
        freed = {}
        mark = {}

        block = ctx.enter_context(nc.Block())

        @block.tensor
        def _(pe):
            gave = [0, 0]

            def bank(who):
                k = gave[who]
                gave[who] += 1
                if k >= 4:
                    pe.wait_ge((dve_took, act_took)[who], k - 3)
                return banks[4 * who + k % 4]

            def give(mm, who):
                mm.then_inc((for_dve, for_act)[who], 1)

            seen = [0] * RING

            def full(p, dmas=1):
                seen[p % RING] += 16 * dmas
                pe.wait_ge(slot_full[p % RING], seen[p % RING])

            def turn_normed():
                for g in range(4):
                    b = bank(0)
                    for k in range(2):
                        for tb in range(TB):
                            mm = pe.transpose(b[:, (2 * k + tb) * P:(2 * k + tb + 1) * P],
                                              hn[:, tb, (2 * g + k) * P:(2 * g + k + 1) * P], ident[:, :])
                    give(mm, 0)

            pe.wait_ge(consts_ready, 1)
            pe.wait_ge(prow_in, 16 * N_PROW)
            b = bank(0)
            for l in range(L):
                pe.transpose(b[:, l * P:(l + 1) * P], prow[:, l, :], ident[:, :])
            for l in range(L):
                mm = pe.transpose(b[:, 2 * P + l * CLEN:2 * P + (l + 1) * CLEN], pe_row[:, l, :],
                                  ident[0:CLEN, 0:CLEN])
            give(mm, 0)

            def products3(o, x_hi, x_lo, w, start, stop, low):
                if low:
                    return pe.matmul(o, x_hi, w, start=False, stop=stop)
                pe.matmul(o, x_hi, w, start=start, stop=False)
                return pe.matmul(o, x_lo, w, start=False, stop=False)

            def ffn(n, x_hi, x_lo, u0, s0, more=None):
                def parts_of(at, low):
                    if low:
                        pe.wait_ge(lo_ready, u0 + (at + 1))
                    else:
                        pe.wait_ge(hi_ready, u0 + (at + 1))
                    return (w_lo if low else w_hi)[:, at % SPLIT, :]

                def project(bank0, c, h, at):
                    for low in (False, True):
                        w = parts_of(at, low).rearrange("p (k n) -> p k n", k=4)
                        for i in range(n):
                            for k in range(4):
                                t = slice(i * P, (i + 1) * P)
                                mm = products3(banks[bank0 + (c * n + i) % 2][:, :], x_hi[:, 4 * h + k, t],
                                               x_lo[:, 4 * h + k, t], w[:, k, :], h == 0 and k == 0,
                                               h == 1 and k == 3, low)
                    mm.then_inc(units_used, 1)

                def down(c, h):
                    if h == 0:
                        pe.wait_ge(hidT_lo_ready, s0 + n * (c + 1))
                    for low in (False, True):
                        w = parts_of(at_down(c, h), low).rearrange("p (f n) -> p f n", f=2)
                        for i in range(n):
                            v = (c * n + i) % 2
                            for half in range(2):
                                for f in range(2):
                                    t = slice((2 * h + f) * P, (2 * h + f + 1) * P)
                                    mm = products3(banks[4 + 2 * i + half][:, :], hidT_hi[:, v, t],
                                                   hidT_lo[:, v, t], w[:, f, half * 512:(half + 1) * 512],
                                                   c == 0 and h == 0 and f == 0,
                                                   c == NCH - 1 and h == 1 and f == 1, low)
                    mm.then_inc(units_used, 1)

                def turn_hid(c):
                    for i in range(n):
                        v = (c * n + i) % 2
                        pe.wait_ge(hid_ready, s0 + (c * n + i + 1))
                        for f in range(FT):
                            mm = pe.transpose(banks[2 + v][:, f * P:(f + 1) * P], hid[:, v, f * P:(f + 1) * P],
                                              ident[:, :])
                        mm.then_inc(hidT_done, 1)

                for c in range(NCH):
                    if n == TB and c >= 1:
                        pe.wait_ge(silu_done, s0 + n * c)
                    project(0, c, 0, at_gate(c, 0))
                    if c >= 1:
                        turn_hid(c - 1)
                    project(0, c, 1, at_gate(c, 1))
                    if n == TB and c >= 1:
                        pe.wait_ge(hidT_lo_ready, s0 + n * c)
                    elif n == 1:
                        pe.wait_ge(hidT_lo_ready, s0 + max(c - 1, 0))
                    project(2, c, 0, at_up(c, 0))
                    project(2, c, 1, at_up(c, 1))
                    if more is not None:
                        more(c)
                    if c >= 1:
                        down(c - 1, 0)
                        if c == NCH - 1 and n == 1:
                            turn_hid(c)
                        down(c - 1, 1)
                if n > 1:
                    turn_hid(NCH - 1)
                down(NCH - 1, 0)
                down(NCH - 1, 1)

            for l in range(L):
                pe.wait_ge(hn_ready, 2 * l + 1)
                turn_normed()
                pe.wait_ge(hT_ready, 2 * l + 1)
                p = BASE_MIX[l]

                for unit, n in ((0, UA), (1, UB + SSD_H)):
                    for h in range(2):
                        full(p + h, 1 + unit)
                    for tb in range(TB):
                        b = bank(1)
                        for k in range(KT):
                            mm = pe.matmul(b[:, 0:n], hT[:, k, tb * P:(tb + 1) * P],
                                           slot_k(p + k // 4)[:, k % 4, 0:n], start=(k == 0), stop=(k == KT - 1))
                        give(mm, 1)
                    for h in range(2):
                        freed[p + h] = (for_act, gave[1])
                    p += 2
                mark["u", l] = gave[1]
                for unit in range(3):
                    for h in range(2):
                        full(p + h, 2 if unit == 2 else 1)
                    for half in range(2):
                        b = bank(0)
                        for i in range(2):
                            if unit == 2 and half == 1:
                                for k in range(KT):
                                    mm = pe.matmul(b[:, i * GW:(i + 1) * GW], hT[:, k, i * P:(i + 1) * P],
                                                   slot_k(p + k // 4)[:, k % 4, GW:2 * GW], start=(k == 0),
                                                   stop=(k == KT - 1))
                            else:
                                c0 = (2 * half + i) * P
                                for k in range(KT):
                                    mm = pe.matmul(b[:, i * S:(i + 1) * S], slot_k(p + k // 4)[:, k % 4, c0:c0 + P],
                                                   hT[:, k, :], start=(k == 0), stop=(k == KT - 1))
                        give(mm, 0)
                    for h in range(2):
                        freed[p + h] = (for_dve, gave[0])
                    p += 2

                pe.wait_ge(cn_ready, l + 1)
                b = bank(0)
                for i in range(2):
                    for tb in range(TB):
                        mm = pe.transpose(b[0:96, (2 * i + tb) * P:(2 * i + tb + 1) * P],
                                          cqn[:, tb, i * 96:(i + 1) * 96], ident[:, :])
                give(mm, 0)
                b = bank(0)
                for tb in range(TB):
                    mm = pe.transpose(b[:, tb * P:(tb + 1) * P], ckvn[:, tb, :], ident[:, :])
                give(mm, 0)
                pe.wait_ge(cT_ready, l + 1)
                pe.wait_ge(mixw_in, 64 * (l + 1))
                for tb in range(TB):
                    b = bank(1)
                    for i in range(2):
                        mm = pe.matmul(b[:, 0:384], cqT[0:96, i, tb * P:(tb + 1) * P], w_uq[:, i, :],
                                       start=(i == 0), stop=(i == 1))
                    give(mm, 1)
                    b = bank(1)
                    give(pe.matmul(b[:, :], ckvT[:, tb * P:(tb + 1) * P], w_ukv[:, :], start=True, stop=True), 1)
                mark["qkv", l] = gave[1]

                pe.wait_ge(nsa_roped, l + 1)
                for hp in range(2):
                    b = bank(1)
                    for i in range(2):
                        c0 = O_NSA + (2 * hp + i) * HD
                        for tb in range(TB):
                            mm = pe.transpose(b[0:HD, (2 * i + tb) * P:(2 * i + tb + 1) * P],
                                              utok[:, tb, c0:c0 + HD], ident[:, :])
                    give(mm, 1)
                b = bank(1)
                for tb in range(TB):
                    pe.transpose(b[:, tb * P:(tb + 1) * P], utok[:, tb, KV0:KV0 + 2 * HD], ident[:, :])
                for tb in range(TB):
                    mm = pe.transpose(b[0:HD, S + tb * P:S + (tb + 1) * P],
                                      utok[:, tb, KV0 + 2 * HD:KV0 + 3 * HD], ident[:, :])
                give(mm, 1)
                b = bank(1)
                for tb in range(TB):
                    mm = pe.transpose(b[0:HD, tb * P:(tb + 1) * P],
                                      utok[:, tb, KV0 + 4 * HD:KV0 + 5 * HD], ident[:, :])
                give(mm, 1)
                mark["nsa", l] = gave[1]
                pe.wait_ge(qk_roped, l + 1)
                for src in (qtok, kcat):
                    for hp in range(2):
                        b = bank(1)
                        for i in range(2):
                            for tb in range(TB):
                                mm = pe.transpose(b[0:QK, (2 * i + tb) * P:(2 * i + tb + 1) * P],
                                                  src[:, tb, 2 * hp + i, :], ident[:, :])
                        give(mm, 1)
                pe.wait_ge(cin_ready, l + 1)
                b = bank(0)
                for j in range(CLEN):
                    pe.matmul(b[0:HD, 0:NC], w_cmp[0:HD, j, :], cin[0:HD, j, :], start=(j == 0),
                              stop=(j == CLEN - 1))
                for j in range(CLEN):
                    mm = pe.matmul(b[0:NC, 64:64 + HD], cin[HD:P, j, :], w_cmp[HD:P, j, :], start=(j == 0),
                                   stop=(j == CLEN - 1))
                give(mm, 0)
                mark["cmp", l] = gave[0]
                pe.wait_ge(act_took, gave[1])

                def scores(n):
                    br, tb = AJ[n]
                    t0, t1 = tb * P, (tb + 1) * P
                    nk = NC if br == "cmp" else t1
                    if br == "cmp":
                        pe.wait_ge(cmp_ready, l + 1)
                    per = 4 if br == "cmp" else 512 // nk
                    for g in range(4 // per):
                        b = bank(0)
                        for i in range(per):
                            h = g * per + i
                            q, k = {"mla": (qT[0:QK, h, t0:t1], kT[0:QK, h, 0:nk]),
                                    "cmp": (nqT[0:HD, h, t0:t1], kcT[0:HD, :]),
                                    "sel": (nqT[0:HD, h, t0:t1], ksT[0:HD, 0:nk]),
                                    "win": (nqT[0:HD, h, t0:t1], kwT[0:HD, 0:nk])}[br]
                            mm = pe.matmul(b[:, i * nk:(i + 1) * nk], q, k, start=True, stop=True)
                        give(mm, 0)

                def turn_probs(n):
                    br, tb = AJ[n]
                    pe.wait_ge(exp_ready, 8 * l + n + 1)
                    nb = 1 if br == "cmp" else tb + 1
                    if br == "cmp":
                        pe.wait_ge(masked, 2 * l + tb + 1)
                    rows = NC if br == "cmp" else P
                    for g in range(nb):
                        b = bank(1)
                        for i in range(4):
                            h, kb = divmod(4 * g + i, nb)
                            mm = pe.transpose(b[0:rows, i * P:(i + 1) * P],
                                              prob[:, n % 2, h, kb * P:kb * P + rows], ident[:, :])
                        give(mm, 1)
                    mark["probT", l, n] = gave[1]

                def products(n):
                    br, tb = AJ[n]
                    pe.wait_ge(act_took, mark["probT", l, n])
                    b = bank(0)
                    nb = 1 if br == "cmp" else tb + 1
                    for h in range(4):
                        for kb in range(nb):
                            i = h * nb + kb
                            rows = NC if br == "cmp" else P
                            v = {"mla": vtok[:, kb, h, :], "cmp": vc[0:NC, :],
                                 "sel": utok[:, kb, KV0 + 3 * HD:KV0 + 4 * HD],
                                 "win": utok[:, kb, KV0 + 5 * HD:KV0 + 6 * HD]}[br]
                            mm = pe.matmul(b[:, h * HD:(h + 1) * HD], probT[0:rows, n % 2, i * P:(i + 1) * P], v,
                                           start=(kb == 0), stop=(kb == nb - 1))
                    give(mm, 0)
                    mark["pv", l, n] = gave[0]

                def lru_gates():
                    pe.wait_ge(lru_conv, l + 1)
                    pe.wait_ge(misc_in, 16 * N_MISC)
                    for g in range(2):
                        b = bank(1)
                        for i in range(2):
                            mm = pe.matmul(b[:, i * S:(i + 1) * S], lru_w[:, l, g, i, :], xb[:, i, :], start=True,
                                           stop=True)
                        give(mm, 1)
                    mark["lgate", l] = gave[1]

                def ssd_sums():
                    pe.wait_ge(ssd_act, 3 * l + 2)
                    b = bank(0)
                    for tb in range(TB):
                        for i in range(2):
                            mm = pe.transpose(b[:, tb * GW + i * P:tb * GW + (i + 1) * P],
                                              xbc[:, i, tb * P:(tb + 1) * P], ident[:, :])
                    give(mm, 0)
                    pe.wait_ge(ssd_vec, 4 * l + 2)
                    b = bank(0)
                    pe.matmul(b[:, 0:SSD_H], upper[:, :], dts[:, 5, 0, :], start=True, stop=True)
                    pe.matmul(b[:, SSD_H:2 * SSD_H], ones[:, :], dts[:, 5, 0, :], start=True, stop=False)
                    give(pe.matmul(b[:, SSD_H:2 * SSD_H], upper[:, :], dts[:, 5, 1, :], start=False, stop=True), 0)
                    for hp in range(2):
                        b = bank(0)
                        for i in range(2):
                            h = 2 * hp + i
                            da = [dts[:, 5, tb, h:h + 1].broadcast_to([P, P]) for tb in range(TB)]
                            pe.matmul(b[:, i * S:i * S + P], da[0], upper[:, :], start=True, stop=True)
                            pe.matmul(b[:, i * S + P:(i + 1) * S], da[0], ones[:, :], start=True, stop=False)
                            mm = pe.matmul(b[:, i * S + P:(i + 1) * S], da[1], upper[:, :], start=False, stop=True)
                        give(mm, 0)

                def ssd_cb():
                    for sb_ in range(TB):
                        b = bank(0)
                        n = S - sb_ * P
                        for g in range(SSD_G):
                            mm = pe.matmul(b[:, g * n:(g + 1) * n], xbc[:, 2 + g, sb_ * P:(sb_ + 1) * P],
                                           xbc[:, 4 + g, sb_ * P:S], start=True, stop=True)
                        give(mm, 0)

                def ssd_products():
                    pe.wait_ge(dec_ready, l + 1)
                    for tb in range(TB):
                        b = bank(0)
                        for h in range(SSD_H):
                            o = b[:, h * HD:(h + 1) * HD]
                            mm = pe.matmul(o, dec0[:, h, tb * P:(tb + 1) * P], xdt[:, 0, h * HD:(h + 1) * HD],
                                           start=True, stop=(tb == 0))
                            if tb == 1:
                                mm = pe.matmul(o, dec1[:, h, :], xdt[:, 1, h * HD:(h + 1) * HD], start=False, stop=True)
                        give(mm, 0)

                def lru_square():
                    pe.wait_ge(lru_act, 5 * l + 4)
                    b = bank(0)
                    for i in range(2):
                        mm = pe.matmul(b[:, 0:S], ones[:, :], lt1[:, i, :], start=(i == 0), stop=(i == 1))
                    give(mm, 0)

                for n in range(len(AJ) + 2):
                    if n < len(AJ):
                        scores(n)
                    if n >= 2:
                        products(n - 2)
                    if 1 <= n <= len(AJ):
                        turn_probs(n - 1)
                    if n == 0:
                        lru_gates()
                    if n == 2:
                        ssd_sums()
                    if n == 4:
                        ssd_cb()
                    if n == 5:
                        ssd_products()
                    if n == 7:
                        lru_square()

                for i in (2, 0, 1):
                    pe.wait_ge(yn_ready, 2 * l + (1 if i == 2 else 2))
                    b = bank(0)
                    for j in range(2):
                        for tb in range(TB):
                            mm = pe.transpose(b[:, (2 * j + tb) * P:(2 * j + tb + 1) * P],
                                              yn[:, i, tb, j * P:(j + 1) * P], ident[:, :])
                    give(mm, 0)

                pe.wait_ge(yT_ready, l + 1)
                for q in range(4):
                    full(p + q)
                for tb in range(TB):
                    for half in range(2):
                        b = bank(0)
                        for k in range(KT):
                            mm = pe.matmul(b[:, :], yT[:, k, tb * P:(tb + 1) * P],
                                           slot_r(p + k // 2)[:, k % 2, half * 512:(half + 1) * 512],
                                           start=(k == 0), stop=(k == KT - 1))
                        give(mm, 0)
                for q in range(4):
                    freed[p + q] = (for_dve, gave[0])

                pe.wait_ge(hn_ready, 2 * l + 2)
                turn_normed()
                pe.wait_ge(hT_ready, 2 * l + 2)
                pe.wait_ge(act_took, gave[1])
                pe.wait_ge(dve_took, gave[0])

                fills.append(list(seen))
                if l == 0:
                    pe.wait_ge(hT_lo_ready, 1)
                    ffn(TB, hT_hi, hT_lo, 0, 0)
                    for i in range(RING):
                        seen[i] += 16 * FFN_SLOTS // RING
                    pe.wait_ge(res_ready, 2)

            pe.wait_ge(misc_in, 16 * N_MISC)
            for tb in range(TB):
                for k in range(KT):
                    mm = pe.matmul(banks[0][:, tb * NE:(tb + 1) * NE], hT[:, k, tb * P:(tb + 1) * P],
                                   router[:, k, :], start=(k == 0), stop=(k == KT - 1))
            mm.then_inc(route_logits, 1)
            pe.wait_ge(sel_ready, 1)
            pe.matmul(banks[1][:, 0:NE], strict[:, :], sel[:, 0, :], start=True, stop=True)
            pe.matmul(banks[1][:, NE:2 * NE], ones[:, :], sel[:, 0, :], start=True, stop=False)
            pe.matmul(banks[1][:, NE:2 * NE], strict[:, :], sel[:, 1, :], start=False, stop=True)
            pe.matmul(banks[1][:, 2 * NE:3 * NE], ones[:, :], sel[:, 0, :], start=True, stop=False)
            pe.matmul(banks[1][:, 2 * NE:3 * NE], ones[:, :], sel[:, 1, :], start=False, stop=True)\
                .then_inc(ranks_done, 1)

            def gather(jobs_before):
                pe.wait_ge(pick_ready, jobs_before + 1)
                for d in range(KT):
                    for tb in range(TB):
                        mm = pe.matmul(banks[6 + d // 4][:, (d % 4) * P:(d % 4 + 1) * P],
                                       hn[:, tb, d * P:(d + 1) * P], pick[:, tb, :], start=(tb == 0),
                                       stop=(tb == TB - 1))
                mm.then_inc(xg_done, 1)

            gather(0)
            pe.wait_ge(pickT_ready, 1)
            for half in range(2):
                mm = pe.matmul(banks[4 + half][:, :], pickT[:, 0, :], ysb[:, half * 512:(half + 1) * 512], start=True,
                               stop=True)
            mm.then_inc(zero_sums, 1)

            def combine(tb, b0):
                for half in range(2):
                    mm = pe.matmul(banks[b0 + half][:, :], pickT[:, tb, :], ysb[:, half * 512:(half + 1) * 512],
                                   start=True, stop=True)
                mm.then_inc(comb_done, 1)

            def job(j, u0, s0):
                def more(c):
                    if c == 0:
                        pe.wait_ge(y_ready, 2 * j + 2)
                        pe.wait_ge(pickT_ready, j + 1)
                        combine(0, 6)
                    if c == 1:
                        pe.wait_ge(comb_took, 2 * j + 1)
                        combine(1, 6)
                    if c == 2:
                        pe.wait_ge(comb_took, 2 * j + 2)
                        pe.wait_ge(pick_ready, j + 1)
                        for tb in range(TB):
                            mm = pe.transpose(banks[6][:, tb * P:(tb + 1) * P], pickw[:, tb, :], ident[:, :])
                        mm.then_inc(pickT_done, 1)
                    if c == 4:
                        pe.wait_ge(pickT_ready, j + 2)
                        gather(j + 1)

                pe.wait_ge(xT_lo_ready, j + 1)
                ffn(1, xT_hi, xT_lo, u0, s0, more)

            with pe.Fori(0, NE) as e:
                job(e, e * FFN_SLOTS + FFN_SLOTS, e * NCH + DENSE)
            pe.wait_ge(steer_ready, 1)
            novf_r = pe.value_load(steer[0:1, 3:4], min_val=0, max_val=3)
            with pe.Fori(0, 3) as o:
                with pe.If(novf_r > o):
                    job(o + NE, o * FFN_SLOTS + (NE + 1) * FFN_SLOTS, o * NCH + (DENSE + NE * NCH))
            pe.wait_ge(y_ready, novf_r * 2 + (2 * NE + 2))
            pe.wait_ge(pickT_ready, novf_r + (NE + 1))
            pe.wait_ge(xg_ready, novf_r + (NE + 1))
            for tb in range(TB):
                combine(tb, 4 + 2 * tb)

        @block.sync
        def _(sp):
            def mixer_loads(l):
                p = BASE_MIX[l]
                for segs in ([(0, 0, UA)], [(0, UA, UB), (UB, O_DT, SSD_H)], [(0, O_LRU, 512)],
                             [(0, O_XBC, 512)], [(0, O_XBC + 512, 256), (256, O_SSD, GW)]):
                    for half in range(2):
                        rows = w_in[l, half * 512:(half + 1) * 512, :].rearrange("(k p) n -> p k n", p=P)
                        wait_free(p)
                        for at, src, n in segs:
                            sp.dma_start(slot_k(p)[:, :, at:at + n], rows[:, :, src:src + n])\
                                .then_inc(slot_full[p % RING], 16)
                        p += 1
                for q in range(4):
                    wait_free(p)
                    sp.dma_start(slot_r(p), w_out[l, q * 256:(q + 1) * 256, :].rearrange("(k p) n -> p k n", p=P))\
                        .then_inc(slot_full[p % RING], 16)
                    p += 1

            def wait_free(p):
                q = p - RING
                if q < 0:
                    return
                if q in freed:
                    sp.wait_ge(*freed[q])
                else:
                    sp.wait_ge(lo_ready, q - BASE_FFN[0] + 1)

            def ffn_load(wg, wu, wd, at, p):
                (w, c), h = FFN_ORDER[at // 2], at % 2
                if w == "down":
                    r0 = c * FC + h * 256
                    dst, src = slot_r(p), wd[r0:r0 + 256, :]
                else:
                    dst = slot_k(p)
                    src = (wg if w == "gate" else wu)[h * 512:(h + 1) * 512, c * FC:(c + 1) * FC]
                sp.dma_start(dst, src.rearrange("(k p) n -> p k n", p=P)).then_inc(slot_full[p % RING], 16)

            def expert_loads(e, j, lo, hi):
                for at in range(lo, hi):
                    first_down = AT["down", 0]
                    if at != first_down:
                        sp.wait_ge(lo_ready, j * FFN_SLOTS
                                   + (FFN_SLOTS + at - RING + (2 if at == first_down - 1 else 1)))
                    ffn_load(moe_w_gate[0, e], moe_w_up[0, e], moe_w_down[0, e], at, BASE_FFN[1] + at)

            for tb in range(TB):
                sp.dma_start(xres[:, tb, :], x[0, tb * P:(tb + 1) * P, :]).then_inc(x_in, 16)

            def rows(name, src, n, cols=P):
                r0 = PR[name]
                sp.dma_start(prow[r0:r0 + n, :, 0:cols], src).then_inc(prow_in, 16)

            sp.wait_ge(prow_zero, 1)
            rows("mix", norm_mix.rearrange("l (a b) -> a l b", b=P), 8)
            rows("ffn", norm_ffn.rearrange("l (a b) -> a l b", b=P), 8)
            rows("grp", group_norm.rearrange("l g (a b) -> (g a) l b", b=P), 8)
            rows("lcw", lru_conv_w.rearrange("l g (a b) -> (g a) l b", b=P), 8)
            rows("lcb", lru_conv_b.rearrange("l (a b) -> a l b", b=P), 2)
            rows("lbg", lru_b_gate.rearrange("l g (a b) -> (g a) l b", b=P), 4)
            rows("lam", lru_lambda.rearrange("l (a b) -> a l b", b=P), 2)
            rows("scw", ssd_conv_w.rearrange("l g (a b) -> (g a) l b", b=P), 24)
            rows("scb", ssd_conv_b.rearrange("l (a b) -> a l b", b=P), 6)
            rows("kvn", mla_kv_norm.rearrange("l (a b) -> a l b", b=P), 1)
            rows("qn", mla_q_norm.rearrange("l (a b) -> a l b", b=96), 2, 96)
            sp.dma_start(pe_row[:, :, :].rearrange("r l (i d) -> r (l i) d", i=2),
                         nsa_cmp_pe.rearrange("l i r d -> r (l i) d")).then_inc(prow_in, 16)
            mixer_loads(0)
            for at in range(FFN_SLOTS):
                wait_free(BASE_FFN[0] + at)
                ffn_load(ffn_w_gate[0], ffn_w_up[0], ffn_w_down[0], at, BASE_FFN[0] + at)
            mixer_loads(1)
            for at in range(RING):
                wait_free(BASE_FFN[1] + at)
                ffn_load(moe_w_gate[0, 0], moe_w_up[0, 0], moe_w_down[0, 0], at, BASE_FFN[1] + at)
            with sp.Fori(0, NE - 1) as e:
                expert_loads(e, e, RING, FFN_SLOTS)
                expert_loads(e + 1, e + 1, 0, RING)
            expert_loads(NE - 1, NE - 1, RING, FFN_SLOTS)
            sp.wait_ge(steer_ready, 1)
            novf_r = sp.value_load(steer[0:1, 3:4], min_val=0, max_val=3)
            with sp.Fori(0, 3) as o:
                with sp.If(novf_r > o):
                    ex = sp.value_load(steer[0:1, bass.ds(o, 1)], min_val=0, max_val=NE - 1)
                    expert_loads(ex, o + NE, 0, FFN_SLOTS)
            for tb in range(TB):
                sp.wait_ge(out_ready, tb + 1)
                sp.dma_start(out[0, tb * P:(tb + 1) * P, :], hn[:, tb, :]).then_inc(out_stored, 16)
            sp.wait_ge(out_stored, 16 * TB)

        @block.gpsimd
        def _(pool):
            chain = [0]

            def link(ins):
                chain[0] += 1
                ins.then_inc(pool_chain, 1)
                pool.wait_ge(pool_chain, chain[0])

            pool.dma_start(pos_i[:, :], positions.rearrange("(t p) -> p t", p=P),
                           allow_slow_non_contiguous=True).then_inc(pos_in, 16)
            def mixer_weights(l):
                pool.dma_start(w_uq[:, :, :], mla_w_uq[l].rearrange("(i p) n -> p i n", p=96)).then_inc(mixw_in, 16)
                pool.dma_start(w_ukv[:, :], mla_w_ukv[l]).then_inc(mixw_in, 16)
                for i in range(2):
                    pool.dma_start(w_cmp[i * HD:(i + 1) * HD, :, :],
                                   nsa_w_cmp[l, i].rearrange("(j d) e -> d j e", d=HD)).then_inc(mixw_in, 16)

            link(pool.memset(ones[:, :], 1.0))
            link(pool.memset(ident[:, :], 0.0))
            link(pool.memset(cbias[:, :], 0.0))
            link(pool.memset(cmask[:, :, :], 1.0))
            link(pool.memset(cmbias[:, :, :], 0.0))
            link(pool.memset(minus_half[:, :], -0.5))
            link(pool.memset(lraw[:, 0:2, 0:3], 0.0))
            link(pool.memset(xraw[:, :, 0:3], 0.0))
            inv_freq = np.float32(ROPE_THETA) ** (-np.arange(0, ROPE, 2, dtype=np.float32) / np.float32(ROPE))
            for i in range(16):
                link(pool.memset(inv[:, i:i + 1], float(inv_freq[i])))
            link(pool.affine_select(out=ident[:, :], in_=ident[:, :], compare_op=ALU.not_equal, fill=1.0, base=0,
                                    pattern=[[-1, P]], channel_multiplier=1))
            link(pool.affine_select(out=upper[:, :], in_=ones[:, :], compare_op=ALU.is_ge, fill=0.0, base=0,
                                    pattern=[[1, P]], channel_multiplier=-1))
            link(pool.affine_select(out=strict[:, :], in_=ones[:, :], compare_op=ALU.is_ge, fill=0.0, base=-1,
                                    pattern=[[1, P]], channel_multiplier=-1))
            link(pool.affine_select(out=cbias[:, P:2 * P], in_=cbias[:, P:2 * P], compare_op=ALU.is_ge, fill=NEG,
                                    base=0, pattern=[[-1, P]], channel_multiplier=1))
            for tb in range(TB):
                for m, fill in ((cmask, 0.0), (cmbias, NEG)):
                    link(pool.affine_select(out=m[:, tb, :], in_=m[:, tb, :], compare_op=ALU.is_ge, fill=fill,
                                            base=tb * P - (CLEN - 1), pattern=[[-CSTRIDE, NC]],
                                            channel_multiplier=1))
            pool.iota(iota[:, :], pattern=[[1, P]], base=0, channel_multiplier=0,
                      allow_small_or_imprecise_dtypes=True).then_inc(consts_ready, 1)
            pool.wait_ge(consts_ready, 1)

            sets = [0, 0]

            def roots(n):
                c0 = 4 * sets[0]
                sets[0] += 1
                sets[1] += n
                pool.wait_ge(ms_ready, sets[1])
                link(pool.tensor_scalar(stat[:, c0:c0 + n], stat[:, c0:c0 + n], EPS, None, ALU.add))
                pool.tensor_tensor(rstd[:, c0:c0 + n], stat[:, c0:c0 + n], minus_half[:, 0:n], ALU.pow)\
                    .then_inc(rstd_ready, 1)

            for l in range(L):
                roots(2)
                if l == 0:
                    mixer_weights(0)
                    for i, src in enumerate((ssd_dt_bias, ssd_a_log, ssd_d)):
                        pool.dma_start(ssd_par[:, :, i, :], src[:, :].partition_broadcast(P)).then_inc(misc_in, 16)
                    pool.wait_ge(lru_w_zero, 1)
                    for odd in range(2):
                        o = odd * 64
                        pool.dma_start(lru_w[o:o + 64, :, :, :, o:o + 64].rearrange("i l g k j -> i (l g k) j"),
                                       lru_w_gate.rearrange("l g (k q) i j -> q i (l g k) j", q=2)[odd])\
                            .then_inc(misc_in, 16)
                    pool.dma_start(router[:, :, :], moe_router[0].rearrange("(k p) e -> p k e", p=P))\
                        .then_inc(misc_in, 16)
                    pool.dma_start(gfin[:, :], norm_final[:].partition_broadcast(P)).then_inc(misc_in, 16)
                roots(4)
                if l == 0:
                    pool.wait_ge(for_dve, mark["cmp", 0])
                    mixer_weights(1)
                roots(2)
                roots(4)
                roots(2)
            roots(2)

        @block.scalar
        def _(act):
            chain = [0]
            took = [0]

            def link(ins):
                chain[0] += 1
                ins.then_inc(act_chain, 1)
                act.wait_ge(act_chain, chain[0])

            def filled():
                b = banks[4 + took[0] % 4]
                took[0] += 1
                act.wait_ge(for_act, took[0])
                return b

            squares = [0]

            def mean_square(dst_set, i, src, n, to):
                if squares[0]:
                    act.wait_ge(ms_ready, squares[0])
                squares[0] += 1
                act.activation(to, src, ACT.Square, scale=float(n) ** -0.5,
                               accum_out=stat[:, 4 * dst_set + i:4 * dst_set + i + 1]).then_inc(ms_ready, 1)

            act.wait_ge(x_in, 16 * TB)
            def ffn(n, u0, s0, fill0, filled0, more=None):
                landed = [0] * RING

                def split(at):
                    i = at % RING
                    landed[i] += 16
                    act.wait_ge(slot_full[i], fill0 + (filled0[i] + landed[i]))
                    if n == 1:
                        act.wait_ge(units_used, u0 + (at - SPLIT + 1))
                    elif at >= SPLIT:
                        act.wait_ge(units_used, at - SPLIT + 1)
                    act.activation(w_hi[:, at % SPLIT, :], ring[:, i, :], ACT.Copy).then_inc(hi_ready, 1)

                def turned(c):
                    for i in range(n):
                        v = (c * n + i) % 2
                        act.wait_ge(hidT_done, s0 + (c * n + i + 1))
                        act.activation(hidT_hi[:, v, :], banks[2 + v][:, :], ACT.Copy).then_inc(hidT_hi_ready, 1)

                for c in range(NCH):
                    split(at_gate(c, 0))
                    split(at_gate(c, 1))
                    if c == 0 and more is not None:
                        more()
                    split(at_up(c, 0))
                    if c >= 1:
                        turned(c - 1)
                    split(at_up(c, 1))
                    act.wait_ge(units_used, u0 + (at_gate(c, 1) + 1))
                    for i in range(n):
                        v = (c * n + i) % 2
                        act.activation(sgate[:, v, :], banks[v][:, :], ACT.Silu).then_inc(silu_done, 1)
                    if c >= 1:
                        split(at_down(c - 1, 0))
                        split(at_down(c - 1, 1))
                split(at_down(NCH - 1, 0))
                split(at_down(NCH - 1, 1))
                turned(NCH - 1)

            for l in range(L):
                if l > 0:
                    act.wait_ge(res_ready, 2 * l)
                for tb in range(TB):
                    mean_square(5 * l, tb, xres[:, tb, :], D, hn[:, tb, :])
                if l == 0:
                    act.wait_ge(rope_args, 1)
                    act.activation(trig[:, :, :, :], rr[:, :, :, :], ACT.Sin).then_inc(trig_ready, 1)
                    act.wait_ge(lam_args, 1)
                    act.activation(lru_t[:, :, 1, :], lru_t[:, :, 0, :], ACT.Exp).then_inc(lam_logs, 1)
                    act.wait_ge(lam_logs, 1)
                    act.activation(lru_t[:, :, 3, :], lru_t[:, :, 1, :], ACT.Ln, bias=1.0).then_inc(lam_logs, 1)
                    act.wait_ge(misc_in, 16 * N_MISC)
                    act.activation(neg_a[:, :, :], ssd_par[:, :, 1, :], ACT.Exp).then_inc(lam_logs, 1)
                for unit, n in ((0, UA), (1, UB + SSD_H)):
                    for tb in range(TB):
                        b = filled()
                        act.activation(utok[:, tb, unit * UA:unit * UA + n], b[:, 0:n], ACT.Copy)\
                            .then_inc(act_took, 1)
                act.wait_ge(act_took, took[0])
                for tb in range(TB):
                    mean_square(5 * l + 1, tb, utok[:, tb, 0:QR], QR, junk[:, 0, 0:QR])
                    mean_square(5 * l + 1, 2 + tb, utok[:, tb, QR:QR + KVR], KVR, junk[:, 1, 0:KVR])
                act.activation(gates[:, :, :], utok[:, :, O_LRU - 3 * NH:O_LRU], ACT.Tanh, scale=0.5)\
                    .then_inc(gate_th, 1)
                act.wait_ge(ssd_vec, 4 * l + 1)
                link(act.activation(dts[:, 2, :, :], dts[:, 1, :, :], ACT.Exp, scale=-1.0))
                act.activation(dts[:, 3, :, :], dts[:, 2, :, :], ACT.Ln, bias=1.0).then_inc(ssd_act, 1)
                for tb in range(TB):
                    b = filled()
                    act.activation(qtok[:, tb, :, :], b[:, 0:MLA_H * QK].rearrange("p (h d) -> p h d", h=MLA_H),
                                   ACT.Copy).then_inc(act_took, 1)
                    v = filled()[:, :].rearrange("p (h d) -> p h d", h=MLA_H)
                    act.activation(kcat[:, tb, :, 0:NOPE], v[:, :, 0:NOPE], ACT.Copy)
                    act.activation(vtok[:, tb, :, :], v[:, :, NOPE:], ACT.Copy).then_inc(act_took, 1)
                for hp in range(2):
                    b = filled()
                    act.activation(nqT[0:HD, 2 * hp:2 * hp + 2, :],
                                   b[0:HD, :].rearrange("p (h t) -> p h t", h=2), ACT.Copy).then_inc(act_took, 1)
                b = filled()
                act.activation(kvcT[:, :], b[:, 0:S], ACT.Copy)
                act.activation(ksT[0:HD, :], b[0:HD, S:2 * S], ACT.Copy).then_inc(act_took, 1)
                b = filled()
                act.activation(kwT[0:HD, :], b[0:HD, 0:S], ACT.Copy).then_inc(act_took, 1)
                for dst in (qT, kT):
                    for hp in range(2):
                        b = filled()
                        act.activation(dst[0:QK, 2 * hp:2 * hp + 2, :],
                                       b[0:QK, :].rearrange("p (h t) -> p h t", h=2), ACT.Copy)\
                            .then_inc(act_took, 1)

                def exps(n):
                    br, tb = AJ[n]
                    nk = NC if br == "cmp" else (tb + 1) * P
                    act.wait_ge(rmax_ready, 8 * l + n + 1)
                    for h in range(4):
                        e = act.activation(prob[:, n % 2, h, 0:nk], prob[:, n % 2, h, 0:nk], ACT.Exp,
                                           bias=rmax[:, n, h:h + 1], accum_out=rsum[:, n, h:h + 1])
                    e.then_inc(exp_ready, 1)

                def turned_probs(n):
                    br, tb = AJ[n]
                    if n >= 2:
                        act.wait_ge(for_dve, mark["pv", l, n - 2])
                    rows = NC if br == "cmp" else P
                    for i in range(1 if br == "cmp" else tb + 1):
                        b = filled()
                        act.activation(probT[0:rows, n % 2, i * 512:(i + 1) * 512], b[0:rows, :], ACT.Copy)\
                            .then_inc(act_took, 1)

                for n in range(len(AJ) + 1):
                    if n < len(AJ):
                        exps(n)
                    if n >= 1:
                        turned_probs(n - 1)
                    if n == 0:
                        if l == 0:
                            act.wait_ge(half_b_ready, 1)
                        for g in range(2):
                            b = filled()
                            for i in range(2):
                                e = act.activation(lth[:, 2 * g + i, :], b[:, i * S:(i + 1) * S], ACT.Tanh, scale=0.5,
                                                   bias=half_b[:, l, 2 * g + i:2 * g + i + 1])
                            e.then_inc(act_took, 1)
                    if n == 1:
                        act.wait_ge(lru_vec, 5 * l + 1)
                        act.activation(lgate[:, :, :], lgate[:, :, :], ACT.Tanh, scale=float(np.sqrt(2 / np.pi)))\
                            .then_inc(lru_act, 1)
                        act.wait_ge(ssd_conv, l + 1)
                        act.activation(xbc[:, :, :], xbc[:, :, :], ACT.Silu)
                        act.activation(zs[:, :, :], zs[:, :, :], ACT.Silu).then_inc(ssd_act, 1)
                    if n == 2:
                        act.wait_ge(lru_vec, 5 * l + 2)
                        act.activation(lt1[:, :, :], la[:, :, :], ACT.Tanh)
                        act.activation(lt2[:, :, :], la[:, :, :], ACT.Tanh, scale=0.5).then_inc(lru_act, 1)
                    if n == 3:
                        act.wait_ge(ssd_vec, 4 * l + 3)
                        act.activation(dec0[:, :, :], dec0[:, :, :], ACT.Exp)
                        act.activation(dec1[:, :, :], dec1[:, :, :], ACT.Exp).then_inc(ssd_act, 1)
                    if n == 4:
                        act.wait_ge(lru_vec, 5 * l + 3)
                        act.activation(lb[:, :, :], lb[:, :, :], ACT.Sqrt).then_inc(lru_act, 1)
                    if n == 6:
                        act.wait_ge(lru_vec, 5 * l + 4)
                        act.activation(lt1[:, :, :], xb[:, :, :], ACT.Square, scale=GW ** -0.5).then_inc(lru_act, 1)
                        act.wait_ge(ssd_vec, 4 * l + 4)
                        for tb in range(TB):
                            mean_square(5 * l + 2, tb, yd[:, tb, :], GW, junk[:, 1, :])
                    if n == 8:
                        act.wait_ge(lru_vec, 5 * l + 5)
                        act.activation(lrstd[:, :], lrstd[:, :], ACT.Sqrt).then_inc(lru_act, 1)

                act.wait_ge(o_ready, l + 1)
                for i, o in enumerate((oa, ob)):
                    for tb in range(TB):
                        mean_square(5 * l + 3, 2 * i + tb, o[:, tb, :], GW, junk[:, 0, :])


                act.wait_ge(res_ready, 2 * l + 1)
                for tb in range(TB):
                    mean_square(5 * l + 4, tb, xres[:, tb, :], D, hn[:, tb, :])
                if l == 0:
                    act.wait_ge(hT_ready, 2)
                    act.activation(hT_hi[:, :, :], hT[:, :, :], ACT.Copy).then_inc(hT_hi_ready, 1)
                    ffn(TB, 0, 0, 0, fills[0])

            act.wait_ge(route_diff, 1)
            act.activation(topw[:, 1, :], topw[:, 0, :], ACT.Exp).then_inc(route_exp, 1)

            PER_JOB = 16 * FFN_SLOTS // RING

            def output_by_slot(u0):
                if u0 is not None:
                    act.wait_ge(units_used, u0)
                for half in range(2):
                    act.activation(ysb[:, half * 512:(half + 1) * 512], banks[4 + half][:, :], ACT.Copy)\
                        .then_inc(y_ready, 1)

            def split_tokens(jobs_before, u_read=None):
                act.wait_ge(xg_ready, jobs_before + 1)
                if u_read is not None:
                    act.wait_ge(units_used, u_read)
                act.activation(xT_hi[:, :, :], xg[:, :, :], ACT.Copy).then_inc(xT_hi_ready, 1)

            split_tokens(0)
            act.wait_ge(zero_sums, 1)

            def job(j, u0, s0):
                def more():
                    output_by_slot(u0)
                ffn(1, u0, s0, j * PER_JOB, fills[1], more)
                split_tokens(j + 1, u0 + (at_up(NCH - 1, 1) + 1))

            with act.Fori(0, NE) as e:
                job(e, e * FFN_SLOTS + FFN_SLOTS, e * NCH + DENSE)
            act.wait_ge(steer_ready, 1)
            novf_r = act.value_load(steer[0:1, 3:4], min_val=0, max_val=3)
            with act.Fori(0, 3) as o:
                with act.If(novf_r > o):
                    job(o + NE, o * FFN_SLOTS + (NE + 1) * FFN_SLOTS, o * NCH + (DENSE + NE * NCH))
            output_by_slot(novf_r * FFN_SLOTS + (NE + 1) * FFN_SLOTS)

        @block.vector
        def _(dve):
            chain = [0]
            took = [0]

            def link(ins):
                chain[0] += 1
                ins.then_inc(dve_chain, 1)
                dve.wait_ge(dve_chain, chain[0])

            counts = {}

            def signal(ins, name, s):
                counts[name] = counts.get(name, 0) + 1
                ins.then_inc(s, 1)
                dve.wait_ge(s, counts[name])

            def filled():
                b = banks[took[0] % 4]
                took[0] += 1
                dve.wait_ge(for_dve, took[0])
                return b

            def take_bank(ins):
                ins.then_inc(dve_took, 1)
                dve.wait_ge(dve_took, took[0])

            dve.memset(prow[:, :, :], 0.0).then_inc(prow_zero, 1)
            dve.memset(lru_w[:, :, :, :, :], 0.0).then_inc(lru_w_zero, 1)

            dve.wait_ge(consts_ready, 1)
            dve.wait_ge(pos_in, 16)
            link(dve.tensor_copy(pos_f[:, :], pos_i[:, :]))
            for tb in range(TB):
                link(dve.tensor_scalar(ang[:, tb, :], inv[:, :], pos_f[:, tb:tb + 1], None, ALU.mult))
            TURN = 2 * np.pi
            MAGIC = 1.5 * 2.0 ** 23
            PARTS = [6.28125, 1.93500518798828125e-3]
            PARTS.append(TURN - sum(PARTS))
            for i in range(2):
                link(dve.tensor_scalar(rk[:, i, :, :], ang[:, :, :], 1 / TURN, 0.25 * i, ALU.mult, ALU.add))
                link(dve.tensor_scalar(rk[:, i, :, :], rk[:, i, :, :], MAGIC, None, ALU.add))
                link(dve.tensor_scalar(rk[:, i, :, :], rk[:, i, :, :], -MAGIC, None, ALU.add))
                src = ang
                for part in PARTS:
                    s_ = src[:, :, :] if src is ang else rr[:, i, :, :]
                    link(dve.scalar_tensor_tensor(out=rr[:, i, :, :], in0=rk[:, i, :, :], scalar=-part, in1=s_,
                                                  op0=ALU.mult, op1=ALU.add))
                    src = rr
            link(dve.tensor_scalar(rr[:, 1, :, :], rr[:, 1, :, :], np.pi / 2, None, ALU.add))
            signal(dve.tensor_scalar(rr[:, :, :, :], rr[:, :, :, :], -3.1415925, 3.1415925, ALU.max, ALU.min),
                   "rope", rope_args)

            b = filled()
            link(dve.tensor_copy(par[:, :, :], b[:, 0:2 * P].rearrange("p (l c) -> p l c", l=L)))
            take_bank(dve.tensor_copy(pe_t[:, :, :], b[:, 2 * P:2 * P + L * CLEN].rearrange("p (l c) -> p l c", l=L)))
            lam = par[:, :, PR["lam"]:PR["lam"] + 2]
            link(dve.tensor_scalar(lru_t[:, :, 5, :], lam, -1.0, None, ALU.mult))
            signal(dve.tensor_tensor(lru_t[:, :, 0, :], lru_t[:, :, 5, :], lam, ALU.min), "lam", lam_args)
            signal(dve.tensor_scalar(half_b[:, :, :], par[:, :, PR["lbg"]:PR["lbg"] + 4], 0.5, None, ALU.mult),
                   "half_b", half_b_ready)
            dve.wait_ge(x_in, 16 * TB)

            def normed(l2, turn_set):
                dve.wait_ge(rstd_ready, turn_set + 1)
                for tb in range(TB):
                    ins = dve.tensor_scalar(hn[:, tb, :], xres[:, tb, :],
                                            rstd[:, 4 * turn_set + tb:4 * turn_set + tb + 1], None, ALU.mult)
                    if tb == TB - 1:
                        signal(ins, "hn", hn_ready)
                l, which = divmod(l2, 2)
                c0 = PR["ffn" if which else "mix"]
                for g in range(4):
                    b = filled()
                    gain = par[:, l, c0 + 2 * g:c0 + 2 * g + 2].unsqueeze(2).broadcast_to([P, 2, S])
                    take_bank(dve.tensor_tensor(hT[:, 2 * g:2 * g + 2, :], b[:, :].rearrange("p (k t) -> p k t", k=2),
                                                gain, ALU.mult))
                signal(dve.tensor_copy(hT_flag[:, 0:1], ones[:, 0:1]), "hT", hT_ready)

            def rope(v, cos, sin, shape):
                n = int(np.prod(shape[1:]))
                names = " ".join("abc"[:len(shape) - 1])
                r = [rt[:, i, 0:n].rearrange(f"p ({names}) -> p {names}", **dict(zip("bc", shape[2:])))
                     if len(shape) > 2 else rt[:, i, 0:n] for i in range(4)]
                for i, (a, t) in enumerate(((v[0], cos), (v[1], sin), (v[1], cos), (v[0], sin))):
                    link(dve.tensor_tensor(r[i], a, t, ALU.mult))
                link(dve.tensor_tensor(v[0], r[0], r[1], ALU.subtract))
                return dve.tensor_tensor(v[1], r[2], r[3], ALU.add)

            def ffn(n, u0, s0, more=None):
                def split(at):
                    dve.wait_ge(hi_ready, u0 + (at + 1))
                    dve.tensor_tensor(w_lo[:, at % SPLIT, :], ring[:, at % RING, :],
                                      w_hi[:, at % SPLIT, :].bitcast(F32), ALU.subtract).then_inc(lo_ready, 1)

                def turned(c):
                    for i in range(n):
                        v = (c * n + i) % 2
                        dve.wait_ge(hidT_hi_ready, s0 + (c * n + i + 1))
                        dve.tensor_tensor(hidT_lo[:, v, :], banks[2 + v][:, :], hidT_hi[:, v, :].bitcast(F32),
                                          ALU.subtract).then_inc(hidT_lo_ready, 1)

                def hidden(c):
                    dve.wait_ge(units_used, u0 + (at_up(c, 1) + 1))
                    dve.wait_ge(silu_done, s0 + n * (c + 1))
                    for i in range(n):
                        v = (c * n + i) % 2
                        dve.tensor_tensor(hid[:, v, :], sgate[:, v, :], banks[2 + v][:, :], ALU.mult)\
                            .then_inc(hid_ready, 1)

                for c in range(NCH):
                    split(at_gate(c, 0))
                    split(at_gate(c, 1))
                    if c == 1:
                        hidden(0)
                        if more is not None:
                            more(0)
                    split(at_up(c, 0))
                    if c >= 1:
                        turned(c - 1)
                    split(at_up(c, 1))
                    if c >= 1:
                        split(at_down(c - 1, 0))
                        split(at_down(c - 1, 1))
                        hidden(c)
                        if more is not None:
                            more(c)
                split(at_down(NCH - 1, 0))
                split(at_down(NCH - 1, 1))
                turned(NCH - 1)

            for l in range(L):
                normed(2 * l, 5 * l)
                if l == 0:
                    dve.wait_ge(lam_logs, 2)
                    e_, w_, lg, d_, t_ = (lru_t[:, :, i, :] for i in (1, 2, 3, 4, 5))
                    link(dve.tensor_scalar(w_, e_, 1.0, None, ALU.add))
                    link(dve.tensor_scalar(w_, w_, -1.0, None, ALU.add))
                    link(dve.tensor_scalar(d_, w_, 1e-30, None, ALU.max))
                    link(dve.reciprocal(d_, d_))
                    link(dve.tensor_tensor(lg, lg, e_, ALU.mult))
                    link(dve.tensor_tensor(lg, lg, d_, ALU.mult))
                    link(dve.scalar_tensor_tensor(out=w_, in0=w_, scalar=0.0, in1=e_, op0=ALU.is_equal, op1=ALU.mult))
                    link(dve.tensor_tensor(lg, lg, w_, ALU.add))
                    link(dve.scalar_tensor_tensor(out=lg, in0=t_, scalar=0.0, in1=lg, op0=ALU.max, op1=ALU.add))
                    link(dve.tensor_scalar(lru_c[:, :, 0:2], lg, -4.0, None, ALU.mult))
                    dve.wait_ge(trig_ready, 1)
                    dve.wait_ge(misc_in, 16 * N_MISC)
                    dve.wait_ge(lam_logs, 3)

                dve.wait_ge(act_took, mark["u", l])
                bias = ssd_par[:, l, 0:1, :].broadcast_to([P, TB, SSD_H])
                link(dve.tensor_tensor(dts[:, 0, :, :], utok[:, :, O_LRU:O_LRU + SSD_H], bias, ALU.add))
                link(dve.tensor_scalar(dts[:, 1, :, :], dts[:, 0, :, :], -1.0, None, ALU.mult))
                signal(dve.tensor_tensor(dts[:, 1, :, :], dts[:, 1, :, :], dts[:, 0, :, :], ALU.max),
                       "ssd_vec", ssd_vec)
                dve.wait_ge(rstd_ready, 5 * l + 2)
                r0 = 4 * (5 * l + 1)
                for tb in range(TB):
                    link(dve.tensor_scalar(cqn[:, tb, :], utok[:, tb, 0:QR], rstd[:, r0 + tb:r0 + tb + 1], None,
                                           ALU.mult))
                    ins = dve.tensor_scalar(ckvn[:, tb, :], utok[:, tb, QR:QR + KVR],
                                            rstd[:, r0 + 2 + tb:r0 + 3 + tb], None, ALU.mult)
                    if tb == 0:
                        link(ins)
                    else:
                        signal(ins, "cn", cn_ready)
                cosn, sinn = trig[:, 1, :, 0:16:2], trig[:, 0, :, 0:16:2]
                for c0, n, step in ((O_NSA, NH, HD), (KV0, 3, 2 * HD)):
                    v = utok[:, :, c0:c0 + n * step].rearrange("p t (h d) -> p t h d", h=n)
                    sh = [P, TB, n, NROT // 2]
                    ins = rope((v[:, :, :, 0:8], v[:, :, :, 8:16]), cosn.unsqueeze(2).broadcast_to(sh),
                               sinn.unsqueeze(2).broadcast_to(sh), sh)
                    if c0 == O_NSA:
                        link(ins)
                    else:
                        signal(ins, "nsa_roped", nsa_roped)
                v = utok[:, :, QR + KVR:QR + KVR + ROPE]
                link(rope((v[:, :, 0:16], v[:, :, 16:32]), trig[:, 1, :, :], trig[:, 0, :, :], [P, TB, 16]))

                for i in range(2):
                    b = filled()
                    take_bank(dve.tensor_copy(lraw[:, 2 * i:2 * i + 2, 3:3 + S],
                                              b[:, :].rearrange("p (k t) -> p k t", k=2)))
                for i in range(3):
                    b = filled()
                    take_bank(dve.tensor_copy(xraw[:, 2 * i:2 * i + 2, 3:3 + S],
                                              b[:, :].rearrange("p (k t) -> p k t", k=2)))
                b = filled()
                take_bank(dve.tensor_copy(zs[:, :, :], b[:, :].rearrange("p (k t) -> p k t", k=2)))

                b = filled()
                gain = par[0:96, l, PR["qn"]:PR["qn"] + 2].unsqueeze(2).broadcast_to([96, 2, S])
                take_bank(dve.tensor_tensor(cqT[0:96, :, :], b[0:96, :].rearrange("p (k t) -> p k t", k=2), gain,
                                            ALU.mult))
                b = filled()
                take_bank(dve.tensor_scalar(ckvT[:, :], b[:, 0:S], pcol(l, "kvn"), None, ALU.mult))
                signal(dve.tensor_copy(hT_flag[:, 0:1], ones[:, 0:1]), "cT", cT_ready)

                def conv(dst, raw, w, bias_, n):
                    for i in range(n):
                        link(dve.tensor_scalar(dst[:, i, :], raw[:, i, 0:S], pcol(l, w, i), pcol(l, bias_, i),
                                               ALU.mult, ALU.add))
                        for t in range(1, 4):
                            ins = dve.scalar_tensor_tensor(out=dst[:, i, :], in0=raw[:, i, t:t + S],
                                                           scalar=pcol(l, w, n * t + i), in1=dst[:, i, :],
                                                           op0=ALU.mult, op1=ALU.add)
                            if not (t == 3 and i == n - 1):
                                link(ins)
                    return ins

                signal(conv(xb, lraw, "lcw", "lcb", 2), "lru_conv", lru_conv)

                dve.wait_ge(act_took, mark["qkv", l])
                sh = [P, TB, MLA_H, ROPE // 2]
                v = qtok[:, :, :, NOPE:QK]
                link(rope((v[:, :, :, 0:16], v[:, :, :, 16:32]), trig[:, 1, :, :].unsqueeze(2).broadcast_to(sh),
                          trig[:, 0, :, :].unsqueeze(2).broadcast_to(sh), sh))
                kpe = utok[:, :, QR + KVR:QR + KVR + ROPE].unsqueeze(2).broadcast_to([P, TB, MLA_H, ROPE])
                signal(dve.tensor_copy(kcat[:, :, :, NOPE:QK], kpe), "qk_roped", qk_roped)

                dve.wait_ge(act_took, mark["nsa", l])
                for i in range(2):
                    src = kvcT[:, 16 * i:16 * i + 16 * NC].rearrange("p (n j) -> p j n", j=16)
                    pos = pe_t[:, l, 16 * i:16 * i + 16].unsqueeze(2).broadcast_to([P, 16, NC])
                    ins = dve.tensor_tensor(cin[:, 16 * i:16 * i + 16, :], src, pos, ALU.add)
                    if i == 0:
                        link(ins)
                    else:
                        signal(ins, "cin", cin_ready)
                signal(conv(xbc, xraw, "scw", "scb", 6), "ssd_conv", ssd_conv)
                b = filled()
                link(dve.tensor_copy(kcT[0:HD, :], b[0:HD, 0:NC]))
                take_bank(dve.tensor_copy(vc[0:NC, :], b[0:NC, 64:64 + HD]))
                signal(dve.tensor_copy(hT_flag[:, 0:1], ones[:, 0:1]), "cmp", cmp_ready)
                dve.wait_ge(gate_th, l + 1)
                link(dve.tensor_scalar(gates[:, :, :], gates[:, :, :], 0.5, 0.5, ALU.mult, ALU.add))

                def score_rows(n):
                    br, tb = AJ[n]
                    nk = NC if br == "cmp" else (tb + 1) * P
                    if n >= 2:
                        dve.wait_ge(act_took, mark["probT", l, n - 2])
                    per = 4 if br == "cmp" else 512 // nk
                    scale = float(QK if br == "mla" else HD) ** -0.5
                    m = cmbias[:, tb, :] if br == "cmp" else cbias[:, P - tb * P:2 * P]
                    for g in range(4 // per):
                        b = filled()
                        take_bank(dve.scalar_tensor_tensor(
                            out=prob[:, n % 2, g * per:(g + 1) * per, 0:nk],
                            in0=b[:, 0:per * nk].rearrange("p (h k) -> p h k", h=per), scalar=scale,
                            in1=m.unsqueeze(1).broadcast_to([P, per, nk]), op0=ALU.mult, op1=ALU.add))
                    link(dve.tensor_reduce(rmax[:, n, :], prob[:, n % 2, :, 0:nk], AX.X, ALU.max))
                    signal(dve.tensor_scalar(rmax[:, n, :], rmax[:, n, :], -1.0, None, ALU.mult),
                           "rmax", rmax_ready)

                def mask_cmp(n):
                    tb = AJ[n][1]
                    dve.wait_ge(exp_ready, 8 * l + n + 1)
                    signal(dve.tensor_tensor(prob[:, n % 2, :, 0:NC], prob[:, n % 2, :, 0:NC],
                                             cmask[:, tb:tb + 1, :].broadcast_to([P, 4, NC]), ALU.mult),
                           "masked", masked)

                def outputs(n):
                    br, tb = AJ[n]
                    dve.wait_ge(exp_ready, 8 * l + n + 1)
                    link(dve.reciprocal(coef[:, n, :], rsum[:, n, :]))
                    if br != "mla":
                        i = ("cmp", "sel", "win").index(br)
                        link(dve.tensor_tensor(coef[:, n, :], coef[:, n, :],
                                               gates[:, tb, i:i + 3 * NH - 2:3], ALU.mult))
                    b = filled()
                    c = coef[:, n, :].unsqueeze(2).broadcast_to([P, 4, HD])
                    dst = {"mla": oa[:, tb, :], "cmp": ob[:, tb, :]}.get(br, ot[:, :])
                    take_bank(dve.tensor_tensor(dst.rearrange("p (h d) -> p h d", h=4),
                                                b[:, 0:GW].rearrange("p (h d) -> p h d", h=4), c, ALU.mult))
                    if br in ("sel", "win"):
                        ins = dve.tensor_tensor(ob[:, tb, :], ob[:, tb, :], ot[:, :], ALU.add)
                        if n == len(AJ) - 1:
                            signal(ins, "o", o_ready)
                        else:
                            link(ins)

                g = lraw[:, 2:4, 3:3 + S]
                for n in range(len(AJ) + 2):
                    if n < len(AJ):
                        score_rows(n)
                    if 1 <= n <= len(AJ) and AJ[n - 1][0] == "cmp":
                        mask_cmp(n - 1)
                    if n >= 2:
                        outputs(n - 2)
                    if n == 0:
                        dve.wait_ge(ssd_act, 3 * l + 1)
                        link(dve.scalar_tensor_tensor(out=dts[:, 4, :, :], in0=dts[:, 0, :, :], scalar=0.0,
                                                      in1=dts[:, 3, :, :], op0=ALU.max, op1=ALU.add))
                        signal(dve.scalar_tensor_tensor(out=dts[:, 5, :, :], in0=dts[:, 4, :, :], scalar=-1.0,
                                                        in1=neg_a[:, l:l + 1, :].broadcast_to([P, TB, SSD_H]),
                                                        op0=ALU.mult, op1=ALU.mult), "ssd_vec", ssd_vec)
                        link(dve.tensor_tensor(lgate[:, :, :], g, g, ALU.mult))
                        link(dve.tensor_scalar(lgate[:, :, :], lgate[:, :, :], 0.044715, 1.0, ALU.mult, ALU.add))
                        signal(dve.tensor_tensor(lgate[:, :, :], lgate[:, :, :], g, ALU.mult), "lru_vec", lru_vec)
                    if n == 1:
                        dve.wait_ge(act_took, mark["lgate", l])
                        for i in range(2):
                            ins = dve.tensor_scalar(la[:, i, :], lth[:, i, :], 1.0, lru_c[:, l, i:i + 1], ALU.add, ALU.mult)
                            if i == 0:
                                link(ins)
                            else:
                                signal(ins, "lru_vec", lru_vec)
                    if n == 2:
                        b = filled()
                        take_bank(dve.tensor_copy(xtok[:, :, :], b[:, :].rearrange("p (t c) -> p t c", t=TB)))
                        for tb in range(TB):
                            link(dve.tensor_tensor(xdt[:, tb, :].rearrange("p (h d) -> p h d", h=SSD_H),
                                                   xtok[:, tb, :].rearrange("p (h d) -> p h d", h=SSD_H),
                                                   dts[:, 4, tb, :].unsqueeze(2).broadcast_to([P, SSD_H, HD]), ALU.mult))
                        b = filled()
                        take_bank(dve.tensor_scalar(nacs[:, :, :], b[:, 0:TB * SSD_H].rearrange("p (t h) -> p t h", t=TB),
                                                    -1.0, None, ALU.mult))
                        for hp in range(2):
                            b = filled()
                            for i in range(2):
                                h = 2 * hp + i
                                link(dve.tensor_scalar(dec0[:, h, :], b[:, i * S:(i + 1) * S], nacs[:, 0, h:h + 1], 0.0,
                                                       ALU.add, ALU.min))
                                ins = dve.tensor_scalar(dec1[:, h, :], b[:, i * S + P:(i + 1) * S], nacs[:, 1, h:h + 1],
                                                        0.0, ALU.add, ALU.min)
                                if i == 0:
                                    link(ins)
                            take_bank(ins)
                        signal(dve.tensor_copy(hT_flag[:, 0:1], ones[:, 0:1]), "ssd_vec", ssd_vec)
                    if n == 3:
                        dve.wait_ge(lru_act, 5 * l + 2)
                        link(dve.tensor_scalar(ld[:, :, :], lt1[:, :, :], -1.0, 1.0, ALU.mult, ALU.add))
                        link(dve.reciprocal(ld[:, :, :], ld[:, :, :]))
                        link(dve.scalar_tensor_tensor(out=lb[:, :, :], in0=lt1[:, :, :], scalar=-2.0, in1=ld[:, :, :],
                                                      op0=ALU.mult, op1=ALU.mult))
                        signal(dve.tensor_scalar(lb[:, :, :], lb[:, :, :], 0.0, None, ALU.max), "lru_vec", lru_vec)
                        link(dve.tensor_scalar(ld[:, :, :], lt2[:, :, :], -1.0, 1.0, ALU.mult, ALU.add))
                        link(dve.reciprocal(ld[:, :, :], ld[:, :, :]))
                        link(dve.scalar_tensor_tensor(out=lt2[:, :, :], in0=lt2[:, :, :], scalar=1.0, in1=ld[:, :, :],
                                                      op0=ALU.add, op1=ALU.mult))
                        link(dve.scalar_tensor_tensor(out=lt1[:, :, :], in0=lth[:, 2:4, :], scalar=1.0, in1=xb[:, :, :],
                                                      op0=ALU.add, op1=ALU.mult))
                        dve.wait_ge(lru_act, 5 * l + 1)
                        link(dve.scalar_tensor_tensor(out=lgate[:, :, :], in0=lgate[:, :, :], scalar=1.0, in1=g,
                                                      op0=ALU.add, op1=ALU.mult))
                    if n == 4:
                        dve.wait_ge(ssd_act, 3 * l + 3)
                        tri = upper[:, :].unsqueeze(1).broadcast_to([P, SSD_H, P])
                        link(dve.tensor_tensor(dec0[:, :, 0:P], dec0[:, :, 0:P], tri, ALU.mult))
                        link(dve.tensor_tensor(dec1[:, :, :], dec1[:, :, :], tri, ALU.mult))
                        for d, n in ((dec0, S), (dec1, P)):
                            b = filled()
                            for g_ in range(SSD_G):
                                v = d[:, 2 * g_:2 * g_ + 2, :]
                                sc = b[:, g_ * n:(g_ + 1) * n].unsqueeze(1).broadcast_to([P, 2, n])
                                ins = dve.tensor_tensor(v, v, sc, ALU.mult)
                                if g_ == 0:
                                    link(ins)
                            take_bank(ins)
                        signal(dve.tensor_copy(hT_flag[:, 0:1], ones[:, 0:1]), "dec", dec_ready)
                    if n == 5:
                        dve.wait_ge(lru_act, 5 * l + 3)
                        link(dve.scalar_tensor_tensor(out=lb[:, :, :], in0=lb[:, :, :], scalar=0.5, in1=lt1[:, :, :],
                                                      op0=ALU.mult, op1=ALU.mult))
                        for i in range(2):
                            link(dve.tensor_tensor_scan(la[:, i, :], lt2[:, i, :], lb[:, i, :], 0.0, ALU.mult, ALU.add))
                        signal(dve.scalar_tensor_tensor(out=xb[:, :, :], in0=lgate[:, :, :], scalar=0.5, in1=la[:, :, :],
                                                        op0=ALU.mult, op1=ALU.mult), "lru_vec", lru_vec)
                        for tb in range(TB):
                            link(dve.tensor_tensor(yd[:, tb, :].rearrange("p (h d) -> p h d", h=SSD_H),
                                                   xtok[:, tb, :].rearrange("p (h d) -> p h d", h=SSD_H),
                                                   ssd_par[:, l, 2, :].unsqueeze(2).broadcast_to([P, SSD_H, HD]), ALU.mult))
                        for tb in range(TB):
                            b = filled()
                            take_bank(dve.tensor_tensor(yd[:, tb, :], yd[:, tb, :], b[:, 0:GW], ALU.add))
                        signal(dve.tensor_tensor(yd[:, :, :], yd[:, :, :], zs[:, :, :], ALU.mult), "ssd_vec", ssd_vec)
                    if n == 7:
                        b = filled()
                        take_bank(dve.tensor_scalar(lrstd[:, :], b[:, 0:S], EPS, None, ALU.add))
                        signal(dve.tensor_copy(hT_flag[:, 0:1], ones[:, 0:1]), "lru_vec", lru_vec)
                    if n == 9:
                        dve.wait_ge(lru_act, 5 * l + 5)
                        link(dve.reciprocal(lrstd[:, :], lrstd[:, :]))
                        for i in range(2):
                            link(dve.scalar_tensor_tensor(out=yT[:, 4 + i, :], in0=xb[:, i, :], scalar=pcol(l, "grp", 4 + i),
                                                          in1=lrstd[:, :], op0=ALU.mult, op1=ALU.mult))

                dve.wait_ge(rstd_ready, 5 * l + 3)
                r0 = 4 * (5 * l + 2)
                for tb in range(TB):
                    ins = dve.tensor_scalar(yn[:, 2, tb, :], yd[:, tb, :], rstd[:, r0 + tb:r0 + tb + 1], None,
                                            ALU.mult)
                    if tb == 0:
                        link(ins)
                    else:
                        signal(ins, "yn", yn_ready)
                dve.wait_ge(rstd_ready, 5 * l + 4)
                r0 = 4 * (5 * l + 3)
                for i, o in enumerate((oa, ob)):
                    for tb in range(TB):
                        ins = dve.tensor_scalar(yn[:, i, tb, :], o[:, tb, :],
                                                rstd[:, r0 + 2 * i + tb:r0 + 2 * i + tb + 1], None, ALU.mult)
                        if (i, tb) == (1, TB - 1):
                            signal(ins, "yn", yn_ready)
                        else:
                            link(ins)
                for grp in (3, 0, 1):
                    b = filled()
                    gain = par[:, l, PR["grp"] + 2 * grp:PR["grp"] + 2 * grp + 2].unsqueeze(2)\
                        .broadcast_to([P, 2, S])
                    take_bank(dve.tensor_tensor(yT[:, 2 * grp:2 * grp + 2, :],
                                                b[:, :].rearrange("p (k t) -> p k t", k=2), gain, ALU.mult))
                signal(dve.tensor_copy(hT_flag[:, 0:1], ones[:, 0:1]), "yT", yT_ready)
                for tb in range(TB):
                    for half in range(2):
                        b = filled()
                        r = xres[:, tb, half * 512:(half + 1) * 512]
                        take_bank(dve.tensor_tensor(r, r, b[:, :], ALU.add))
                signal(dve.tensor_copy(hT_flag[:, 0:1], ones[:, 0:1]), "res", res_ready)
                normed(2 * l + 1, 5 * l + 4)

                if l == 0:
                    dve.wait_ge(hT_hi_ready, 1)
                    dve.tensor_tensor(hT_lo[:, :, :], hT[:, :, :], hT_hi[:, :, :].bitcast(F32), ALU.subtract)\
                        .then_inc(hT_lo_ready, 1)
                    ffn(TB, 0, 0)
                    dve.wait_ge(units_used, FFN_SLOTS)
                    for tb in range(TB):
                        for half in range(2):
                            r = xres[:, tb, half * 512:(half + 1) * 512]
                            ins = dve.tensor_tensor(r, r, banks[4 + 2 * tb + half][:, :], ALU.add)
                            if (tb, half) == (1, 1):
                                signal(ins, "res", res_ready)
                            else:
                                link(ins)

            dve.wait_ge(route_logits, 1)
            link(dve.tensor_copy(logit[:, :, :], banks[0][:, 0:TB * NE].rearrange("p (t e) -> p t e", t=TB)))
            for tb in range(TB):
                link(dve.max(out=top[:, tb, :], in_=logit[:, tb, :]))
                link(dve.max_index(out=topi[:, tb, :], in_max=top[:, tb, :], in_values=logit[:, tb, :]))
            link(dve.tensor_copy(topf[:, :, :], topi[:, :, :]))
            signal(dve.tensor_tensor(topw[:, 0, :], top[:, :, 1], top[:, :, 0], ALU.subtract), "diff", route_diff)
            for i in range(2):
                for tb in range(TB):
                    link(dve.tensor_scalar(hot[:, i, tb, :], iota[:, 0:NE], topf[:, tb, i:i + 1], None,
                                           ALU.is_equal))
            signal(dve.tensor_tensor(sel[:, :, :], hot[:, 0, :, :], hot[:, 1, :, :], ALU.add), "sel", sel_ready)
            dve.wait_ge(route_exp, 1)
            link(dve.tensor_scalar(topw[:, 2, :], topw[:, 1, :], 1.0, None, ALU.add))
            link(dve.reciprocal(topw[:, 2, :], topw[:, 2, :]))
            link(dve.tensor_tensor(topw[:, 3, :], topw[:, 1, :], topw[:, 2, :], ALU.mult))
            for tb in range(TB):
                link(dve.tensor_scalar(gatew[:, tb, :], hot[:, 0, tb, :], topw[:, 2, tb:tb + 1], None, ALU.mult))
                link(dve.scalar_tensor_tensor(out=gatew[:, tb, :], in0=hot[:, 1, tb, :],
                                              scalar=topw[:, 3, tb:tb + 1], in1=gatew[:, tb, :], op0=ALU.mult,
                                              op1=ALU.add))
            dve.wait_ge(ranks_done, 1)
            link(dve.scalar_tensor_tensor(out=rank1[:, :, :],
                                          in0=banks[1][:, 0:TB * NE].rearrange("p (t e) -> p t e", t=TB), scalar=1.0,
                                          in1=sel[:, :, :], op0=ALU.add, op1=ALU.mult))
            link(dve.memset(rank[:, :, NE:JT], -1.0))
            link(dve.memset(jgate[:, :, NE:JT], 0.0))
            link(dve.tensor_scalar(rank[:, :, 0:NE], rank1[:, :, :], -1.0, None, ALU.add))
            link(dve.tensor_copy(jgate[:, :, 0:NE], gatew[:, :, :]))
            link(dve.tensor_scalar(ovf[:, :], banks[1][:, 2 * NE:3 * NE], float(P), None, ALU.is_gt))
            link(dve.tensor_tensor_scan(ovpos[:, :], ones[:, 0:NE], ovf[:, :], 0.0, ALU.mult, ALU.add))
            for o in range(3):
                link(dve.scalar_tensor_tensor(out=in_job[:, :], in0=ovpos[:, :], scalar=float(o + 1), in1=ovf[:, :],
                                              op0=ALU.is_equal, op1=ALU.mult))
                pickj = in_job[:, :].unsqueeze(1).broadcast_to([P, TB, NE])
                for src, dst in ((rank1, rank), (gatew, jgate)):
                    link(dve.tensor_tensor(prod8[:, :, :], src[:, :, :], pickj, ALU.mult))
                    link(dve.tensor_reduce(dst[:, :, NE + o:NE + o + 1], prod8[:, :, :], AX.X, ALU.add))
                link(dve.tensor_scalar(rank[:, :, NE + o:NE + o + 1], rank[:, :, NE + o:NE + o + 1], -1.0 - P, None,
                                       ALU.add))
                link(dve.tensor_tensor(prod8[:, 0, :], in_job[:, :], iota[:, 0:NE], ALU.mult))
                link(dve.tensor_reduce(steer_f[:, o:o + 1], prod8[:, 0, :], AX.X, ALU.add))
            link(dve.tensor_reduce(steer_f[:, 3:4], ovf[:, :], AX.X, ALU.add))
            signal(dve.tensor_copy(steer[0:1, :], steer_f[0:1, :]), "steer", steer_ready)

            def picks(j):
                for tb in range(TB):
                    dve.tensor_scalar(pick[:, tb, :], iota[:, :], rank[:, tb, bass.ds(j, 1)], None, ALU.is_equal)
                    ins = dve.tensor_scalar(pickw[:, tb, :], iota[:, :], rank[:, tb, bass.ds(j, 1)],
                                            jgate[:, tb, bass.ds(j, 1)], ALU.is_equal, ALU.mult)
                ins.then_inc(pick_ready, 1)

            def gathered(jobs_before):
                dve.wait_ge(xg_done, jobs_before + 1)
                for i in range(2):
                    gain = par[:, 1, PR["ffn"] + 4 * i:PR["ffn"] + 4 * i + 4].unsqueeze(2).broadcast_to([P, 4, P])
                    ins = dve.tensor_tensor(xg[:, 4 * i:4 * i + 4, :],
                                            banks[6 + i][:, :].rearrange("p (d t) -> p d t", d=4), gain, ALU.mult)
                ins.then_inc(xg_ready, 1)

            def split_tokens(jobs_before):
                dve.wait_ge(xT_hi_ready, jobs_before + 1)
                dve.tensor_tensor(xT_lo[:, :, :], xg[:, :, :], xT_hi[:, :, :].bitcast(F32), ALU.subtract)\
                    .then_inc(xT_lo_ready, 1)

            def add_combined(tb, b0, blocks_before):
                dve.wait_ge(comb_done, blocks_before + 1)
                for half in range(2):
                    r = xres[:, tb, half * 512:(half + 1) * 512]
                    ins = dve.tensor_tensor(r, r, banks[b0 + half][:, :], ALU.add)
                ins.then_inc(comb_took, 1)

            link(dve.memset(ysb[:, :], 0.0))
            dve.memset(pickT[:, :, :], 0.0).then_inc(pickT_ready, 1)
            picks(0)
            gathered(0)
            split_tokens(0)

            def job(j, u0, s0):
                def more(c):
                    if c < TB:
                        add_combined(c, 6, 2 * j + c)
                    if c == 2:
                        dve.wait_ge(pickT_done, j + 1)
                        dve.tensor_copy(pickT[:, :, :], banks[6][:, 0:TB * P].rearrange("p (t s) -> p t s", t=TB))\
                            .then_inc(pickT_ready, 1)
                    if c == 3:
                        picks(j + 1)
                    if c == 5:
                        gathered(j + 1)

                ffn(1, u0, s0, more)
                split_tokens(j + 1)

            with dve.Fori(0, NE) as e:
                job(e, e * FFN_SLOTS + FFN_SLOTS, e * NCH + DENSE)
            novf_r = dve.value_load(steer[0:1, 3:4], min_val=0, max_val=3)
            with dve.Fori(0, 3) as o:
                with dve.If(novf_r > o):
                    job(o + NE, o * FFN_SLOTS + (NE + 1) * FFN_SLOTS, o * NCH + (DENSE + NE * NCH))
            for tb in range(TB):
                add_combined(tb, 4 + 2 * tb, novf_r * 2 + (2 * NE + tb))

            dve.wait_ge(comb_took, novf_r * 2 + (2 * NE + 2))
            for tb in range(TB):
                dve.tensor_tensor_reduce(hn[:, tb, :], xres[:, tb, :], xres[:, tb, :], 1.0 / D, 0.0, ALU.mult,
                                         ALU.add, stat[:, 40 + tb:41 + tb]).then_inc(ms_ready, 1)
            dve.wait_ge(rstd_ready, 5 * L + 1)
            for tb in range(TB):
                dve.scalar_tensor_tensor(out=hn[:, tb, :], in0=xres[:, tb, :], scalar=rstd[:, 40 + tb:41 + tb],
                                         in1=gfin[:, :], op0=ALU.mult, op1=ALU.mult).then_inc(out_ready, 1)


_INS = ['x', 'positions', 'norm_mix', 'w_in', 'mla_q_norm', 'mla_w_uq', 'mla_kv_norm', 'mla_w_ukv', 'nsa_cmp_pe',
        'nsa_w_cmp', 'lru_conv_w', 'lru_conv_b', 'lru_w_gate', 'lru_b_gate', 'lru_lambda', 'ssd_conv_w',
        'ssd_conv_b', 'ssd_dt_bias', 'ssd_a_log', 'ssd_d', 'group_norm', 'w_out', 'norm_ffn', 'ffn_w_gate',
        'ffn_w_up', 'ffn_w_down', 'moe_router', 'moe_w_gate', 'moe_w_up', 'moe_w_down', 'norm_final']


def kernel(**inputs):
    import concourse.bacc as bacc
    from concourse.bass_utils import run_bass_kernel_spmd

    nc = bacc.Bacc("TRN2", target_bir_lowering=False, num_devices=1)
    arrays, args = {}, []
    for name in _INS:
        a = np.ascontiguousarray(inputs[name])
        arrays[f"in_{name}_dram"] = a
        args.append(nc.dram_tensor(f"in_{name}_dram", a.shape, mybir.dt.from_np(a.dtype), kind="ExternalInput").ap())
    out = nc.dram_tensor("out_dram", inputs["x"].shape, F32, kind="ExternalOutput").ap()
    trunk(nc, *args, out)
    r = run_bass_kernel_spmd(nc, [arrays], core_ids=[0])
    return r.results[0]["out_dram"]
```

```python
from contextlib import ExitStack

import numpy as np

import concourse.bass as bass
from concourse import mybir

F32 = mybir.dt.float32
F32R = mybir.dt.float32r
I32 = mybir.dt.int32
U32 = mybir.dt.uint32
ALU = mybir.AluOpType
ACT = mybir.ActivationFunctionType
AX = mybir.AxisListType

P = 128
ROPE_THETA = 500000.0
EPS = 1e-6
NEG = -1e30
MLA_H, NOPE, ROPE, QR, KVR = 4, 64, 32, 192, 128
QK = NOPE + ROPE
HD, NROT, NH = 64, 16, 4
CSTRIDE, CLEN = 16, 32
SSD_H, SSD_G = 4, 2
GW = 256
RING = 7
SLOT = 2048
FC = 512
SPLIT = 3
W_OUT_ORDER = (2, 3, 0, 1)


def trunk(nc, x, positions, norm_mix, w_in, mla_q_norm, mla_w_uq, mla_kv_norm, mla_w_ukv, nsa_cmp_pe,
          nsa_w_cmp, lru_conv_w, lru_conv_b, lru_w_gate, lru_b_gate, lru_lambda, ssd_conv_w, ssd_conv_b,
          ssd_dt_bias, ssd_a_log, ssd_d, group_norm, w_out, norm_ffn, ffn_w_gate, ffn_w_up, ffn_w_down,
          moe_router, moe_w_gate, moe_w_up, moe_w_down, norm_final, out):
    D = x.shape[2]
    S = x.shape[1]
    L = norm_mix.shape[0]
    TB = S // P
    KT = D // P
    FF = ffn_w_gate.shape[2]
    NCH = FF // FC
    FT = FC // P
    NE = moe_w_gate.shape[1]
    NC = S // CSTRIDE - 1
    O_NSA = QR + KVR + ROPE
    O_LRU = O_NSA + NH * HD + 6 * HD + 3 * NH
    O_SSD = O_LRU + 2 * GW
    O_XBC = O_SSD + GW
    O_DT = O_XBC + 3 * GW
    IN = O_DT + SSD_H
    assert L == 2 and TB == 2 and KT == 8 and FF % FC == 0 and w_in.shape[2] == IN
    assert S // 64 <= 16 and S <= 512
    UA = 512
    UB = O_LRU - UA
    UT = O_LRU + SSD_H
    MIX_SLOTS, FFN_SLOTS = 14, 6 * NCH
    assert MIX_SLOTS % RING == 0 and FFN_SLOTS % RING == 0
    BASE_MIX = [0, MIX_SLOTS + FFN_SLOTS]
    BASE_FFN = [MIX_SLOTS, 2 * MIX_SLOTS + FFN_SLOTS]
    JOBS = NE + 3
    JT = JOBS + 1

    ctx = ExitStack()
    with ctx:
        def sb(name, shape, dt=F32):
            return ctx.enter_context(nc.sbuf_tensor(name, shape, dt))

        def sem(name):
            return ctx.enter_context(nc.semaphore(name))

        ring = sb("ring", [P, RING, SLOT])
        ident = sb("ident", [P, P])
        upper = sb("upper", [P, P])
        strict = sb("strict", [P, P])
        ones = sb("ones", [P, P])
        cbias = sb("cbias", [P, 2 * P])
        cmask = sb("cmask", [P, TB, NC])
        cmbias = sb("cmbias", [P, TB, NC])
        iota = sb("iota", [P, P])
        minus_half = sb("minus_half", [P, 4])
        prow = sb("prow", [P, L, P])
        par = sb("par", [P, L, P])
        w_uq = sb("w_uq", [96, 2, 384])
        w_ukv = sb("w_ukv", [P, 512])
        w_cmp = sb("w_cmp", [P, CLEN, HD])
        pe_row = sb("pe_row", [CLEN, L, P])
        pe_t = sb("pe_t", [P, L, CLEN])
        lru_w = sb("lru_w", [P, L, 2, 2, P])
        ssd_par = sb("ssd_par", [P, L, 3, SSD_H])
        neg_a = sb("neg_a", [P, L, SSD_H])
        lru_c = sb("lru_c", [P, L, 4])
        lru_t = sb("lru_t", [P, L, 6, 2])
        half_b = sb("half_b", [P, L, 4])
        router = sb("router", [P, KT, NE])
        gfin = sb("gfin", [P, D])
        pos_i = sb("pos_i", [P, TB], I32)
        pos_f = sb("pos_f", [P, TB])
        inv = sb("inv", [P, 16])
        ang = sb("ang", [P, TB, 16])
        rk = sb("rk", [P, 2, TB, 16])
        rr = sb("rr", [P, 2, TB, 16])
        trig = sb("trig", [P, 2, TB, 16])
        xres = sb("xres", [P, TB, D])
        hn = sb("hn", [P, TB, D])
        hT = sb("hT", [P, KT, S])
        stat = sb("stat", [P, 44])
        rstd = sb("rstd", [P, 44])
        flag = sb("flag", [P, 1])
        WORK = 24832
        work_at = -(-nc.sbuf_base // 32) * 32
        work = sb("work", [P, WORK])
        used = [0]

        def take(*shape):
            n = int(np.prod(shape))
            at = used[0]
            used[0] += n
            assert used[0] <= WORK, used
            v = work[:, at:at + n]
            if len(shape) > 1:
                names = " ".join("abcd"[:len(shape)])
                v = v.rearrange(f"p ({names}) -> p {names}", **dict(zip("bcd", shape[1:])))
            return v

        lraw = take(4, 3 + S)
        yd = work[:, 0:TB * GW].rearrange("p (t c) -> p t c", t=TB)
        xraw = take(6, 3 + S)
        yn = work[:, used[0] - 6 * (3 + S):used[0] - 6 * (3 + S) + 3 * TB * GW]\
            .rearrange("p (i t c) -> p i t c", i=3, t=TB)
        ffn_scratch = used[0]

        def parts(name, *shape):
            used[0] += -used[0] % 8
            t = nc.alloc_sbuf_tensor_at(name, [P] + list(shape), F32R, offset=work_at + 4 * used[0])
            used[0] += int(np.prod(shape))
            assert used[0] <= WORK, used
            return t

        sgate = take(2, FC)
        hid = take(2, FC)
        split_at = used[0]
        w_hi = parts("w_hi", SPLIT, SLOT)
        w_lo = parts("w_lo", SPLIT, SLOT)
        split_end = used[0]
        hidT_hi = parts("hidT_hi", 2, FT * P)
        hidT_lo = parts("hidT_lo", 2, FT * P)
        in_scratch = used[0]
        hT_hi = parts("hT_hi", KT, S)
        hT_lo = parts("hT_lo", KT, S)
        yT_hi, yT_lo = hT_hi, hT_lo
        dense_end = used[0]
        used[0] = ffn_scratch
        utok = take(TB, UT)
        assert used[0] <= split_at
        used[0] = split_at
        cqT = take(2, S)
        ckvT = take(S)
        qtok = take(TB, MLA_H, QK)
        kcat = take(TB, MLA_H, QK)
        vtok = take(TB, MLA_H, HD)
        qT = take(MLA_H, S)
        kT = take(MLA_H, S)
        nqT = take(NH, S)
        kvcT = take(S)
        ksT = take(S)
        kwT = take(S)
        cin = take(CLEN, NC)
        kcT = take(NC)
        vc = take(HD)
        xb = take(2, S)
        xbc = take(6, S)
        xtok = take(TB, GW)
        xdt = take(TB, GW)
        nacs = take(TB, SSD_H)
        conv_at = used[0]
        dec0 = take(SSD_H, S)
        dec1 = take(SSD_H, P)
        assert used[0] <= split_end
        used[0] = split_end
        junk = take(2, 256)
        cqn = take(TB, QR)
        ckvn = take(TB, KVR)
        rt = take(4, TB * 4 * 16)
        gates = take(TB, 3 * NH)
        dts = take(6, TB, SSD_H)
        ot = take(GW)
        assert used[0] <= in_scratch
        used[0] = in_scratch
        prob = take(2, 4, S)
        probT = take(2, 8 * P)
        assert used[0] <= dense_end
        used[0] = dense_end
        zs = take(TB, GW)
        oa = take(TB, GW)
        ob = take(TB, GW)
        rmin = take(8, 4)
        rsum = take(8, 4)
        coef = take(8, 4)
        lth = hn[:, 0, :].rearrange("p (i t) -> p i t", i=4)
        lt1, lt2 = (hn[:, 1, i * 2 * S:(i + 1) * 2 * S].rearrange("p (i t) -> p i t", i=2) for i in range(2))
        lrstd = lt2[:, 0, :]
        la, ld, lb, lgate = (hT[:, 2 * i:2 * i + 2, :] for i in range(4))
        yT = hT
        used[0] = in_scratch
        xT_hi = parts("xT_hi", KT, P)
        xT_lo = parts("xT_lo", KT, P)
        xg = take(KT, P)
        ysb = take(D)
        assert used[0] <= dense_end
        used[0] = dense_end
        pick = take(TB, P)
        pickw = take(TB, P)
        pickT = take(TB, P)
        logit = take(TB, NE)
        top = take(TB, 8)
        topf = take(TB, 8)
        topw = take(4, TB)
        hot = take(2, TB, NE)
        sel = take(TB, NE)
        gatew = take(TB, NE)
        rank1 = take(TB, NE)
        rank = take(TB, JT)
        jgate = take(TB, JT)
        cnt = take(NE)
        ovf = take(NE)
        ovpos = take(NE)
        in_job = take(NE)
        prod8 = take(TB, NE)
        steer_f = take(4)
        topi = sb("topi", [P, TB, 8], U32)
        steer = sb("steer", [1, 4], I32)

        banks = [ctx.enter_context(nc.psum_tensor(f"bank{i}", [P, 512], F32)) for i in range(8)]

        slot_full = [sem(f"slot_full{i}") for i in range(RING)]
        x_in, prow_in, mixw_in, misc_in = sem("x_in"), sem("prow_in"), sem("mixw_in"), sem("misc_in")
        pos_in, prow_zero, lru_w_zero = sem("pos_in"), sem("prow_zero"), sem("lru_w_zero")
        consts_ready, inv_ready = sem("consts_ready"), sem("inv_ready")
        pool_chain, dve_chain, act_chain = sem("pool_chain"), sem("dve_chain"), sem("act_chain")
        for_dve, dve_took = sem("for_dve"), sem("dve_took")
        for_act, act_took = sem("for_act"), sem("act_took")
        lam_args, lam_logs, half_b_ready = sem("lam_args"), sem("lam_logs"), sem("half_b_ready")
        rope_args, trig_ready = sem("rope_args"), sem("trig_ready")
        ms_ready, rstd_ready = sem("ms_ready"), sem("rstd_ready")
        hn_ready, proj_done, res_ready = sem("hn_ready"), sem("proj_done"), sem("res_ready")
        yT_hi_ready, yT_lo_ready = sem("yT_hi_ready"), sem("yT_lo_ready")
        cn_ready, cT_ready = sem("cn_ready"), sem("cT_ready")
        qk_roped, nsa_roped, cin_ready, gate_th = sem("qk_roped"), sem("nsa_roped"), sem("cin_ready"), sem("gate_th")
        cmp_ready, exp_ready, masked = sem("cmp_ready"), sem("exp_ready"), sem("masked")
        o_ready, yn_ready, yT_ready = sem("o_ready"), sem("yn_ready"), sem("yT_ready")
        lru_conv, ssd_conv = sem("lru_conv"), sem("ssd_conv")
        lru_vec, lru_act, ssd_vec, ssd_act = sem("lru_vec"), sem("lru_act"), sem("ssd_vec"), sem("ssd_act")
        dec_ready = sem("dec_ready")
        hi_ready, lo_ready, units_used = sem("hi_ready"), sem("lo_ready"), sem("units_used")
        hT_hi_ready, hT_lo_ready = sem("hT_hi_ready"), sem("hT_lo_ready")
        silu_done, hid_ready, hidT_done = sem("silu_done"), sem("hid_ready"), sem("hidT_done")
        hidT_hi_ready, hidT_lo_ready = sem("hidT_hi_ready"), sem("hidT_lo_ready")
        route_logits, route_diff, route_exp = sem("route_logits"), sem("route_diff"), sem("route_exp")
        sel_ready, ranks_done, steer_ready = sem("sel_ready"), sem("ranks_done"), sem("steer_ready")
        pick_ready, pickT_done, pickT_ready = sem("pick_ready"), sem("pickT_done"), sem("pickT_ready")
        xg_done, xg_ready = sem("xg_done"), sem("xg_ready")
        xT_hi_ready, xT_lo_ready = sem("xT_hi_ready"), sem("xT_lo_ready")
        zero_sums, y_ready = sem("zero_sums"), sem("y_ready")
        comb_done, comb_took = sem("comb_done"), sem("comb_took")
        out_ready, out_stored = sem("out_ready"), sem("out_stored")

        PR, n = {}, 0
        for name, rows in (("mix", 8), ("ffn", 8), ("grp", 8), ("lcw", 8), ("lcb", 2), ("lbg", 4), ("lam", 2),
                           ("scw", 24), ("scb", 6), ("kvn", 1), ("qn", 2)):
            PR[name] = n
            n += rows
        assert n <= P
        N_PROW = 12
        N_MISC = 3 + 2 + 2

        def pcol(l, name, i=0, rows=P):
            return par[0:rows, l, PR[name] + i:PR[name] + i + 1]

        def slot(p):
            return ring[:, p % RING, :]

        def slot_k(p):
            return slot(p).rearrange("p (k n) -> p k n", k=4)

        def slot_r(p):
            return slot(p).rearrange("p (k n) -> p k n", k=2)

        AJ = [(br, tb) for br in ("mla", "sel", "win", "cmp") for tb in range(TB)]
        KV0 = O_NSA + NH * HD
        FFN_ORDER = []
        for c in range(NCH + 1):
            if c < NCH:
                FFN_ORDER += [("gate", c), ("up", c)]
            if c >= 1:
                FFN_ORDER += [("down", c - 1)]
        AT = {key: 2 * i for i, key in enumerate(FFN_ORDER)}
        assert 2 * len(FFN_ORDER) == FFN_SLOTS
        DENSE = NCH * TB
        assert FFN_SLOTS % SPLIT == 0
        def at_gate(c, h):
            return AT["gate", c] + h

        def at_up(c, h):
            return AT["up", c] + h

        def at_down(c, h):
            return AT["down", c] + h

        filled_by = [[], []]
        mark = {}

        block = ctx.enter_context(nc.Block())

        @block.tensor
        def _(pe):
            gave = [0, 0]

            def bank(who):
                k = gave[who]
                gave[who] += 1
                if k >= 4:
                    pe.wait_ge((dve_took, act_took)[who], k - 3)
                return banks[4 * who + k % 4]

            given = [0, 0]

            def give(mm, who):
                given[who] += 1
                s = (for_dve, for_act)[who]
                filled_by[who].append((s, given[who]))
                mm.then_inc(s, 1)

            def turn_normed(norm):
                b = [bank(0) for _ in range(4)]
                for tb in range(TB):
                    pe.wait_ge(hn_ready, TB * norm + tb + 1)
                    for g in range(4):
                        for k in range(2):
                            mm = pe.transpose(b[g][:, (2 * k + tb) * P:(2 * k + tb + 1) * P],
                                              hn[:, tb, (2 * g + k) * P:(2 * g + k + 1) * P], ident[:, :])
                        if tb == TB - 1:
                            give(mm, 0)
                            mark["turned", norm, g] = gave[0] - 3 + g

            pe.wait_ge(consts_ready, 1)
            pe.wait_ge(prow_in, 16 * N_PROW)
            b = bank(0)
            for l in range(L):
                pe.transpose(b[:, l * P:(l + 1) * P], prow[:, l, :], ident[:, :])
            for l in range(L):
                mm = pe.transpose(b[:, 2 * P + l * CLEN:2 * P + (l + 1) * CLEN], pe_row[:, l, :],
                                  ident[0:CLEN, 0:CLEN])
            give(mm, 0)

            def products3(o, x_hi, x_lo, w, start, stop, low):
                if low:
                    return pe.matmul(o, x_hi, w, start=False, stop=stop)
                pe.matmul(o, x_hi, w, start=start, stop=False)
                return pe.matmul(o, x_lo, w, start=False, stop=False)

            def parts_of(u0, base, at, low):
                if low:
                    pe.wait_ge(lo_ready, u0 + (at + 1))
                else:
                    pe.wait_ge(hi_ready, u0 + (at + 1))
                return (w_lo if low else w_hi)[:, (base + at) % SPLIT, :]

            def ffn(n, base, x_hi, x_lo, u0, s0, more=None):
                def project(bank0, c, h, at):
                    if n == TB and bank0 == 0 and c == 0:
                        pe.wait_ge(hT_lo_ready, 4 + 2 * h + 2)
                    for low in (False, True):
                        w = parts_of(u0, base, at, low).rearrange("p (k n) -> p k n", k=4)
                        for i in range(n):
                            for k in range(4):
                                t = slice(i * P, (i + 1) * P)
                                mm = products3(banks[bank0 + (c * n + i) % 2][:, :], x_hi[:, 4 * h + k, t],
                                               x_lo[:, 4 * h + k, t], w[:, k, :], h == 0 and k == 0,
                                               h == 1 and k == 3, low)
                    mm.then_inc(units_used, 1)

                def down(c, h):
                    if h == 0:
                        pe.wait_ge(hidT_lo_ready, s0 + n * (c + 1))
                    last = c == NCH - 1 and h == 1
                    order = [(i, low) for i in range(n) for low in (False, True)] if last else \
                        [(i, low) for low in (False, True) for i in range(n)]
                    for i, low in order:
                        w = parts_of(u0, base, at_down(c, h), low).rearrange("p (f n) -> p f n", f=2)
                        v = (c * n + i) % 2
                        for half in range(2):
                            for f in range(2):
                                t = slice((2 * h + f) * P, (2 * h + f + 1) * P)
                                mm = products3(banks[4 + 2 * i + half][:, :], hidT_hi[:, v, t],
                                               hidT_lo[:, v, t], w[:, f, half * 512:(half + 1) * 512],
                                               c == 0 and h == 0 and f == 0, last and f == 1, low)
                        if last and low and i < n - 1:
                            mm.then_inc(proj_done, 1)
                    mm.then_inc(units_used, 1)

                def turn_hid(c):
                    for i in range(n):
                        v = (c * n + i) % 2
                        pe.wait_ge(hid_ready, s0 + (c * n + i + 1))
                        for f in range(FT):
                            mm = pe.transpose(banks[2 + v][:, f * P:(f + 1) * P], hid[:, v, f * P:(f + 1) * P],
                                              ident[:, :])
                        mm.then_inc(hidT_done, 1)

                for c in range(NCH):
                    if n == TB and c >= 1:
                        pe.wait_ge(silu_done, s0 + n * c)
                    project(0, c, 0, at_gate(c, 0))
                    if c >= 1:
                        turn_hid(c - 1)
                    project(0, c, 1, at_gate(c, 1))
                    if n == TB and c >= 1:
                        pe.wait_ge(hidT_lo_ready, s0 + n * c)
                    elif n == 1:
                        pe.wait_ge(hidT_lo_ready, s0 + max(c - 1, 0))
                    project(2, c, 0, at_up(c, 0))
                    project(2, c, 1, at_up(c, 1))
                    if more is not None:
                        more(c)
                    if c >= 1:
                        down(c - 1, 0)
                        if c == NCH - 1 and n == 1:
                            turn_hid(c)
                        down(c - 1, 1)
                if n > 1:
                    turn_hid(NCH - 1)
                down(NCH - 1, 0)
                down(NCH - 1, 1)

            for l in range(L):
                turn_normed(2 * l)
                p = BASE_MIX[l]

                def by_token(p, n, first):
                    b = [bank(1), bank(1)]
                    for h in range(2):
                        if first:
                            pe.wait_ge(hT_lo_ready, 8 * l + 2 * h + 2)
                        for low in (False, True):
                            w = parts_of(p, p, h, low).rearrange("p (k n) -> p k n", k=4)
                            for tb in range(TB):
                                t = slice(tb * P, (tb + 1) * P)
                                for k in range(4):
                                    mm = products3(b[tb][:, 0:n], hT_hi[:, 4 * h + k, t], hT_lo[:, 4 * h + k, t],
                                                   w[:, k, 0:n], h == 0 and k == 0, h == 1 and k == 3, low)
                                if h == 1 and low and tb == 0:
                                    give(mm, 1)
                        mm.then_inc(units_used, 1)
                    filled_by[1].append((units_used, p + 2))

                def by_channel(p, who, z=False):
                    b = [bank(who) for _ in range(4)]
                    for h in range(2):
                        for low in (False, True):
                            w = parts_of(p, p, h, low).rearrange("p (k n) -> p k n", k=4)
                            for i in range(4):
                                for k in range(4):
                                    start, stop = h == 0 and k == 0, h == 1 and k == 3
                                    if z and i >= 2:
                                        t = slice((i - 2) * P, (i - 1) * P)
                                        mm = products3(b[i][:, 0:GW], hT_hi[:, 4 * h + k, t], hT_lo[:, 4 * h + k, t],
                                                       w[:, k, GW:2 * GW], start, stop, low)
                                        continue
                                    wk = w[:, k, i * P:(i + 1) * P]
                                    mm = pe.matmul(b[i][:, 0:S], wk, hT_hi[:, 4 * h + k, :],
                                                   start=start and not low, stop=stop and low)
                                    if not low:
                                        pe.matmul(b[i][:, 0:S], wk, hT_lo[:, 4 * h + k, :], start=False, stop=False)
                                if h == 1 and low and i < 3:
                                    give(mm, who)
                        mm.then_inc(units_used, 1)
                    filled_by[who].append((units_used, p + 2))

                by_token(p, UA, True)
                by_token(p + 2, UB + SSD_H, False)
                mark["u", l] = gave[1]
                by_channel(p + 4, 0)
                by_channel(p + 6, 1)
                mark["D", l] = gave[1]
                by_channel(p + 8, 0, z=True)
                mark["E", l] = gave[0]
                p += 10

                pe.wait_ge(cn_ready, l + 1)
                b = bank(0)
                for i in range(2):
                    for tb in range(TB):
                        mm = pe.transpose(b[0:96, (2 * i + tb) * P:(2 * i + tb + 1) * P],
                                          cqn[:, tb, i * 96:(i + 1) * 96], ident[:, :])
                give(mm, 0)
                b = bank(0)
                for tb in range(TB):
                    mm = pe.transpose(b[:, tb * P:(tb + 1) * P], ckvn[:, tb, :], ident[:, :])
                give(mm, 0)
                pe.wait_ge(cT_ready, l + 1)
                pe.wait_ge(mixw_in, 64 * (l + 1))
                for tb in range(TB):
                    b = bank(1)
                    for i in range(2):
                        mm = pe.matmul(b[:, 0:384], cqT[0:96, i, tb * P:(tb + 1) * P], w_uq[:, i, :],
                                       start=(i == 0), stop=(i == 1))
                    give(mm, 1)
                    b = bank(1)
                    give(pe.matmul(b[:, :], ckvT[:, tb * P:(tb + 1) * P], w_ukv[:, :], start=True, stop=True), 1)
                mark["qkv", l] = gave[1]

                pe.wait_ge(nsa_roped, l + 1)
                for hp in range(2):
                    b = bank(1)
                    for i in range(2):
                        c0 = O_NSA + (2 * hp + i) * HD
                        for tb in range(TB):
                            mm = pe.transpose(b[0:HD, (2 * i + tb) * P:(2 * i + tb + 1) * P],
                                              utok[:, tb, c0:c0 + HD], ident[:, :])
                    give(mm, 1)
                b = bank(1)
                for tb in range(TB):
                    pe.transpose(b[:, tb * P:(tb + 1) * P], utok[:, tb, KV0:KV0 + 2 * HD], ident[:, :])
                for tb in range(TB):
                    mm = pe.transpose(b[0:HD, S + tb * P:S + (tb + 1) * P],
                                      utok[:, tb, KV0 + 2 * HD:KV0 + 3 * HD], ident[:, :])
                give(mm, 1)
                b = bank(1)
                for tb in range(TB):
                    mm = pe.transpose(b[0:HD, tb * P:(tb + 1) * P],
                                      utok[:, tb, KV0 + 4 * HD:KV0 + 5 * HD], ident[:, :])
                give(mm, 1)
                mark["nsa", l] = gave[1]
                pe.wait_ge(qk_roped, l + 1)
                for src in (qtok, kcat):
                    for hp in range(2):
                        b = bank(1)
                        for i in range(2):
                            for tb in range(TB):
                                mm = pe.transpose(b[0:QK, (2 * i + tb) * P:(2 * i + tb + 1) * P],
                                                  src[:, tb, 2 * hp + i, :], ident[:, :])
                        give(mm, 1)
                pe.wait_ge(act_took, gave[1])

                def scores(n):
                    br, tb = AJ[n]
                    t0, t1 = tb * P, (tb + 1) * P
                    nk = NC if br == "cmp" else t1
                    if br == "cmp":
                        pe.wait_ge(cmp_ready, 2 * l + 1)
                    per = 4 if br == "cmp" else 512 // nk
                    for g in range(4 // per):
                        b = bank(0)
                        for i in range(per):
                            h = g * per + i
                            q, k = {"mla": (qT[0:QK, h, t0:t1], kT[0:QK, h, 0:nk]),
                                    "cmp": (nqT[0:HD, h, t0:t1], kcT[0:HD, :]),
                                    "sel": (nqT[0:HD, h, t0:t1], ksT[0:HD, 0:nk]),
                                    "win": (nqT[0:HD, h, t0:t1], kwT[0:HD, 0:nk])}[br]
                            mm = pe.matmul(b[:, i * nk:(i + 1) * nk], q, k, start=True, stop=True)
                        give(mm, 0)
                    mark["scores", l, n] = gave[0]

                def turn_probs(n):
                    br, tb = AJ[n]
                    pe.wait_ge(exp_ready, 8 * l + n + 1)
                    nb = 1 if br == "cmp" else tb + 1
                    if br == "cmp":
                        pe.wait_ge(masked, 2 * l + tb + 1)
                    rows = NC if br == "cmp" else P
                    for g in range(nb):
                        b = bank(1)
                        for i in range(4):
                            h, kb = divmod(4 * g + i, nb)
                            mm = pe.transpose(b[0:rows, i * P:(i + 1) * P],
                                              prob[:, n % 2, h, kb * P:kb * P + rows], ident[:, :])
                        give(mm, 1)
                    mark["probT", l, n] = gave[1]

                def products(n):
                    br, tb = AJ[n]
                    if br == "cmp":
                        pe.wait_ge(cmp_ready, 2 * l + 2)
                    pe.wait_ge(act_took, mark["probT", l, n])
                    b = bank(0)
                    nb = 1 if br == "cmp" else tb + 1
                    for h in range(4):
                        for kb in range(nb):
                            i = h * nb + kb
                            rows = NC if br == "cmp" else P
                            v = {"mla": vtok[:, kb, h, :], "cmp": vc[0:NC, :],
                                 "sel": utok[:, kb, KV0 + 3 * HD:KV0 + 4 * HD],
                                 "win": utok[:, kb, KV0 + 5 * HD:KV0 + 6 * HD]}[br]
                            mm = pe.matmul(b[:, h * HD:(h + 1) * HD], probT[0:rows, n % 2, i * P:(i + 1) * P], v,
                                           start=(kb == 0), stop=(kb == nb - 1))
                    give(mm, 0)
                    mark["pv", l, n] = gave[0]

                def compressed_keys():
                    pe.wait_ge(cin_ready, l + 1)
                    b = bank(0)
                    for j in range(CLEN):
                        mm = pe.matmul(b[0:HD, 0:NC], w_cmp[0:HD, j, :], cin[0:HD, j, :], start=(j == 0),
                                       stop=(j == CLEN - 1))
                    give(mm, 0)

                def compressed_values():
                    b = bank(0)
                    for j in range(CLEN):
                        mm = pe.matmul(b[0:NC, 0:HD], cin[HD:P, j, :], w_cmp[HD:P, j, :], start=(j == 0),
                                       stop=(j == CLEN - 1))
                    give(mm, 0)
                    mark["cmp", l] = gave[0]

                def lru_gates():
                    pe.wait_ge(lru_conv, l + 1)
                    pe.wait_ge(misc_in, 16 * N_MISC)
                    for g in range(2):
                        b = bank(1)
                        for i in range(2):
                            mm = pe.matmul(b[:, i * S:(i + 1) * S], lru_w[:, l, g, i, :], xb[:, i, :], start=True,
                                           stop=True)
                        give(mm, 1)
                    mark["lgate", l] = gave[1]

                def ssd_sums():
                    pe.wait_ge(ssd_act, 3 * l + 2)
                    b = bank(0)
                    for tb in range(TB):
                        for i in range(2):
                            mm = pe.transpose(b[:, tb * GW + i * P:tb * GW + (i + 1) * P],
                                              xbc[:, i, tb * P:(tb + 1) * P], ident[:, :])
                    give(mm, 0)
                    pe.wait_ge(ssd_vec, 4 * l + 2)
                    b = bank(0)
                    pe.matmul(b[:, 0:SSD_H], upper[:, :], dts[:, 5, 0, :], start=True, stop=True)
                    pe.matmul(b[:, SSD_H:2 * SSD_H], ones[:, :], dts[:, 5, 0, :], start=True, stop=False)
                    give(pe.matmul(b[:, SSD_H:2 * SSD_H], upper[:, :], dts[:, 5, 1, :], start=False, stop=True), 0)
                    for hp in range(2):
                        b = bank(0)
                        for i in range(2):
                            h = 2 * hp + i
                            da = [dts[:, 5, tb, h:h + 1].broadcast_to([P, P]) for tb in range(TB)]
                            pe.matmul(b[:, i * S:i * S + P], da[0], upper[:, :], start=True, stop=True)
                            pe.matmul(b[:, i * S + P:(i + 1) * S], da[0], ones[:, :], start=True, stop=False)
                            mm = pe.matmul(b[:, i * S + P:(i + 1) * S], da[1], upper[:, :], start=False, stop=True)
                        give(mm, 0)

                def ssd_cb():
                    for sb_ in range(TB):
                        b = bank(0)
                        n = S - sb_ * P
                        for g in range(SSD_G):
                            mm = pe.matmul(b[:, g * n:(g + 1) * n], xbc[:, 2 + g, sb_ * P:(sb_ + 1) * P],
                                           xbc[:, 4 + g, sb_ * P:S], start=True, stop=True)
                        give(mm, 0)

                def ssd_products():
                    pe.wait_ge(dec_ready, l + 1)
                    for tb in range(TB):
                        b = bank(0)
                        for h in range(SSD_H):
                            o = b[:, h * HD:(h + 1) * HD]
                            mm = pe.matmul(o, dec0[:, h, tb * P:(tb + 1) * P], xdt[:, 0, h * HD:(h + 1) * HD],
                                           start=True, stop=(tb == 0))
                            if tb == 1:
                                mm = pe.matmul(o, dec1[:, h, :], xdt[:, 1, h * HD:(h + 1) * HD], start=False, stop=True)
                        give(mm, 0)

                def lru_square():
                    pe.wait_ge(lru_act, 5 * l + 4)
                    b = bank(0)
                    for i in range(2):
                        mm = pe.matmul(b[:, 0:S], ones[:, :], lt1[:, i, :], start=(i == 0), stop=(i == 1))
                    give(mm, 0)

                for n in range(len(AJ) + 2):
                    if n < len(AJ):
                        scores(n)
                    if n >= 2:
                        products(n - 2)
                    if 1 <= n <= len(AJ):
                        turn_probs(n - 1)
                    if n == 0:
                        lru_gates()
                    if n == 3:
                        ssd_sums()
                        compressed_keys()
                    if n == 5:
                        ssd_cb()
                    if n == 6:
                        compressed_values()
                        ssd_products()
                    if n == 7:
                        lru_square()

                def turn_output(i):
                    pe.wait_ge(yn_ready, 2 * l + (1 if i == 2 else 2))
                    b = bank(0)
                    for j in range(2):
                        for tb in range(TB):
                            mm = pe.transpose(b[:, (2 * j + tb) * P:(2 * j + tb + 1) * P],
                                              yn[:, i, tb, j * P:(j + 1) * P], ident[:, :])
                    give(mm, 0)
                    mark["yT", l, i] = gave[0]

                def project_output(i):
                    if i == 0:
                        pe.wait_ge(act_took, gave[1])
                    pe.wait_ge(yT_lo_ready, 4 * l + i + 1)
                    last = i == 3
                    order = [(tb, low) for tb in range(TB) for low in (False, True)] if last else \
                        [(tb, low) for low in (False, True) for tb in range(TB)]
                    for tb, low in order:
                        w = parts_of(p, p, i, low).rearrange("p (k n) -> p k n", k=2)
                        for half in range(2):
                            for k in range(2):
                                kk, t = 2 * W_OUT_ORDER[i] + k, slice(tb * P, (tb + 1) * P)
                                mm = products3(banks[4 + 2 * tb + half][:, :], yT_hi[:, kk, t], yT_lo[:, kk, t],
                                               w[:, k, half * 512:(half + 1) * 512], i == 0 and k == 0,
                                               last and k == 1, low)
                        if last and low and tb == 0:
                            mm.then_inc(proj_done, 1)
                    mm.then_inc(units_used, 1)

                turn_output(2)
                project_output(0)
                turn_output(0)
                turn_output(1)
                for i in range(1, 4):
                    project_output(i)

                turn_normed(2 * l + 1)
                pe.wait_ge(act_took, gave[1])
                pe.wait_ge(dve_took, gave[0])
                if l == 0:
                    ffn(TB, BASE_FFN[0], hT_hi, hT_lo, BASE_FFN[0], 0)
                    pe.wait_ge(res_ready, 4)

            pe.wait_ge(misc_in, 16 * N_MISC)
            for tb in range(TB):
                for k in range(KT):
                    mm = pe.matmul(banks[0][:, tb * NE:(tb + 1) * NE], hT[:, k, tb * P:(tb + 1) * P],
                                   router[:, k, :], start=(k == 0), stop=(k == KT - 1))
            mm.then_inc(route_logits, 1)
            pe.wait_ge(sel_ready, 1)
            pe.matmul(banks[1][:, 0:NE], strict[:, :], sel[:, 0, :], start=True, stop=True)
            pe.matmul(banks[1][:, NE:2 * NE], ones[:, :], sel[:, 0, :], start=True, stop=False)
            pe.matmul(banks[1][:, NE:2 * NE], strict[:, :], sel[:, 1, :], start=False, stop=True)
            pe.matmul(banks[1][:, 2 * NE:3 * NE], ones[:, :], sel[:, 0, :], start=True, stop=False)
            pe.matmul(banks[1][:, 2 * NE:3 * NE], ones[:, :], sel[:, 1, :], start=False, stop=True)\
                .then_inc(ranks_done, 1)

            def gather(jobs_before):
                pe.wait_ge(pick_ready, jobs_before + 1)
                for d in range(KT):
                    for tb in range(TB):
                        mm = pe.matmul(banks[6 + d // 4][:, (d % 4) * P:(d % 4 + 1) * P],
                                       hn[:, tb, d * P:(d + 1) * P], pick[:, tb, :], start=(tb == 0),
                                       stop=(tb == TB - 1))
                mm.then_inc(xg_done, 1)

            gather(0)
            pe.wait_ge(pickT_ready, 1)
            for half in range(2):
                mm = pe.matmul(banks[4 + half][:, :], pickT[:, 0, :], ysb[:, half * 512:(half + 1) * 512], start=True,
                               stop=True)
            mm.then_inc(zero_sums, 1)

            def combine(tb, b0):
                for half in range(2):
                    mm = pe.matmul(banks[b0 + half][:, :], pickT[:, tb, :], ysb[:, half * 512:(half + 1) * 512],
                                   start=True, stop=True)
                mm.then_inc(comb_done, 1)

            def job(j, u0, s0):
                def more(c):
                    if c == 0:
                        pe.wait_ge(y_ready, 2 * j + 2)
                        pe.wait_ge(pickT_ready, j + 1)
                        combine(0, 6)
                    if c == 1:
                        pe.wait_ge(comb_took, 2 * j + 1)
                        combine(1, 6)
                    if c == 2:
                        pe.wait_ge(comb_took, 2 * j + 2)
                        pe.wait_ge(pick_ready, j + 1)
                        for tb in range(TB):
                            mm = pe.transpose(banks[6][:, tb * P:(tb + 1) * P], pickw[:, tb, :], ident[:, :])
                        mm.then_inc(pickT_done, 1)
                    if c == 4:
                        pe.wait_ge(pickT_ready, j + 2)
                        gather(j + 1)

                pe.wait_ge(xT_lo_ready, j + 1)
                ffn(1, BASE_FFN[1], xT_hi, xT_lo, u0, s0, more)

            with pe.Fori(0, NE) as e:
                job(e, e * FFN_SLOTS + BASE_FFN[1], e * NCH + DENSE)
            pe.wait_ge(steer_ready, 1)
            novf_r = pe.value_load(steer[0:1, 3:4], min_val=0, max_val=3)
            with pe.Fori(0, 3) as o:
                with pe.If(novf_r > o):
                    job(o + NE, o * FFN_SLOTS + (BASE_FFN[1] + NE * FFN_SLOTS), o * NCH + (DENSE + NE * NCH))
            pe.wait_ge(y_ready, novf_r * 2 + (2 * NE + 2))
            pe.wait_ge(pickT_ready, novf_r + (NE + 1))
            pe.wait_ge(xg_ready, novf_r + (NE + 1))
            for tb in range(TB):
                combine(tb, 4 + 2 * tb)

        @block.sync
        def _(sp):
            def mixer_loads(l):
                p = BASE_MIX[l]
                for segs in ([(0, 0, UA)], [(0, UA, UB), (UB, O_DT, SSD_H)], [(0, O_LRU, 512)],
                             [(0, O_XBC, 512)], [(0, O_XBC + 512, 256), (256, O_SSD, GW)]):
                    for half in range(2):
                        rows = w_in[l, half * 512:(half + 1) * 512, :].rearrange("(k p) n -> p k n", p=P)
                        wait_free(p)
                        for at, src, n in segs:
                            sp.dma_start(slot_k(p)[:, :, at:at + n], rows[:, :, src:src + n])\
                                .then_inc(slot_full[p % RING], 16)
                        p += 1
                for q in W_OUT_ORDER:
                    wait_free(p)
                    sp.dma_start(slot_r(p), w_out[l, q * 256:(q + 1) * 256, :].rearrange("(k p) n -> p k n", p=P))\
                        .then_inc(slot_full[p % RING], 16)
                    p += 1

            def wait_free(p):
                if p >= RING:
                    sp.wait_ge(lo_ready, p - RING + 1)

            def ffn_load(wg, wu, wd, at, p):
                (w, c), h = FFN_ORDER[at // 2], at % 2
                if w == "down":
                    r0 = c * FC + h * 256
                    dst, src = slot_r(p), wd[r0:r0 + 256, :]
                else:
                    dst = slot_k(p)
                    src = (wg if w == "gate" else wu)[h * 512:(h + 1) * 512, c * FC:(c + 1) * FC]
                sp.dma_start(dst, src.rearrange("(k p) n -> p k n", p=P)).then_inc(slot_full[p % RING], 16)

            def expert_loads(e, j, lo, hi):
                for at in range(lo, hi):
                    first_down = AT["down", 0]
                    if at != first_down:
                        sp.wait_ge(lo_ready, j * FFN_SLOTS
                                   + (BASE_FFN[1] + at - RING + (2 if at == first_down - 1 else 1)))
                    ffn_load(moe_w_gate[0, e], moe_w_up[0, e], moe_w_down[0, e], at, BASE_FFN[1] + at)

            for tb in range(TB):
                sp.dma_start(xres[:, tb, :], x[0, tb * P:(tb + 1) * P, :]).then_inc(x_in, 16)

            def rows(name, src, n, cols=P):
                r0 = PR[name]
                sp.dma_start(prow[r0:r0 + n, :, 0:cols], src).then_inc(prow_in, 16)

            sp.wait_ge(prow_zero, 1)
            rows("mix", norm_mix.rearrange("l (a b) -> a l b", b=P), 8)
            rows("ffn", norm_ffn.rearrange("l (a b) -> a l b", b=P), 8)
            rows("grp", group_norm.rearrange("l g (a b) -> (g a) l b", b=P), 8)
            rows("lcw", lru_conv_w.rearrange("l g (a b) -> (g a) l b", b=P), 8)
            rows("lcb", lru_conv_b.rearrange("l (a b) -> a l b", b=P), 2)
            rows("lbg", lru_b_gate.rearrange("l g (a b) -> (g a) l b", b=P), 4)
            rows("lam", lru_lambda.rearrange("l (a b) -> a l b", b=P), 2)
            rows("scw", ssd_conv_w.rearrange("l g (a b) -> (g a) l b", b=P), 24)
            rows("scb", ssd_conv_b.rearrange("l (a b) -> a l b", b=P), 6)
            rows("kvn", mla_kv_norm.rearrange("l (a b) -> a l b", b=P), 1)
            rows("qn", mla_q_norm.rearrange("l (a b) -> a l b", b=96), 2, 96)
            sp.dma_start(pe_row[:, :, :].rearrange("r l (i d) -> r (l i) d", i=2),
                         nsa_cmp_pe.rearrange("l i r d -> r (l i) d")).then_inc(prow_in, 16)
            mixer_loads(0)
            for at in range(FFN_SLOTS):
                wait_free(BASE_FFN[0] + at)
                ffn_load(ffn_w_gate[0], ffn_w_up[0], ffn_w_down[0], at, BASE_FFN[0] + at)
            mixer_loads(1)
            for at in range(RING):
                wait_free(BASE_FFN[1] + at)
                ffn_load(moe_w_gate[0, 0], moe_w_up[0, 0], moe_w_down[0, 0], at, BASE_FFN[1] + at)
            with sp.Fori(0, NE - 1) as e:
                expert_loads(e, e, RING, FFN_SLOTS)
                expert_loads(e + 1, e + 1, 0, RING)
            expert_loads(NE - 1, NE - 1, RING, FFN_SLOTS)
            sp.wait_ge(steer_ready, 1)
            novf_r = sp.value_load(steer[0:1, 3:4], min_val=0, max_val=3)
            with sp.Fori(0, 3) as o:
                with sp.If(novf_r > o):
                    ex = sp.value_load(steer[0:1, bass.ds(o, 1)], min_val=0, max_val=NE - 1)
                    expert_loads(ex, o + NE, 0, FFN_SLOTS)
            for tb in range(TB):
                sp.wait_ge(out_ready, tb + 1)
                sp.dma_start(out[0, tb * P:(tb + 1) * P, :], hn[:, tb, :]).then_inc(out_stored, 16)
            sp.wait_ge(out_stored, 16 * TB)

        @block.gpsimd
        def _(pool):
            chain = [0]

            def link(ins):
                chain[0] += 1
                ins.then_inc(pool_chain, 1)
                pool.wait_ge(pool_chain, chain[0])

            pool.dma_start(pos_i[:, :], positions.rearrange("(t p) -> p t", p=P),
                           allow_slow_non_contiguous=True).then_inc(pos_in, 16)
            def mixer_weights(l):
                pool.dma_start(w_uq[:, :, :], mla_w_uq[l].rearrange("(i p) n -> p i n", p=96)).then_inc(mixw_in, 16)
                pool.dma_start(w_ukv[:, :], mla_w_ukv[l]).then_inc(mixw_in, 16)
                for i in range(2):
                    pool.dma_start(w_cmp[i * HD:(i + 1) * HD, :, :],
                                   nsa_w_cmp[l, i].rearrange("(j d) e -> d j e", d=HD)).then_inc(mixw_in, 16)

            inv_freq = np.float32(ROPE_THETA) ** (-np.arange(0, ROPE, 2, dtype=np.float32) / np.float32(ROPE))
            for i in range(16):
                pool.memset(inv[:, i:i + 1], float(inv_freq[i])).then_inc(inv_ready, 1)
            link(pool.memset(ones[:, :], 1.0))
            link(pool.memset(ident[:, :], 0.0))
            link(pool.memset(cbias[:, :], 0.0))
            link(pool.memset(cmask[:, :, :], 1.0))
            link(pool.memset(cmbias[:, :, :], 0.0))
            link(pool.memset(minus_half[:, :], -0.5))
            link(pool.affine_select(out=ident[:, :], in_=ident[:, :], compare_op=ALU.not_equal, fill=1.0, base=0,
                                    pattern=[[-1, P]], channel_multiplier=1))
            link(pool.affine_select(out=upper[:, :], in_=ones[:, :], compare_op=ALU.is_ge, fill=0.0, base=0,
                                    pattern=[[1, P]], channel_multiplier=-1))
            link(pool.affine_select(out=strict[:, :], in_=ones[:, :], compare_op=ALU.is_ge, fill=0.0, base=-1,
                                    pattern=[[1, P]], channel_multiplier=-1))
            link(pool.affine_select(out=cbias[:, P:2 * P], in_=cbias[:, P:2 * P], compare_op=ALU.is_ge, fill=NEG,
                                    base=0, pattern=[[-1, P]], channel_multiplier=1))
            for tb in range(TB):
                for m, fill in ((cmask, 0.0), (cmbias, NEG)):
                    link(pool.affine_select(out=m[:, tb, :], in_=m[:, tb, :], compare_op=ALU.is_ge, fill=fill,
                                            base=tb * P - (CLEN - 1), pattern=[[-CSTRIDE, NC]],
                                            channel_multiplier=1))
            pool.iota(iota[:, :], pattern=[[1, P]], base=0, channel_multiplier=0,
                      allow_small_or_imprecise_dtypes=True).then_inc(consts_ready, 1)
            pool.wait_ge(consts_ready, 1)

            sets = [0, 0]

            def roots(n, i=0, last=True):
                c0 = 4 * sets[0] + i
                sets[0] += last
                sets[1] += n
                pool.wait_ge(ms_ready, sets[1])
                link(pool.tensor_scalar(stat[:, c0:c0 + n], stat[:, c0:c0 + n], EPS, None, ALU.add))
                pool.tensor_tensor(rstd[:, c0:c0 + n], stat[:, c0:c0 + n], minus_half[:, 0:n], ALU.pow)\
                    .then_inc(rstd_ready, 1)

            for l in range(L):
                roots(1, 0, False)
                roots(1, 1)
                if l == 0:
                    mixer_weights(0)
                    for i, src in enumerate((ssd_dt_bias, ssd_a_log, ssd_d)):
                        pool.dma_start(ssd_par[:, :, i, :], src[:, :].partition_broadcast(P)).then_inc(misc_in, 16)
                    pool.wait_ge(lru_w_zero, 1)
                    for odd in range(2):
                        o = odd * 64
                        pool.dma_start(lru_w[o:o + 64, :, :, :, o:o + 64].rearrange("i l g k j -> i (l g k) j"),
                                       lru_w_gate.rearrange("l g (k q) i j -> q i (l g k) j", q=2)[odd])\
                            .then_inc(misc_in, 16)
                    pool.dma_start(router[:, :, :], moe_router[0].rearrange("(k p) e -> p k e", p=P))\
                        .then_inc(misc_in, 16)
                    pool.dma_start(gfin[:, :], norm_final[:].partition_broadcast(P)).then_inc(misc_in, 16)
                roots(4)
                pool.wait_ge(act_took, mark["D", l])
                pool.wait_ge(dve_took, mark["E", l])
                taps = work[:, conv_at:conv_at + 6 * S].rearrange("p (i t) -> p i t", i=6)

                def over_time(name, i):
                    return par[:, l, PR[name] + i:PR[name] + i + 6].unsqueeze(2).broadcast_to([P, 6, S])

                link(pool.tensor_tensor(xbc[:, :, :], xraw[:, :, 0:S], over_time("scw", 0), ALU.mult))
                link(pool.tensor_tensor(xbc[:, :, :], xbc[:, :, :], over_time("scb", 0), ALU.add))
                for t in range(1, 4):
                    link(pool.tensor_tensor(taps, xraw[:, :, t:t + S], over_time("scw", 6 * t), ALU.mult))
                    ins = pool.tensor_tensor(xbc[:, :, :], xbc[:, :, :], taps, ALU.add)
                    if t < 3:
                        link(ins)
                    else:
                        ins.then_inc(ssd_conv, 1)
                roots(2)
                roots(4)
                if l == 0:
                    pool.wait_ge(*filled_by[0][mark["cmp", 0] - 1])
                    mixer_weights(1)
                roots(1, 0, False)
                roots(1, 1)
            roots(1, 0, False)
            roots(1, 1)

        @block.scalar
        def _(act):
            chain = [0]
            took = [0]

            def link(ins):
                chain[0] += 1
                ins.then_inc(act_chain, 1)
                act.wait_ge(act_chain, chain[0])

            def filled():
                b = banks[4 + took[0] % 4]
                act.wait_ge(*filled_by[1][took[0]])
                took[0] += 1
                return b

            squares = [0]

            def mean_square(dst_set, i, src, n, to):
                if squares[0]:
                    act.wait_ge(ms_ready, squares[0])
                squares[0] += 1
                act.activation(to, src, ACT.Square, scale=float(n) ** -0.5,
                               accum_out=stat[:, 4 * dst_set + i:4 * dst_set + i + 1]).then_inc(ms_ready, 1)

            act.wait_ge(x_in, 16 * TB)
            fills = [0] * RING

            def split(p, dmas=1, n=512):
                fills[p % RING] += 16 * dmas
                act.wait_ge(slot_full[p % RING], fills[p % RING])
                if p >= SPLIT:
                    act.wait_ge(units_used, p - SPLIT + 1)
                dst = w_hi[:, p % SPLIT, :].rearrange("p (k n) -> p k n", k=4)
                act.activation(dst[:, :, 0:n], slot_k(p)[:, :, 0:n], ACT.Copy).then_inc(hi_ready, 1)

            def split_input(norm):
                for g in range(4):
                    act.wait_ge(dve_took, mark["turned", norm, g])
                    act.activation(hT_hi[:, 2 * g:2 * g + 2, :], hT[:, 2 * g:2 * g + 2, :], ACT.Copy)\
                        .then_inc(hT_hi_ready, 1)

            def ffn(n, base, u0, s0, fill0, filled0, ahead, more=None):
                landed = [0] * RING

                def split(at):
                    i = (base + at) % RING
                    landed[i] += 16
                    if at < ahead:
                        return
                    act.wait_ge(slot_full[i], fill0 + (filled0[i] + landed[i]))
                    act.wait_ge(units_used, u0 + (at - SPLIT + 1))
                    act.activation(w_hi[:, (base + at) % SPLIT, :], ring[:, i, :], ACT.Copy).then_inc(hi_ready, 1)

                def turned(c):
                    for i in range(n):
                        v = (c * n + i) % 2
                        act.wait_ge(hidT_done, s0 + (c * n + i + 1))
                        act.activation(hidT_hi[:, v, :], banks[2 + v][:, :], ACT.Copy).then_inc(hidT_hi_ready, 1)

                for c in range(NCH):
                    split(at_gate(c, 0))
                    split(at_gate(c, 1))
                    if c == 0 and more is not None:
                        more()
                    split(at_up(c, 0))
                    if c >= 1:
                        turned(c - 1)
                    split(at_up(c, 1))
                    act.wait_ge(units_used, u0 + (at_gate(c, 1) + 1))
                    for i in range(n):
                        v = (c * n + i) % 2
                        act.activation(sgate[:, v, :], banks[v][:, :], ACT.Silu).then_inc(silu_done, 1)
                    if c >= 1:
                        split(at_down(c - 1, 0))
                        split(at_down(c - 1, 1))
                split(at_down(NCH - 1, 0))
                split(at_down(NCH - 1, 1))
                turned(NCH - 1)

            for l in range(L):
                p = BASE_MIX[l]
                if l > 0:
                    split(p)
                for tb in range(TB):
                    if l > 0:
                        act.wait_ge(res_ready, 2 + tb + 1)
                    mean_square(5 * l, tb, xres[:, tb, :], D, hn[:, tb, :])
                if l == 0:
                    split(p)
                    split_input(0)
                split(p + 1)
                if l > 0:
                    split_input(2 * l)
                split(p + 2, 2, UB + SSD_H)
                if l == 0:
                    act.wait_ge(rope_args, 1)
                    act.activation(trig[:, :, :, :], rr[:, :, :, :], ACT.Sin).then_inc(trig_ready, 1)
                    act.wait_ge(lam_args, 1)
                    act.activation(lru_t[:, :, 1, :], lru_t[:, :, 0, :], ACT.Exp).then_inc(lam_logs, 1)
                    act.wait_ge(lam_logs, 1)
                    act.activation(lru_t[:, :, 3, :], lru_t[:, :, 1, :], ACT.Ln, bias=1.0).then_inc(lam_logs, 1)
                for unit, n in ((0, UA), (1, UB + SSD_H)):
                    split(p + 3 + 2 * unit, 1 if unit else 2, 512 if unit else UB + SSD_H)
                    split(p + 4 + 2 * unit)
                    for tb in range(TB):
                        b = filled()
                        act.activation(utok[:, tb, unit * UA:unit * UA + n], b[:, 0:n], ACT.Copy)\
                            .then_inc(act_took, 1)
                act.wait_ge(act_took, took[0])
                for tb in range(TB):
                    mean_square(5 * l + 1, tb, utok[:, tb, 0:QR], QR, junk[:, 0, 0:QR])
                    mean_square(5 * l + 1, 2 + tb, utok[:, tb, QR:QR + KVR], KVR, junk[:, 1, 0:KVR])
                act.activation(gates[:, :, :], utok[:, :, O_LRU - 3 * NH:O_LRU], ACT.Tanh, scale=0.5)\
                    .then_inc(gate_th, 1)
                split(p + 7)
                if l == 0:
                    act.wait_ge(misc_in, 16 * N_MISC)
                    act.activation(neg_a[:, :, :], ssd_par[:, :, 1, :], ACT.Exp).then_inc(lam_logs, 1)
                act.wait_ge(ssd_vec, 4 * l + 1)
                link(act.activation(dts[:, 2, :, :], dts[:, 1, :, :], ACT.Exp, scale=-1.0))
                act.activation(dts[:, 3, :, :], dts[:, 2, :, :], ACT.Ln, bias=1.0).then_inc(ssd_act, 1)
                split(p + 8, 2)
                split(p + 9, 2)
                for i in range(4):
                    b = filled()
                    act.activation(xraw[:, i, 3:3 + S], b[:, 0:S], ACT.Copy).then_inc(act_took, 1)
                for tb in range(TB):
                    b = filled()
                    act.activation(qtok[:, tb, :, :], b[:, 0:MLA_H * QK].rearrange("p (h d) -> p h d", h=MLA_H),
                                   ACT.Copy).then_inc(act_took, 1)
                    v = filled()[:, :].rearrange("p (h d) -> p h d", h=MLA_H)
                    act.activation(kcat[:, tb, :, 0:NOPE], v[:, :, 0:NOPE], ACT.Copy)
                    act.activation(vtok[:, tb, :, :], v[:, :, NOPE:], ACT.Copy).then_inc(act_took, 1)
                for hp in range(2):
                    b = filled()
                    act.activation(nqT[0:HD, 2 * hp:2 * hp + 2, :],
                                   b[0:HD, :].rearrange("p (h t) -> p h t", h=2), ACT.Copy).then_inc(act_took, 1)
                b = filled()
                act.activation(kvcT[:, :], b[:, 0:S], ACT.Copy)
                act.activation(ksT[0:HD, :], b[0:HD, S:2 * S], ACT.Copy).then_inc(act_took, 1)
                b = filled()
                act.activation(kwT[0:HD, :], b[0:HD, 0:S], ACT.Copy).then_inc(act_took, 1)
                for dst in (qT, kT):
                    for hp in range(2):
                        b = filled()
                        act.activation(dst[0:QK, 2 * hp:2 * hp + 2, :],
                                       b[0:QK, :].rearrange("p (h t) -> p h t", h=2), ACT.Copy)\
                            .then_inc(act_took, 1)

                def exps(n):
                    br, tb = AJ[n]
                    nk = NC if br == "cmp" else (tb + 1) * P
                    act.wait_ge(dve_took, mark["scores", l, n])
                    for h in range(4):
                        e = act.activation(prob[:, n % 2, h, 0:nk], prob[:, n % 2, h, 0:nk], ACT.Exp,
                                           scale=-1.0, bias=rmin[:, n, h:h + 1], accum_out=rsum[:, n, h:h + 1])
                    e.then_inc(exp_ready, 1)

                def turned_probs(n):
                    br, tb = AJ[n]
                    if n >= 2:
                        act.wait_ge(*filled_by[0][mark["pv", l, n - 2] - 1])
                    rows = NC if br == "cmp" else P
                    for i in range(1 if br == "cmp" else tb + 1):
                        b = filled()
                        act.activation(probT[0:rows, n % 2, i * 512:(i + 1) * 512], b[0:rows, :], ACT.Copy)\
                            .then_inc(act_took, 1)

                for n in range(len(AJ) + 1):
                    if n < len(AJ):
                        exps(n)
                    if n >= 1:
                        turned_probs(n - 1)
                    if n == 0:
                        if l == 0:
                            act.wait_ge(half_b_ready, 1)
                        for g in range(2):
                            b = filled()
                            for i in range(2):
                                e = act.activation(lth[:, 2 * g + i, :], b[:, i * S:(i + 1) * S], ACT.Tanh, scale=0.5,
                                                   bias=half_b[:, l, 2 * g + i:2 * g + i + 1])
                            e.then_inc(act_took, 1)
                    if n == 1:
                        act.wait_ge(lru_vec, 5 * l + 1)
                        act.activation(lgate[:, :, :], lgate[:, :, :], ACT.Tanh, scale=float(np.sqrt(2 / np.pi)))\
                            .then_inc(lru_act, 1)
                        act.wait_ge(lru_vec, 5 * l + 2)
                        act.activation(lt2[:, :, :], la[:, :, :], ACT.Tanh, scale=0.5).then_inc(lru_act, 1)
                    if n == 2:
                        act.wait_ge(ssd_conv, l + 1)
                        act.activation(xbc[:, :, :], xbc[:, :, :], ACT.Silu)
                        act.activation(zs[:, :, :], zs[:, :, :], ACT.Silu).then_inc(ssd_act, 1)
                    if n == 4:
                        act.wait_ge(ssd_vec, 4 * l + 3)
                        act.activation(dec0[:, :, :], dec0[:, :, :], ACT.Exp)
                        act.activation(dec1[:, :, :], dec1[:, :, :], ACT.Exp).then_inc(ssd_act, 1)
                    if n == 4:
                        act.wait_ge(lru_vec, 5 * l + 3)
                        act.activation(lb[:, :, :], lb[:, :, :], ACT.Sqrt).then_inc(lru_act, 1)
                    if n == 6:
                        act.wait_ge(lru_vec, 5 * l + 4)
                        act.activation(lt1[:, :, :], lgate[:, :, :], ACT.Square, scale=GW ** -0.5).then_inc(lru_act, 1)
                    if n == 7:
                        act.wait_ge(ssd_vec, 4 * l + 4)
                        for tb in range(TB):
                            mean_square(5 * l + 2, tb, yd[:, tb, :], GW, junk[:, 1, :])
                    if n == 8:
                        act.wait_ge(lru_vec, 5 * l + 5)
                        act.activation(lrstd[:, :], lrstd[:, :], ACT.Sqrt).then_inc(lru_act, 1)

                act.wait_ge(o_ready, l + 1)
                for i, o in enumerate((oa, ob)):
                    for tb in range(TB):
                        mean_square(5 * l + 3, 2 * i + tb, o[:, tb, :], GW, junk[:, 0, :])


                for i, q in enumerate(W_OUT_ORDER):
                    if i < 3:
                        split(p + 10 + i)
                    if q == 2:
                        act.wait_ge(yT_ready, l + 1)
                    else:
                        act.wait_ge(dve_took, mark["yT", l, 2 if q == 3 else q])
                    act.activation(yT_hi[:, 2 * q:2 * q + 2, :], yT[:, 2 * q:2 * q + 2, :], ACT.Copy)\
                        .then_inc(yT_hi_ready, 1)
                split(p + 13)

                filled0 = list(fills)
                if l == 0:
                    split(p + 14)
                for tb in range(TB):
                    act.wait_ge(res_ready, 4 * l + tb + 1)
                    mean_square(5 * l + 4, tb, xres[:, tb, :], D, hn[:, tb, :])
                if l == 0:
                    split(p + 15)
                    split_input(1)
                    split(p + 16)
                    ffn(TB, BASE_FFN[0], BASE_FFN[0], 0, 0, filled0, 3)
                    fills[:] = [n + 16 * FFN_SLOTS // RING for n in filled0]

            act.wait_ge(route_diff, 1)
            act.activation(topw[:, 1, :], topw[:, 0, :], ACT.Exp).then_inc(route_exp, 1)

            PER_JOB = 16 * FFN_SLOTS // RING

            def output_by_slot(u0):
                if u0 is not None:
                    act.wait_ge(units_used, u0)
                for half in range(2):
                    act.activation(ysb[:, half * 512:(half + 1) * 512], banks[4 + half][:, :], ACT.Copy)\
                        .then_inc(y_ready, 1)

            def split_tokens(jobs_before, u_read=None):
                act.wait_ge(xg_ready, jobs_before + 1)
                if u_read is not None:
                    act.wait_ge(units_used, u_read)
                act.activation(xT_hi[:, :, :], xg[:, :, :], ACT.Copy).then_inc(xT_hi_ready, 1)

            split_tokens(0)
            act.wait_ge(zero_sums, 1)

            def job(j, u0, s0):
                def more():
                    output_by_slot(u0)
                ffn(1, BASE_FFN[1], u0, s0, j * PER_JOB, fills, 0, more)
                split_tokens(j + 1, u0 + (at_up(NCH - 1, 1) + 1))

            with act.Fori(0, NE) as e:
                job(e, e * FFN_SLOTS + BASE_FFN[1], e * NCH + DENSE)
            act.wait_ge(steer_ready, 1)
            novf_r = act.value_load(steer[0:1, 3:4], min_val=0, max_val=3)
            with act.Fori(0, 3) as o:
                with act.If(novf_r > o):
                    job(o + NE, o * FFN_SLOTS + (BASE_FFN[1] + NE * FFN_SLOTS), o * NCH + (DENSE + NE * NCH))
            output_by_slot(novf_r * FFN_SLOTS + (BASE_FFN[1] + NE * FFN_SLOTS))

        @block.vector
        def _(dve):
            chain = [0]
            took = [0]

            def link(ins):
                chain[0] += 1
                ins.then_inc(dve_chain, 1)
                dve.wait_ge(dve_chain, chain[0])

            counts = {}

            def signal(ins, name, s):
                counts[name] = counts.get(name, 0) + 1
                ins.then_inc(s, 1)
                dve.wait_ge(s, counts[name])

            def filled():
                b = banks[took[0] % 4]
                dve.wait_ge(*filled_by[0][took[0]])
                took[0] += 1
                return b

            def take_bank(ins):
                ins.then_inc(dve_took, 1)
                dve.wait_ge(dve_took, took[0])

            dve.memset(prow[:, :, :], 0.0).then_inc(prow_zero, 1)
            dve.memset(lru_w[:, :, :, :, :], 0.0).then_inc(lru_w_zero, 1)

            dve.wait_ge(inv_ready, ROPE // 2)
            dve.wait_ge(pos_in, 16)
            link(dve.tensor_copy(pos_f[:, :], pos_i[:, :]))
            for tb in range(TB):
                link(dve.tensor_scalar(ang[:, tb, :], inv[:, :], pos_f[:, tb:tb + 1], None, ALU.mult))
            TURN = 2 * np.pi
            MAGIC = 1.5 * 2.0 ** 23
            PARTS = [6.28125, 1.93500518798828125e-3]
            PARTS.append(TURN - sum(PARTS))
            for i in range(2):
                link(dve.tensor_scalar(rk[:, i, :, :], ang[:, :, :], 1 / TURN, 0.25 * i, ALU.mult, ALU.add))
                link(dve.tensor_scalar(rk[:, i, :, :], rk[:, i, :, :], MAGIC, None, ALU.add))
                link(dve.tensor_scalar(rk[:, i, :, :], rk[:, i, :, :], -MAGIC, None, ALU.add))
                src = ang
                for part in PARTS:
                    s_ = src[:, :, :] if src is ang else rr[:, i, :, :]
                    link(dve.scalar_tensor_tensor(out=rr[:, i, :, :], in0=rk[:, i, :, :], scalar=-part, in1=s_,
                                                  op0=ALU.mult, op1=ALU.add))
                    src = rr
            link(dve.tensor_scalar(rr[:, 1, :, :], rr[:, 1, :, :], np.pi / 2, None, ALU.add))
            signal(dve.tensor_scalar(rr[:, :, :, :], rr[:, :, :, :], -3.1415925, 3.1415925, ALU.max, ALU.min),
                   "rope", rope_args)

            b = filled()
            link(dve.tensor_copy(par[:, :, :], b[:, 0:2 * P].rearrange("p (l c) -> p l c", l=L)))
            take_bank(dve.tensor_copy(pe_t[:, :, :], b[:, 2 * P:2 * P + L * CLEN].rearrange("p (l c) -> p l c", l=L)))
            lam = par[:, :, PR["lam"]:PR["lam"] + 2]
            link(dve.tensor_scalar(lru_t[:, :, 5, :], lam, -1.0, None, ALU.mult))
            signal(dve.tensor_tensor(lru_t[:, :, 0, :], lru_t[:, :, 5, :], lam, ALU.min), "lam", lam_args)
            signal(dve.tensor_scalar(half_b[:, :, :], par[:, :, PR["lbg"]:PR["lbg"] + 4], 0.5, None, ALU.mult),
                   "half_b", half_b_ready)
            dve.wait_ge(x_in, 16 * TB)

            def normed(l2, turn_set):
                for tb in range(TB):
                    dve.wait_ge(rstd_ready, 7 * (l2 // 2) + 5 * (l2 % 2) + tb + 1)
                    signal(dve.tensor_scalar(hn[:, tb, :], xres[:, tb, :],
                                             rstd[:, 4 * turn_set + tb:4 * turn_set + tb + 1], None, ALU.mult),
                           "hn", hn_ready)
                l, which = divmod(l2, 2)
                c0 = PR["ffn" if which else "mix"]
                for g in range(6):
                    if g < 4:
                        b = filled()
                        gain = par[:, l, c0 + 2 * g:c0 + 2 * g + 2].unsqueeze(2).broadcast_to([P, 2, S])
                        take_bank(dve.tensor_tensor(hT[:, 2 * g:2 * g + 2, :],
                                                    b[:, :].rearrange("p (k t) -> p k t", k=2), gain, ALU.mult))
                    if g >= 2 and l2 < 3:
                        dve.wait_ge(hT_hi_ready, 4 * l2 + g - 1)
                        at = slice(2 * (g - 2), 2 * (g - 1))
                        dve.tensor_tensor(hT_lo[:, at, :], hT[:, at, :], hT_hi[:, at, :].bitcast(F32), ALU.subtract)\
                            .then_inc(hT_lo_ready, 1)

            def rope(v, cos, sin, shape):
                n = int(np.prod(shape[1:]))
                names = " ".join("abc"[:len(shape) - 1])
                r = [rt[:, i, 0:n].rearrange(f"p ({names}) -> p {names}", **dict(zip("bc", shape[2:])))
                     if len(shape) > 2 else rt[:, i, 0:n] for i in range(4)]
                for i, (a, t) in enumerate(((v[0], cos), (v[1], sin), (v[1], cos), (v[0], sin))):
                    link(dve.tensor_tensor(r[i], a, t, ALU.mult))
                link(dve.tensor_tensor(v[0], r[0], r[1], ALU.subtract))
                return dve.tensor_tensor(v[1], r[2], r[3], ALU.add)

            def split(p, n=512):
                dve.wait_ge(hi_ready, p + 1)
                hi = w_hi[:, p % SPLIT, :].bitcast(F32).rearrange("p (k n) -> p k n", k=4)
                dst = w_lo[:, p % SPLIT, :].rearrange("p (k n) -> p k n", k=4)
                dve.tensor_tensor(dst[:, :, 0:n], slot_k(p)[:, :, 0:n], hi[:, :, 0:n], ALU.subtract)\
                    .then_inc(lo_ready, 1)

            def add_sums(tb):
                for half in range(2):
                    r = xres[:, tb, half * 512:(half + 1) * 512]
                    ins = dve.tensor_tensor(r, r, banks[4 + 2 * tb + half][:, :], ALU.add)
                    if half == 1:
                        signal(ins, "res", res_ready)
                    else:
                        link(ins)

            def ffn(n, base, u0, s0, ahead, more=None):
                def split(at):
                    if at < ahead:
                        return
                    dve.wait_ge(hi_ready, u0 + (at + 1))
                    v = (base + at) % SPLIT
                    dve.tensor_tensor(w_lo[:, v, :], ring[:, (base + at) % RING, :], w_hi[:, v, :].bitcast(F32),
                                      ALU.subtract).then_inc(lo_ready, 1)

                def turned(c):
                    for i in range(n):
                        v = (c * n + i) % 2
                        dve.wait_ge(hidT_hi_ready, s0 + (c * n + i + 1))
                        dve.tensor_tensor(hidT_lo[:, v, :], banks[2 + v][:, :], hidT_hi[:, v, :].bitcast(F32),
                                          ALU.subtract).then_inc(hidT_lo_ready, 1)

                def hidden(c):
                    dve.wait_ge(units_used, u0 + (at_up(c, 1) + 1))
                    dve.wait_ge(silu_done, s0 + n * (c + 1))
                    for i in range(n):
                        v = (c * n + i) % 2
                        dve.tensor_tensor(hid[:, v, :], sgate[:, v, :], banks[2 + v][:, :], ALU.mult)\
                            .then_inc(hid_ready, 1)

                for c in range(NCH):
                    split(at_gate(c, 0))
                    split(at_gate(c, 1))
                    if c == 1:
                        hidden(0)
                        if more is not None:
                            more(0)
                    split(at_up(c, 0))
                    if c >= 1:
                        turned(c - 1)
                    split(at_up(c, 1))
                    if c >= 1:
                        split(at_down(c - 1, 0))
                        split(at_down(c - 1, 1))
                        hidden(c)
                        if more is not None:
                            more(c)
                split(at_down(NCH - 1, 0))
                split(at_down(NCH - 1, 1))
                turned(NCH - 1)

            for l in range(L):
                p = BASE_MIX[l]
                link(dve.memset(lraw[:, 0:2, 0:3], 0.0))
                link(dve.memset(xraw[:, :, 0:3], 0.0))
                if l > 0:
                    split(p)
                normed(2 * l, 5 * l)
                if l == 0:
                    split(p)
                split(p + 1)
                split(p + 2, UB + SSD_H)
                if l == 0:
                    dve.wait_ge(lam_logs, 2)
                    e_, w_, lg, d_, t_ = (lru_t[:, :, i, :] for i in (1, 2, 3, 4, 5))
                    link(dve.tensor_scalar(w_, e_, 1.0, None, ALU.add))
                    link(dve.tensor_scalar(w_, w_, -1.0, None, ALU.add))
                    link(dve.tensor_scalar(d_, w_, 1e-30, None, ALU.max))
                    link(dve.reciprocal(d_, d_))
                    link(dve.tensor_tensor(lg, lg, e_, ALU.mult))
                    link(dve.tensor_tensor(lg, lg, d_, ALU.mult))
                    link(dve.scalar_tensor_tensor(out=w_, in0=w_, scalar=0.0, in1=e_, op0=ALU.is_equal, op1=ALU.mult))
                    link(dve.tensor_tensor(lg, lg, w_, ALU.add))
                    link(dve.scalar_tensor_tensor(out=lg, in0=t_, scalar=0.0, in1=lg, op0=ALU.max, op1=ALU.add))
                    link(dve.tensor_scalar(lru_c[:, :, 0:2], lg, -4.0, None, ALU.mult))
                    dve.wait_ge(trig_ready, 1)

                split(p + 3, UB + SSD_H)
                for i in range(4, 7):
                    split(p + i)
                if l == 0:
                    dve.wait_ge(misc_in, 16 * N_MISC)
                dve.wait_ge(act_took, mark["u", l])
                bias = ssd_par[:, l, 0:1, :].broadcast_to([P, TB, SSD_H])
                link(dve.tensor_tensor(dts[:, 0, :, :], utok[:, :, O_LRU:O_LRU + SSD_H], bias, ALU.add))
                link(dve.tensor_scalar(dts[:, 1, :, :], dts[:, 0, :, :], -1.0, None, ALU.mult))
                signal(dve.tensor_tensor(dts[:, 1, :, :], dts[:, 1, :, :], dts[:, 0, :, :], ALU.max),
                       "ssd_vec", ssd_vec)
                split(p + 7)
                dve.wait_ge(rstd_ready, 7 * l + 3)
                r0 = 4 * (5 * l + 1)
                for tb in range(TB):
                    link(dve.tensor_scalar(cqn[:, tb, :], utok[:, tb, 0:QR], rstd[:, r0 + tb:r0 + tb + 1], None,
                                           ALU.mult))
                    ins = dve.tensor_scalar(ckvn[:, tb, :], utok[:, tb, QR:QR + KVR],
                                            rstd[:, r0 + 2 + tb:r0 + 3 + tb], None, ALU.mult)
                    if tb == 0:
                        link(ins)
                    else:
                        signal(ins, "cn", cn_ready)
                split(p + 8)
                for i in range(4):
                    b = filled()
                    take_bank(dve.tensor_copy(lraw[:, i, 3:3 + S], b[:, 0:S]))
                cosn, sinn = trig[:, 1, :, 0:16:2], trig[:, 0, :, 0:16:2]
                for c0, n, step in ((O_NSA, NH, HD), (KV0, 3, 2 * HD)):
                    v = utok[:, :, c0:c0 + n * step].rearrange("p t (h d) -> p t h d", h=n)
                    sh = [P, TB, n, NROT // 2]
                    ins = rope((v[:, :, :, 0:8], v[:, :, :, 8:16]), cosn.unsqueeze(2).broadcast_to(sh),
                               sinn.unsqueeze(2).broadcast_to(sh), sh)
                    if c0 == O_NSA:
                        link(ins)
                    else:
                        signal(ins, "nsa_roped", nsa_roped)
                v = utok[:, :, QR + KVR:QR + KVR + ROPE]
                link(rope((v[:, :, 0:16], v[:, :, 16:32]), trig[:, 1, :, :], trig[:, 0, :, :], [P, TB, 16]))

                split(p + 9)
                for i in range(2):
                    b = filled()
                    take_bank(dve.tensor_copy(xraw[:, 4 + i, 3:3 + S], b[:, 0:S]))
                for tb in range(TB):
                    b = filled()
                    take_bank(dve.tensor_copy(zs[:, tb, :], b[:, 0:GW]))

                b = filled()
                gain = par[0:96, l, PR["qn"]:PR["qn"] + 2].unsqueeze(2).broadcast_to([96, 2, S])
                take_bank(dve.tensor_tensor(cqT[0:96, :, :], b[0:96, :].rearrange("p (k t) -> p k t", k=2), gain,
                                            ALU.mult))
                b = filled()
                take_bank(dve.tensor_scalar(ckvT[:, :], b[:, 0:S], pcol(l, "kvn"), None, ALU.mult))
                signal(dve.tensor_copy(flag[:, 0:1], ones[:, 0:1]), "cT", cT_ready)

                def conv(dst, raw, w, bias_, n):
                    for i in range(n):
                        link(dve.tensor_scalar(dst[:, i, :], raw[:, i, 0:S], pcol(l, w, i), pcol(l, bias_, i),
                                               ALU.mult, ALU.add))
                        for t in range(1, 4):
                            ins = dve.scalar_tensor_tensor(out=dst[:, i, :], in0=raw[:, i, t:t + S],
                                                           scalar=pcol(l, w, n * t + i), in1=dst[:, i, :],
                                                           op0=ALU.mult, op1=ALU.add)
                            if not (t == 3 and i == n - 1):
                                link(ins)
                    return ins

                signal(conv(xb, lraw, "lcw", "lcb", 2), "lru_conv", lru_conv)

                dve.wait_ge(act_took, mark["qkv", l])
                sh = [P, TB, MLA_H, ROPE // 2]
                v = qtok[:, :, :, NOPE:QK]
                link(rope((v[:, :, :, 0:16], v[:, :, :, 16:32]), trig[:, 1, :, :].unsqueeze(2).broadcast_to(sh),
                          trig[:, 0, :, :].unsqueeze(2).broadcast_to(sh), sh))
                kpe = utok[:, :, QR + KVR:QR + KVR + ROPE].unsqueeze(2).broadcast_to([P, TB, MLA_H, ROPE])
                signal(dve.tensor_copy(kcat[:, :, :, NOPE:QK], kpe), "qk_roped", qk_roped)

                dve.wait_ge(act_took, mark["nsa", l])
                for i in range(2):
                    src = kvcT[:, 16 * i:16 * i + 16 * NC].rearrange("p (n j) -> p j n", j=16)
                    pos = pe_t[:, l, 16 * i:16 * i + 16].unsqueeze(2).broadcast_to([P, 16, NC])
                    ins = dve.tensor_tensor(cin[:, 16 * i:16 * i + 16, :], src, pos, ALU.add)
                    if i == 0:
                        link(ins)
                    else:
                        signal(ins, "cin", cin_ready)
                dve.wait_ge(gate_th, l + 1)
                link(dve.tensor_scalar(gates[:, :, :], gates[:, :, :], 0.5, 0.5, ALU.mult, ALU.add))

                def score_rows(n):
                    br, tb = AJ[n]
                    nk = NC if br == "cmp" else (tb + 1) * P
                    if n >= 2:
                        dve.wait_ge(act_took, mark["probT", l, n - 2])
                    per = 4 if br == "cmp" else 512 // nk
                    scale = float(QK if br == "mla" else HD) ** -0.5
                    m = cmbias[:, tb, :] if br == "cmp" else cbias[:, P - tb * P:2 * P]
                    for g in range(4 // per):
                        b = filled()
                        for i in range(per):
                            h = g * per + i
                            ins = dve.tensor_tensor_reduce(prob[:, n % 2, h, 0:nk], b[:, i * nk:(i + 1) * nk], m,
                                                           -scale, -NEG, ALU.add, ALU.min, rmin[:, n, h:h + 1])
                        take_bank(ins)

                def mask_cmp(n):
                    tb = AJ[n][1]
                    dve.wait_ge(exp_ready, 8 * l + n + 1)
                    signal(dve.tensor_tensor(prob[:, n % 2, :, 0:NC], prob[:, n % 2, :, 0:NC],
                                             cmask[:, tb:tb + 1, :].broadcast_to([P, 4, NC]), ALU.mult),
                           "masked", masked)

                def outputs(n):
                    br, tb = AJ[n]
                    dve.wait_ge(exp_ready, 8 * l + n + 1)
                    link(dve.reciprocal(coef[:, n, :], rsum[:, n, :]))
                    if br != "mla":
                        i = ("cmp", "sel", "win").index(br)
                        link(dve.tensor_tensor(coef[:, n, :], coef[:, n, :],
                                               gates[:, tb, i:i + 3 * NH - 2:3], ALU.mult))
                    b = filled()
                    c = coef[:, n, :].unsqueeze(2).broadcast_to([P, 4, HD])
                    dst = {"mla": oa[:, tb, :], "sel": ob[:, tb, :]}.get(br, ot[:, :])
                    take_bank(dve.tensor_tensor(dst.rearrange("p (h d) -> p h d", h=4),
                                                b[:, 0:GW].rearrange("p (h d) -> p h d", h=4), c, ALU.mult))
                    if br in ("win", "cmp"):
                        ins = dve.tensor_tensor(ob[:, tb, :], ob[:, tb, :], ot[:, :], ALU.add)
                        if n == len(AJ) - 1:
                            signal(ins, "o", o_ready)
                        else:
                            link(ins)

                g = lraw[:, 2:4, 3:3 + S]
                for n in range(len(AJ) + 2):
                    if n < len(AJ):
                        score_rows(n)
                    if 1 <= n <= len(AJ) and AJ[n - 1][0] == "cmp":
                        mask_cmp(n - 1)
                    if n >= 2:
                        outputs(n - 2)
                    if n == 0:
                        dve.wait_ge(ssd_act, 3 * l + 1)
                        dve.wait_ge(lam_logs, 3)
                        link(dve.scalar_tensor_tensor(out=dts[:, 4, :, :], in0=dts[:, 0, :, :], scalar=0.0,
                                                      in1=dts[:, 3, :, :], op0=ALU.max, op1=ALU.add))
                        signal(dve.scalar_tensor_tensor(out=dts[:, 5, :, :], in0=dts[:, 4, :, :], scalar=-1.0,
                                                        in1=neg_a[:, l:l + 1, :].broadcast_to([P, TB, SSD_H]),
                                                        op0=ALU.mult, op1=ALU.mult), "ssd_vec", ssd_vec)
                        link(dve.tensor_tensor(lgate[:, :, :], g, g, ALU.mult))
                        link(dve.tensor_scalar(lgate[:, :, :], lgate[:, :, :], 0.044715, 1.0, ALU.mult, ALU.add))
                        signal(dve.tensor_tensor(lgate[:, :, :], lgate[:, :, :], g, ALU.mult), "lru_vec", lru_vec)
                    if n == 1:
                        dve.wait_ge(act_took, mark["lgate", l])
                        for i in range(2):
                            ins = dve.tensor_scalar(la[:, i, :], lth[:, i, :], 1.0, lru_c[:, l, i:i + 1], ALU.add, ALU.mult)
                            if i == 0:
                                link(ins)
                            else:
                                signal(ins, "lru_vec", lru_vec)
                    if n == 2:
                        dve.wait_ge(lru_act, 5 * l + 2)
                        link(dve.tensor_scalar(ld[:, :, :], lt2[:, :, :], -1.0, 1.0, ALU.mult, ALU.add))
                        link(dve.reciprocal(ld[:, :, :], ld[:, :, :]))
                        link(dve.scalar_tensor_tensor(out=lb[:, :, :], in0=lt2[:, :, :], scalar=-4.0, in1=ld[:, :, :],
                                                      op0=ALU.mult, op1=ALU.mult))
                        signal(dve.scalar_tensor_tensor(out=lb[:, :, :], in0=lb[:, :, :], scalar=0.0,
                                                        in1=ld[:, :, :], op0=ALU.max, op1=ALU.mult),
                               "lru_vec", lru_vec)
                        link(dve.scalar_tensor_tensor(out=lt2[:, :, :], in0=lt2[:, :, :], scalar=1.0, in1=ld[:, :, :],
                                                      op0=ALU.add, op1=ALU.mult))
                        link(dve.scalar_tensor_tensor(out=lt1[:, :, :], in0=lth[:, 2:4, :], scalar=1.0, in1=xb[:, :, :],
                                                      op0=ALU.add, op1=ALU.mult))
                        dve.wait_ge(lru_act, 5 * l + 1)
                        link(dve.scalar_tensor_tensor(out=lgate[:, :, :], in0=lgate[:, :, :], scalar=1.0, in1=g,
                                                      op0=ALU.add, op1=ALU.mult))
                    if n == 3:
                        b = filled()
                        take_bank(dve.tensor_copy(xtok[:, :, :], b[:, :].rearrange("p (t c) -> p t c", t=TB)))
                        for tb in range(TB):
                            link(dve.tensor_tensor(xdt[:, tb, :].rearrange("p (h d) -> p h d", h=SSD_H),
                                                   xtok[:, tb, :].rearrange("p (h d) -> p h d", h=SSD_H),
                                                   dts[:, 4, tb, :].unsqueeze(2).broadcast_to([P, SSD_H, HD]), ALU.mult))
                        b = filled()
                        take_bank(dve.tensor_scalar(nacs[:, :, :], b[:, 0:TB * SSD_H].rearrange("p (t h) -> p t h", t=TB),
                                                    -1.0, None, ALU.mult))
                        for hp in range(2):
                            b = filled()
                            for i in range(2):
                                h = 2 * hp + i
                                link(dve.tensor_scalar(dec0[:, h, :], b[:, i * S:(i + 1) * S], nacs[:, 0, h:h + 1], 0.0,
                                                       ALU.add, ALU.min))
                                ins = dve.tensor_scalar(dec1[:, h, :], b[:, i * S + P:(i + 1) * S], nacs[:, 1, h:h + 1],
                                                        0.0, ALU.add, ALU.min)
                                if i == 0:
                                    link(ins)
                            take_bank(ins)
                        signal(dve.tensor_copy(flag[:, 0:1], ones[:, 0:1]), "ssd_vec", ssd_vec)
                    if n == 3:
                        b = filled()
                        take_bank(dve.tensor_copy(kcT[0:HD, :], b[0:HD, 0:NC]))
                        signal(dve.tensor_copy(flag[:, 0:1], ones[:, 0:1]), "cmp", cmp_ready)
                    if n == 6:
                        b = filled()
                        take_bank(dve.tensor_copy(vc[0:NC, :], b[0:NC, 0:HD]))
                        signal(dve.tensor_copy(flag[:, 0:1], ones[:, 0:1]), "cmp", cmp_ready)
                    if n == 5:
                        dve.wait_ge(ssd_act, 3 * l + 3)
                        tri = upper[:, :].unsqueeze(1).broadcast_to([P, SSD_H, P])
                        link(dve.tensor_tensor(dec0[:, :, 0:P], dec0[:, :, 0:P], tri, ALU.mult))
                        link(dve.tensor_tensor(dec1[:, :, :], dec1[:, :, :], tri, ALU.mult))
                        for d, w in ((dec0, S), (dec1, P)):
                            b = filled()
                            for g_ in range(SSD_G):
                                v = d[:, 2 * g_:2 * g_ + 2, :]
                                sc = b[:, g_ * w:(g_ + 1) * w].unsqueeze(1).broadcast_to([P, 2, w])
                                ins = dve.tensor_tensor(v, v, sc, ALU.mult)
                                if g_ == 0:
                                    link(ins)
                            take_bank(ins)
                        signal(dve.tensor_copy(flag[:, 0:1], ones[:, 0:1]), "dec", dec_ready)
                    if n == 5:
                        dve.wait_ge(lru_act, 5 * l + 3)
                        link(dve.scalar_tensor_tensor(out=lb[:, :, :], in0=lb[:, :, :], scalar=0.5, in1=lt1[:, :, :],
                                                      op0=ALU.mult, op1=ALU.mult))
                        for i in range(2):
                            link(dve.tensor_tensor_scan(la[:, i, :], lt2[:, i, :], lb[:, i, :], 0.0, ALU.mult, ALU.add))
                        signal(dve.scalar_tensor_tensor(out=lgate[:, :, :], in0=lgate[:, :, :], scalar=0.5, in1=la[:, :, :],
                                                        op0=ALU.mult, op1=ALU.mult), "lru_vec", lru_vec)
                    if n == 6:
                        for tb in range(TB):
                            link(dve.tensor_tensor(yd[:, tb, :].rearrange("p (h d) -> p h d", h=SSD_H),
                                                   xtok[:, tb, :].rearrange("p (h d) -> p h d", h=SSD_H),
                                                   ssd_par[:, l, 2, :].unsqueeze(2).broadcast_to([P, SSD_H, HD]), ALU.mult))
                        for tb in range(TB):
                            b = filled()
                            take_bank(dve.tensor_tensor(yd[:, tb, :], yd[:, tb, :], b[:, 0:GW], ALU.add))
                        signal(dve.tensor_tensor(yd[:, :, :], yd[:, :, :], zs[:, :, :], ALU.mult), "ssd_vec", ssd_vec)
                    if n == 7:
                        b = filled()
                        take_bank(dve.tensor_scalar(lrstd[:, :], b[:, 0:S], EPS, None, ALU.add))
                        signal(dve.tensor_copy(flag[:, 0:1], ones[:, 0:1]), "lru_vec", lru_vec)
                    if n == 9:
                        dve.wait_ge(lru_act, 5 * l + 5)
                        link(dve.reciprocal(lrstd[:, :], lrstd[:, :]))
                        for i in range(2):
                            ins = dve.scalar_tensor_tensor(out=yT[:, 4 + i, :], in0=lgate[:, i, :],
                                                           scalar=pcol(l, "grp", 4 + i), in1=lrstd[:, :],
                                                           op0=ALU.mult, op1=ALU.mult)
                            if i == 0:
                                link(ins)
                            else:
                                signal(ins, "yT", yT_ready)

                dve.wait_ge(rstd_ready, 7 * l + 4)
                r0 = 4 * (5 * l + 2)
                for tb in range(TB):
                    ins = dve.tensor_scalar(yn[:, 2, tb, :], yd[:, tb, :], rstd[:, r0 + tb:r0 + tb + 1], None,
                                            ALU.mult)
                    if tb == 0:
                        link(ins)
                    else:
                        signal(ins, "yn", yn_ready)

                def turned_output(grp):
                    b = filled()
                    gain = par[:, l, PR["grp"] + 2 * grp:PR["grp"] + 2 * grp + 2].unsqueeze(2)\
                        .broadcast_to([P, 2, S])
                    take_bank(dve.tensor_tensor(yT[:, 2 * grp:2 * grp + 2, :],
                                                b[:, :].rearrange("p (k t) -> p k t", k=2), gain, ALU.mult))

                def split_output(i):
                    dve.wait_ge(yT_hi_ready, 4 * l + i + 1)
                    q = W_OUT_ORDER[i]
                    dve.tensor_tensor(yT_lo[:, 2 * q:2 * q + 2, :], yT[:, 2 * q:2 * q + 2, :],
                                      yT_hi[:, 2 * q:2 * q + 2, :].bitcast(F32), ALU.subtract)\
                        .then_inc(yT_lo_ready, 1)

                split_output(0)
                split(p + 10)
                turned_output(3)
                dve.wait_ge(rstd_ready, 7 * l + 5)
                r0 = 4 * (5 * l + 3)
                for i, o in enumerate((oa, ob)):
                    for tb in range(TB):
                        ins = dve.tensor_scalar(yn[:, i, tb, :], o[:, tb, :],
                                                rstd[:, r0 + 2 * i + tb:r0 + 2 * i + tb + 1], None, ALU.mult)
                        if (i, tb) == (1, TB - 1):
                            signal(ins, "yn", yn_ready)
                        else:
                            link(ins)
                split_output(1)
                split(p + 11)
                turned_output(0)
                turned_output(1)
                split_output(2)
                split(p + 12)
                split_output(3)
                split(p + 13)
                if l == 0:
                    split(p + 14)
                dve.wait_ge(proj_done, 2 * l + 1)
                add_sums(0)
                dve.wait_ge(units_used, p + 14)
                add_sums(1)
                normed(2 * l + 1, 5 * l + 4)

                if l == 0:
                    split(p + 15)
                    split(p + 16)
                    ffn(TB, BASE_FFN[0], BASE_FFN[0], 0, 3)
                    dve.wait_ge(proj_done, 2)
                    add_sums(0)
                    dve.wait_ge(units_used, BASE_FFN[0] + FFN_SLOTS)
                    add_sums(1)

            link(dve.memset(ysb[:, :], 0.0))
            dve.memset(pickT[:, :, :], 0.0).then_inc(pickT_ready, 1)
            dve.wait_ge(route_logits, 1)
            link(dve.tensor_copy(logit[:, :, :], banks[0][:, 0:TB * NE].rearrange("p (t e) -> p t e", t=TB)))
            for tb in range(TB):
                link(dve.max(out=top[:, tb, :], in_=logit[:, tb, :]))
                link(dve.max_index(out=topi[:, tb, :], in_max=top[:, tb, :], in_values=logit[:, tb, :]))
            link(dve.tensor_copy(topf[:, :, :], topi[:, :, :]))
            signal(dve.tensor_tensor(topw[:, 0, :], top[:, :, 1], top[:, :, 0], ALU.subtract), "diff", route_diff)
            for i in range(2):
                for tb in range(TB):
                    link(dve.tensor_scalar(hot[:, i, tb, :], iota[:, 0:NE], topf[:, tb, i:i + 1], None,
                                           ALU.is_equal))
            signal(dve.tensor_tensor(sel[:, :, :], hot[:, 0, :, :], hot[:, 1, :, :], ALU.add), "sel", sel_ready)
            dve.wait_ge(route_exp, 1)
            link(dve.tensor_scalar(topw[:, 2, :], topw[:, 1, :], 1.0, None, ALU.add))
            link(dve.reciprocal(topw[:, 2, :], topw[:, 2, :]))
            link(dve.tensor_tensor(topw[:, 3, :], topw[:, 1, :], topw[:, 2, :], ALU.mult))
            for tb in range(TB):
                link(dve.tensor_scalar(gatew[:, tb, :], hot[:, 0, tb, :], topw[:, 2, tb:tb + 1], None, ALU.mult))
                link(dve.scalar_tensor_tensor(out=gatew[:, tb, :], in0=hot[:, 1, tb, :],
                                              scalar=topw[:, 3, tb:tb + 1], in1=gatew[:, tb, :], op0=ALU.mult,
                                              op1=ALU.add))
            dve.wait_ge(ranks_done, 1)
            link(dve.scalar_tensor_tensor(out=rank1[:, :, :],
                                          in0=banks[1][:, 0:TB * NE].rearrange("p (t e) -> p t e", t=TB), scalar=1.0,
                                          in1=sel[:, :, :], op0=ALU.add, op1=ALU.mult))
            link(dve.memset(rank[:, :, NE:JT], -1.0))
            link(dve.memset(jgate[:, :, NE:JT], 0.0))
            link(dve.tensor_scalar(rank[:, :, 0:NE], rank1[:, :, :], -1.0, None, ALU.add))
            link(dve.tensor_copy(jgate[:, :, 0:NE], gatew[:, :, :]))
            def picks(j):
                for tb in range(TB):
                    dve.tensor_scalar(pick[:, tb, :], iota[:, :], rank[:, tb, bass.ds(j, 1)], None, ALU.is_equal)
                    ins = dve.tensor_scalar(pickw[:, tb, :], iota[:, :], rank[:, tb, bass.ds(j, 1)],
                                            jgate[:, tb, bass.ds(j, 1)], ALU.is_equal, ALU.mult)
                ins.then_inc(pick_ready, 1)

            def gathered(jobs_before):
                dve.wait_ge(xg_done, jobs_before + 1)
                for i in range(2):
                    gain = par[:, 1, PR["ffn"] + 4 * i:PR["ffn"] + 4 * i + 4].unsqueeze(2).broadcast_to([P, 4, P])
                    ins = dve.tensor_tensor(xg[:, 4 * i:4 * i + 4, :],
                                            banks[6 + i][:, :].rearrange("p (d t) -> p d t", d=4), gain, ALU.mult)
                ins.then_inc(xg_ready, 1)

            def split_tokens(jobs_before):
                dve.wait_ge(xT_hi_ready, jobs_before + 1)
                dve.tensor_tensor(xT_lo[:, :, :], xg[:, :, :], xT_hi[:, :, :].bitcast(F32), ALU.subtract)\
                    .then_inc(xT_lo_ready, 1)

            def add_combined(tb, b0, blocks_before):
                dve.wait_ge(comb_done, blocks_before + 1)
                for half in range(2):
                    r = xres[:, tb, half * 512:(half + 1) * 512]
                    ins = dve.tensor_tensor(r, r, banks[b0 + half][:, :], ALU.add)
                ins.then_inc(comb_took, 1)

            picks(0)
            link(dve.tensor_scalar(ovf[:, :], banks[1][:, 2 * NE:3 * NE], float(P), None, ALU.is_gt))
            link(dve.tensor_tensor_scan(ovpos[:, :], ones[:, 0:NE], ovf[:, :], 0.0, ALU.mult, ALU.add))
            for o in range(3):
                link(dve.scalar_tensor_tensor(out=in_job[:, :], in0=ovpos[:, :], scalar=float(o + 1), in1=ovf[:, :],
                                              op0=ALU.is_equal, op1=ALU.mult))
                pickj = in_job[:, :].unsqueeze(1).broadcast_to([P, TB, NE])
                for src, dst in ((rank1, rank), (gatew, jgate)):
                    link(dve.tensor_tensor(prod8[:, :, :], src[:, :, :], pickj, ALU.mult))
                    link(dve.tensor_reduce(dst[:, :, NE + o:NE + o + 1], prod8[:, :, :], AX.X, ALU.add))
                link(dve.tensor_scalar(rank[:, :, NE + o:NE + o + 1], rank[:, :, NE + o:NE + o + 1], -1.0 - P, None,
                                       ALU.add))
                link(dve.tensor_tensor(prod8[:, 0, :], in_job[:, :], iota[:, 0:NE], ALU.mult))
                link(dve.tensor_reduce(steer_f[:, o:o + 1], prod8[:, 0, :], AX.X, ALU.add))
            link(dve.tensor_reduce(steer_f[:, 3:4], ovf[:, :], AX.X, ALU.add))
            signal(dve.tensor_copy(steer[0:1, :], steer_f[0:1, :]), "steer", steer_ready)
            gathered(0)
            split_tokens(0)

            def job(j, u0, s0):
                def more(c):
                    if c < TB:
                        add_combined(c, 6, 2 * j + c)
                    if c == 2:
                        dve.wait_ge(pickT_done, j + 1)
                        dve.tensor_copy(pickT[:, :, :], banks[6][:, 0:TB * P].rearrange("p (t s) -> p t s", t=TB))\
                            .then_inc(pickT_ready, 1)
                    if c == 3:
                        picks(j + 1)
                    if c == 5:
                        gathered(j + 1)

                ffn(1, BASE_FFN[1], u0, s0, 0, more)
                split_tokens(j + 1)

            with dve.Fori(0, NE) as e:
                job(e, e * FFN_SLOTS + BASE_FFN[1], e * NCH + DENSE)
            novf_r = dve.value_load(steer[0:1, 3:4], min_val=0, max_val=3)
            with dve.Fori(0, 3) as o:
                with dve.If(novf_r > o):
                    job(o + NE, o * FFN_SLOTS + (BASE_FFN[1] + NE * FFN_SLOTS), o * NCH + (DENSE + NE * NCH))
            for tb in range(TB):
                add_combined(tb, 4 + 2 * tb, novf_r * 2 + (2 * NE + tb))

            dve.wait_ge(comb_took, novf_r * 2 + (2 * NE + 2))
            for tb in range(TB):
                dve.tensor_tensor_reduce(hn[:, tb, :], xres[:, tb, :], xres[:, tb, :], 1.0 / D, 0.0, ALU.mult,
                                         ALU.add, stat[:, 40 + tb:41 + tb]).then_inc(ms_ready, 1)
            for tb in range(TB):
                dve.wait_ge(rstd_ready, 7 * L + tb + 1)
                dve.scalar_tensor_tensor(out=hn[:, tb, :], in0=xres[:, tb, :], scalar=rstd[:, 40 + tb:41 + tb],
                                         in1=gfin[:, :], op0=ALU.mult, op1=ALU.mult).then_inc(out_ready, 1)


_INS = ['x', 'positions', 'norm_mix', 'w_in', 'mla_q_norm', 'mla_w_uq', 'mla_kv_norm', 'mla_w_ukv', 'nsa_cmp_pe',
        'nsa_w_cmp', 'lru_conv_w', 'lru_conv_b', 'lru_w_gate', 'lru_b_gate', 'lru_lambda', 'ssd_conv_w',
        'ssd_conv_b', 'ssd_dt_bias', 'ssd_a_log', 'ssd_d', 'group_norm', 'w_out', 'norm_ffn', 'ffn_w_gate',
        'ffn_w_up', 'ffn_w_down', 'moe_router', 'moe_w_gate', 'moe_w_up', 'moe_w_down', 'norm_final']


def kernel(**inputs):
    import concourse.bacc as bacc
    from concourse.bass_utils import run_bass_kernel_spmd

    nc = bacc.Bacc("TRN2", target_bir_lowering=False, num_devices=1)
    arrays, args = {}, []
    for name in _INS:
        a = np.ascontiguousarray(inputs[name])
        arrays[f"in_{name}_dram"] = a
        args.append(nc.dram_tensor(f"in_{name}_dram", a.shape, mybir.dt.from_np(a.dtype), kind="ExternalInput").ap())
    out = nc.dram_tensor("out_dram", inputs["x"].shape, F32, kind="ExternalOutput").ap()
    trunk(nc, *args, out)
    r = run_bass_kernel_spmd(nc, [arrays], core_ids=[0])
    return r.results[0]["out_dram"]
```
